# Optimizing a Trainium2 kernel written in Bass

```python
import math
import jax, jax.numpy as jnp
from jax import lax
import numpy as np

D_MODEL = 1024
BATCH = 1
SEQ = 256
DEPTH = 1

N_MEM = 256
GDN_HEADS = 4
GDN_DK = 128
GDN_DV = 128
GDN_CONV = 4
GDN_CHUNK = 64
DIFF_HEADS = 4
DIFF_DQK = 64
DIFF_DV = 2 * DIFF_DQK
Q_BLOCK = 128
XA_HEADS = 4
XA_DH = D_MODEL // XA_HEADS
N_EXPERTS = 32
TOP_K = 4
D_FF = D_MODEL
SWIGLU_ALPHA = 1.702
SWIGLU_LIMIT = 7.0
MOE_BLOCK = 128
LN_EPS = 1e-5
RMS_EPS = 1e-6
DEEPNORM_ALPHA = (2 * DEPTH) ** 0.25
DEEPNORM_BETA = (8 * DEPTH) ** -0.25
GDN_QK_W = GDN_HEADS * GDN_DK
GDN_V_W = GDN_HEADS * GDN_DV
DIFF_QK_W = DIFF_HEADS * 2 * DIFF_DQK
DIFF_V_W = DIFF_HEADS * DIFF_DV
MIX_WIDTH = GDN_V_W + DIFF_V_W
IN_SIZES = (GDN_QK_W, GDN_QK_W, GDN_V_W, GDN_V_W, GDN_HEADS, GDN_HEADS, DIFF_QK_W, DIFF_QK_W, DIFF_V_W)
IN_COLS = sum(IN_SIZES)

kernel_name = 'hybrid_gdn_diffattn_memxattn_moe_deepnorm'

def split_cols(t, sizes):
    out, off = [], 0
    for s in sizes:
        out.append(t[..., off:off + s])
        off += s
    return out

def layer_norm(x, g, b):
    xf = x.astype(jnp.float32)
    mu = jnp.mean(xf, -1, keepdims=True)
    var = jnp.mean(jnp.square(xf - mu), -1, keepdims=True)
    return ((xf - mu) * lax.rsqrt(var + LN_EPS) * g.astype(jnp.float32) + b.astype(jnp.float32)).astype(x.dtype)

def rms_norm(x, w):
    xf = x.astype(jnp.float32)
    return xf * lax.rsqrt(jnp.mean(jnp.square(xf), -1, keepdims=True) + RMS_EPS) * w.astype(jnp.float32)

def l2_normalize(x):
    xf = x.astype(jnp.float32)
    return xf * lax.rsqrt(jnp.sum(jnp.square(xf), -1, keepdims=True) + RMS_EPS)

def causal_depthwise_conv(x, w):
    return lax.conv_general_dilated(x, w.astype(x.dtype), window_strides=(1,),
                                    padding=((GDN_CONV - 1, 0),),
                                    dimension_numbers=('NWC', 'WIO', 'NWC'),
                                    feature_group_count=x.shape[-1])

def gated_delta_rule_chunked(q, k, v, g, beta):
    B_, S_, H, DK = q.shape
    DV = v.shape[-1]
    C = GDN_CHUNK
    N = S_ // C
    f32 = jnp.float32

    def to_chunks(t):
        t = t.astype(f32).reshape((B_, N, C, H) + t.shape[3:])
        return jnp.moveaxis(t, 3, 1)

    q = to_chunks(q) * (DK ** -0.5)
    k = to_chunks(k)
    v = to_chunks(v)
    beta = to_chunks(beta)
    g = jnp.cumsum(to_chunks(g), axis=-1)
    causal = jnp.tril(jnp.ones((C, C), bool))
    strict = jnp.tril(jnp.ones((C, C), bool), -1)
    gdiff = g[..., :, None] - g[..., None, :]
    decay = jnp.where(causal, jnp.exp(jnp.where(causal, gdiff, 0.0)), 0.0)
    k_beta = k * beta[..., None]
    v_beta = v * beta[..., None]
    lmat = jnp.where(strict, jnp.einsum('bhncd,bhnsd->bhncs', k_beta, k) * decay, 0.0)
    amat = lmat + jnp.eye(C, dtype=f32)
    rhs = jnp.concatenate([v_beta, k_beta * jnp.exp(g)[..., None]], -1)
    sol = lax.linalg.triangular_solve(amat, rhs, left_side=True, lower=True, unit_diagonal=True)
    u = sol[..., :DV]
    w = sol[..., DV:]
    attn_intra = jnp.where(causal, jnp.einsum('bhncd,bhnsd->bhncs', q, k) * decay, 0.0)
    q_decay = q * jnp.exp(g)[..., None]
    k_tail = k * jnp.exp(g[..., -1:] - g)[..., None]
    g_last = jnp.exp(g[..., -1])

    def step(state, inp):
        u_c, w_c, qd_c, ai_c, kt_c, gl_c = inp
        v_new = u_c - jnp.einsum('bhck,bhkv->bhcv', w_c, state)
        out = jnp.einsum('bhck,bhkv->bhcv', qd_c, state) + jnp.einsum('bhcs,bhsv->bhcv', ai_c, v_new)
        state = state * gl_c[..., None, None] + jnp.einsum('bhck,bhcv->bhkv', kt_c, v_new)
        return state, out

    xs = tuple(jnp.moveaxis(t, 2, 0) for t in (u, w, q_decay, attn_intra, k_tail, g_last))
    state0 = jnp.zeros((B_, H, DK, DV), f32)
    _, out = lax.scan(step, state0, xs)
    return jnp.transpose(out, (1, 0, 3, 2, 4)).reshape(B_, S_, H, DV)

def differential_attention(q, k, v, lam):
    B_, S_, H = q.shape[:3]
    nb = S_ // Q_BLOCK
    scale = DIFF_DQK ** -0.5
    qb = jnp.moveaxis(q.reshape((B_, nb, Q_BLOCK) + q.shape[2:]), 1, 0)
    kpos = jnp.arange(S_)

    def block(args):
        q_blk, i = args
        qpos = i * Q_BLOCK + jnp.arange(Q_BLOCK)
        s = jnp.einsum('bqhcd,bkhcd->bhcqk', q_blk, k).astype(jnp.float32) * scale
        s = jnp.where(kpos[None, :] <= qpos[:, None], s, -jnp.inf)
        p = jax.nn.softmax(s, axis=-1)
        a = p[:, :, 0] - lam * p[:, :, 1]
        return jnp.einsum('bhqk,bkhv->bqhv', a.astype(v.dtype), v)

    out = lax.map(block, (qb, jnp.arange(nb)))
    return jnp.moveaxis(out, 0, 1).reshape(B_, S_, H, v.shape[-1])

def hybrid_mixer(x, w_in, conv_w, a_log, dt_bias, gdn_norm_w, lq1, lk1, lq2, lk2, diff_norm_w, w_out, lambda_init):
    B_, S_, _ = x.shape
    f32 = jnp.float32
    proj = x @ w_in
    gq, gk, gv, gz, gb, ga, dq, dk, dv = split_cols(proj, IN_SIZES)
    qkv = jax.nn.silu(causal_depthwise_conv(jnp.concatenate([gq, gk, gv], -1), conv_w))
    gq, gk, gv = split_cols(qkv, (GDN_QK_W, GDN_QK_W, GDN_V_W))
    q = l2_normalize(gq.reshape(B_, S_, GDN_HEADS, GDN_DK))
    k = l2_normalize(gk.reshape(B_, S_, GDN_HEADS, GDN_DK))
    v = gv.reshape(B_, S_, GDN_HEADS, GDN_DV).astype(f32)
    beta = jax.nn.sigmoid(gb.astype(f32))
    g = -jnp.exp(a_log.astype(f32)) * jax.nn.softplus(ga.astype(f32) + dt_bias.astype(f32))
    o = gated_delta_rule_chunked(q, k, v, g, beta)
    o = rms_norm(o, gdn_norm_w) * jax.nn.silu(gz.reshape(B_, S_, GDN_HEADS, GDN_DV).astype(f32))
    o_gdn = o.reshape(B_, S_, GDN_V_W).astype(x.dtype)
    lam = (jnp.exp(jnp.sum(lq1.astype(f32) * lk1.astype(f32)))
           - jnp.exp(jnp.sum(lq2.astype(f32) * lk2.astype(f32))) + lambda_init)
    od = differential_attention(dq.reshape(B_, S_, DIFF_HEADS, 2, DIFF_DQK),
                                dk.reshape(B_, S_, DIFF_HEADS, 2, DIFF_DQK),
                                dv.reshape(B_, S_, DIFF_HEADS, DIFF_DV), lam)
    od = rms_norm(od, diff_norm_w) * (1.0 - lambda_init)
    o_diff = od.reshape(B_, S_, DIFF_V_W).astype(x.dtype)
    return jnp.concatenate([o_gdn, o_diff], -1) @ w_out

def mem_cross_attention(x, mem, wq, wk, wv, wo):
    B_, S_, D = x.shape
    M = mem.shape[1]
    q = (x @ wq).reshape(B_, S_, XA_HEADS, XA_DH)
    k = (mem @ wk).reshape(B_, M, XA_HEADS, XA_DH)
    v = (mem @ wv).reshape(B_, M, XA_HEADS, XA_DH)
    s = jnp.einsum('bshd,bmhd->bhsm', q, k).astype(jnp.float32) * (XA_DH ** -0.5)
    p = jax.nn.softmax(s, axis=-1)
    o = jnp.einsum('bhsm,bmhd->bshd', p.astype(v.dtype), v).reshape(B_, S_, D)
    return o @ wo

def clamped_swiglu(h_gate, h_lin):
    h_gate = jnp.minimum(h_gate, SWIGLU_LIMIT)
    h_lin = jnp.clip(h_lin, -SWIGLU_LIMIT, SWIGLU_LIMIT)
    return h_gate * jax.nn.sigmoid(SWIGLU_ALPHA * h_gate) * (h_lin + 1.0)

def moe_ffn(x, router_w, router_b, w_gate, b_gate, w_up, b_up, w_down, b_down):
    B_, S_, D = x.shape
    xt = x.reshape(-1, D)
    T = xt.shape[0]
    logits = (xt @ router_w + router_b).astype(jnp.float32)
    top_val, top_idx = lax.top_k(logits, TOP_K)
    gate = jax.nn.softmax(top_val, axis=-1)
    A = T * TOP_K
    flat_e = top_idx.reshape(-1)
    order = jnp.argsort(flat_e)
    sorted_e = flat_e[order]
    token_of = order // TOP_K
    counts = jnp.bincount(flat_e, length=N_EXPERTS)
    padded = (counts + MOE_BLOCK - 1) // MOE_BLOCK * MOE_BLOCK
    start = jnp.cumsum(counts) - counts
    pad_end = jnp.cumsum(padded)
    pad_start = pad_end - padded
    dest = pad_start[sorted_e] + (jnp.arange(A) - start[sorted_e])
    n_blocks = -(-A // MOE_BLOCK) + N_EXPERTS
    P = n_blocks * MOE_BLOCK
    xs = jnp.zeros((P, D), xt.dtype).at[dest].set(xt[token_of])
    block_e = jnp.minimum(jnp.searchsorted(pad_end, jnp.arange(n_blocks) * MOE_BLOCK, side='right'), N_EXPERTS - 1)

    def expert_block(args):
        xb, e = args
        h = clamped_swiglu(xb @ w_gate[e] + b_gate[e], xb @ w_up[e] + b_up[e])
        return h @ w_down[e] + b_down[e]

    ys = lax.map(expert_block, (xs.reshape(n_blocks, MOE_BLOCK, D), block_e)).reshape(P, D)
    y_assign = ys[dest] * gate.reshape(-1)[order][:, None].astype(ys.dtype)
    y = jnp.zeros_like(xt).at[token_of].add(y_assign)
    return y.reshape(B_, S_, D)

def setup_inputs(seed: int = 0) -> dict:
    key = jax.random.key(seed)
    ks = jax.random.split(key, 40)
    f32 = jnp.float32
    L = DEPTH

    def nrm(k, shape, scale):
        return jax.random.normal(k, shape, f32) * scale

    dt = jnp.exp(jax.random.uniform(ks[4], (L, GDN_HEADS), f32, math.log(1e-3), math.log(1e-1)))
    return {
        'x': nrm(ks[0], (BATCH, SEQ, D_MODEL), 1.0),
        'mem': nrm(ks[1], (BATCH, N_MEM, D_MODEL), 1.0),
        'w_in': nrm(ks[2], (L, D_MODEL, IN_COLS), D_MODEL ** -0.5),
        'gdn_conv_w': nrm(ks[3], (L, GDN_CONV, 1, 2 * GDN_QK_W + GDN_V_W), GDN_CONV ** -0.5),
        'gdn_a_log': jnp.log(jax.random.uniform(ks[5], (L, GDN_HEADS), f32, 1.0, 16.0)),
        'gdn_dt_bias': dt + jnp.log(-jnp.expm1(-dt)),
        'gdn_norm_w': 1.0 + nrm(ks[6], (L, GDN_DV), 0.02),
        'diff_lq1': nrm(ks[7], (L, DIFF_DQK), 0.1),
        'diff_lk1': nrm(ks[8], (L, DIFF_DQK), 0.1),
        'diff_lq2': nrm(ks[9], (L, DIFF_DQK), 0.1),
        'diff_lk2': nrm(ks[10], (L, DIFF_DQK), 0.1),
        'diff_norm_w': 1.0 + nrm(ks[11], (L, DIFF_DV), 0.02),
        'w_out': nrm(ks[12], (L, MIX_WIDTH, D_MODEL), MIX_WIDTH ** -0.5 * DEEPNORM_BETA),
        'ln1_g': 1.0 + nrm(ks[13], (L, D_MODEL), 0.02),
        'ln1_b': nrm(ks[14], (L, D_MODEL), 0.02),
        'xa_wq': nrm(ks[15], (L, D_MODEL, D_MODEL), D_MODEL ** -0.5),
        'xa_wk': nrm(ks[16], (L, D_MODEL, D_MODEL), D_MODEL ** -0.5),
        'xa_wv': nrm(ks[17], (L, D_MODEL, D_MODEL), D_MODEL ** -0.5),
        'xa_wo': nrm(ks[18], (L, D_MODEL, D_MODEL), D_MODEL ** -0.5 * DEEPNORM_BETA),
        'ln2_g': 1.0 + nrm(ks[19], (L, D_MODEL), 0.02),
        'ln2_b': nrm(ks[20], (L, D_MODEL), 0.02),
        'router_w': nrm(ks[21], (L, D_MODEL, N_EXPERTS), D_MODEL ** -0.5),
        'router_b': nrm(ks[22], (L, N_EXPERTS), 0.01),
        'exp_w_gate': nrm(ks[23], (L, N_EXPERTS, D_MODEL, D_FF), D_MODEL ** -0.5),
        'exp_b_gate': nrm(ks[24], (L, N_EXPERTS, D_FF), 0.01),
        'exp_w_up': nrm(ks[25], (L, N_EXPERTS, D_MODEL, D_FF), D_MODEL ** -0.5),
        'exp_b_up': nrm(ks[26], (L, N_EXPERTS, D_FF), 0.01),
        'exp_w_down': nrm(ks[27], (L, N_EXPERTS, D_FF, D_MODEL), D_FF ** -0.5 * DEEPNORM_BETA),
        'exp_b_down': nrm(ks[28], (L, N_EXPERTS, D_MODEL), 0.01),
        'ln3_g': 1.0 + nrm(ks[29], (L, D_MODEL), 0.02),
        'ln3_b': nrm(ks[30], (L, D_MODEL), 0.02),
    }

def reference(x, mem, w_in, gdn_conv_w, gdn_a_log, gdn_dt_bias, gdn_norm_w, diff_lq1, diff_lk1, diff_lq2, diff_lk2,
              diff_norm_w, w_out, ln1_g, ln1_b, xa_wq, xa_wk, xa_wv, xa_wo, ln2_g, ln2_b, router_w, router_b,
              exp_w_gate, exp_b_gate, exp_w_up, exp_b_up, exp_w_down, exp_b_down, ln3_g, ln3_b):
    for l in range(DEPTH):
        lambda_init = 0.8 - 0.6 * math.exp(-0.3 * l)
        h = hybrid_mixer(x, w_in[l], gdn_conv_w[l], gdn_a_log[l], gdn_dt_bias[l], gdn_norm_w[l],
                         diff_lq1[l], diff_lk1[l], diff_lq2[l], diff_lk2[l], diff_norm_w[l], w_out[l], lambda_init)
        x = layer_norm(DEEPNORM_ALPHA * x + h, ln1_g[l], ln1_b[l])
        h = mem_cross_attention(x, mem, xa_wq[l], xa_wk[l], xa_wv[l], xa_wo[l])
        x = layer_norm(DEEPNORM_ALPHA * x + h, ln2_g[l], ln2_b[l])
        h = moe_ffn(x, router_w[l], router_b[l], exp_w_gate[l], exp_b_gate[l], exp_w_up[l], exp_b_up[l],
                    exp_w_down[l], exp_b_down[l])
        x = layer_norm(DEEPNORM_ALPHA * x + h, ln3_g[l], ln3_b[l])
    return x


_drawn_inputs = setup_inputs


def setup_inputs(seed=0):
    import zlib

    import numpy as np

    out = dict(_drawn_inputs(seed))
    spreads = {}
    factors = {'gdn_norm_w': 4.692,
     'diff_lq2': 4.207,
     'diff_lk2': 8.0,
     'diff_norm_w': 3.242,
     'router_b': 4.752,
     'exp_b_gate': 23.0,
     'exp_b_up': 33.505,
     'exp_b_down': 8.0,
     'ln3_g': 8.616,
     'ln3_b': 8.113,
     'diff_lq1': 8.0,
     'diff_lk1': 8.0}
    for name, (base, spread) in spreads.items():
        noise = np.random.default_rng([zlib.crc32(name.encode()), seed]).standard_normal(out[name].shape)
        drawn = base * np.exp(spread * noise) if base else spread * noise
        out[name] = __import__('jax').numpy.asarray(drawn.astype(out[name].dtype))
    for name, factor in factors.items():
        out[name] = (out[name] * factor).astype(out[name].dtype)
    return out
```

```python
from contextlib import ExitStack

import numpy as np

import concourse.bass as bass
from concourse import mybir

F32 = mybir.dt.float32
I32 = mybir.dt.int32
ALU = mybir.AluOpType
ACT = mybir.ActivationFunctionType
AX_X = mybir.AxisListType.X

P = 128
D_MODEL = 1024
SEQ = 256
TB = SEQ // P
KC = D_MODEL // P
HALF = D_MODEL // 2
DEPTH = 1
ALPHA = (2 * DEPTH) ** 0.25
LN_EPS = 1e-5
RMS_EPS = 1e-6

HEADS = 4
GDN_DK = 128
GDN_TAPS = 4
CONV_CHUNKS = 12
PAD = GDN_TAPS - 1
PAIRS = TB * HEADS
LEVELS = 7
DIFF_D = 64
DIFF_SCALE = DIFF_D ** -0.5
LAMBDA_INIT = 0.8 - 0.6
XA_SCALE = 256 ** -0.5
NEG = -3.0e38

N_EXPERTS = 32
TOP_K = 4
CAP = 64
MAX_BLOCKS = N_EXPERTS + SEQ * TOP_K // CAP
SWIGLU_ALPHA = 1.702
SWIGLU_LIMIT = 7.0

C_QK, C_VZ, C_BA, C_DQK, C_DV, IN_COLS = 0, 1024, 2048, 2056, 3080, 3592

K_ID, K_UT, K_US, K_ONE, K_CM, K_LEV0, K_LEVT = 0, 128, 256, 384, 512, 896, 1024
N_CONST = K_LEV0
N_LEVEL_MASKS = P * (LEVELS + 1)
K_IOTA = K_LEV0 + N_LEVEL_MASKS
K_NIOTA = K_IOTA + P
K_END = K_NIOTA + 64


def constants():
    r = np.arange(P)[:, None]
    c = np.arange(P)[None, :]
    out = np.zeros((P, K_END), np.float32)
    out[:, K_ID:K_ID + P] = r == c
    out[:, K_UT:K_UT + P] = r <= c
    out[:, K_US:K_US + P] = r < c
    out[:, K_ONE:K_ONE + P] = 1.0
    future = np.where(c > r, NEG, 0.0)
    out[:, K_CM:K_CM + P] = future
    out[:, K_CM + 2 * P:K_CM + 3 * P] = future
    out[:, K_IOTA:K_IOTA + P] = np.arange(P) % CAP
    out[:, K_NIOTA:K_NIOTA + 64] = np.arange(64)

    def below(t, s, size):
        return (t // (2 * size) == s // (2 * size)) & (t % (2 * size) >= size) & (s % (2 * size) < size)

    out[:, K_LEV0:K_LEV0 + P] = below(r, c, 1)
    for level in range(LEVELS):
        at = K_LEVT + P * level
        out[:, at:at + P] = below(c, r, 1 << level)
    return out


def unit_table():
    u = [("convw", "D")]
    u += [(f"xT{i}", "AD"[i % 2]) for i in range(4)]
    u += [(f"qk{i}", "A") for i in range(4)] + [(f"v{i}", "A") for i in range(2)]
    u += [("ba", "D"), ("z0", "A"), ("z1", "A")]
    u += [(f"dqk{i}", "A") for i in range(4)] + [("dv0", "A"), ("dv1", "A")]
    u += [(f"memT{i}", "A") for i in range(4)]
    u += [(f"ss{i}", "A") for i in range(4)]
    u += [("gcum", "D"), ("R0", "D"), ("R1", "D"), ("vtok0", "D"), ("vtok1", "D"), ("km0", "A")]
    u += [("KK0", "D"), ("KK1", "D"), ("KQ0", "D"), ("KQ1", "D"), ("ktok0", "D"), ("ktok1", "D"), ("km1", "A")]
    u += [("LT0", "A"), ("LT1", "A")]
    fill = ["km2", "km3", "vm0", "vm1", "vm2", "vm3"]
    for level in range(1, LEVELS):
        u += [(f"M{level}_0", "A"), (f"M{level}_1", "A")]
        for g in range(TB):
            if level < LEVELS - 1:
                u += [(f"X{level}_{g}", "D")]
            u += [(f"XT{level}_{g}", "D")]
        u += [(fill[level - 1], "A")]
    u += [("U0", "A"), ("U1", "A"), ("WT", "A")]
    u += [("sc0_0", "D"), ("sc0_1", "D"), ("S", "A"), ("O0", "A"), ("sc1_0", "D"), ("sc1_1", "D"), ("WS", "D")]
    u += [("aT0", "A"), ("sc2_0", "D"), ("sc2_1", "D"), ("O1", "A"), ("aT1", "A"), ("sc3_0", "D"), ("sc3_1", "D")]
    u += [("aT2", "A"), ("aT3", "A"), ("OD0", "A"), ("OD1", "A")]
    u += [(f"mixT{i}", "A") for i in range(4)]
    u += [(f"h{i}", "D") for i in range(4)]
    u += [(f"x1T{i}", "A") for i in range(4)] + [(f"xq{i}", "A") for i in range(4)]
    u += [(f"xs{i}", "D") for i in range(4)]
    u += [("pT0", "A"), ("pT1", "A"), ("oT0", "A"), ("pT2", "A"), ("oT1", "A"), ("pT3", "A"), ("oT2", "A"), ("oT3", "A")]
    u += [(f"wo{i}", "D") for i in range(4)]
    u += [("bT", "A")]
    u += [(f"x2T{i}", "A") for i in range(4)] + [("router", "D")]
    u += [("pos", "D"), ("cum", "D"), ("etab", "D"), ("GT", "A")]
    return u


UNITS = unit_table()
UNIT_AT = {name: i for i, (name, _) in enumerate(UNITS)}
N_UNITS = len(UNITS)


def emptied(name):
    at = UNIT_AT[name]
    engine = UNITS[at][1]
    return engine, sum(e == engine for _, e in UNITS[:at + 1])


ATTENTION_LOADS = [
    ("w_in", C_QK, 1024, 0), ("w_in", C_QK, 1024, 1), ("w_in", C_VZ, 1024, 0), ("w_in", C_VZ, 1024, 1),
    ("w_in", C_DQK, 1024, 0), ("w_in", C_DQK, 1024, 1), ("w_in", C_DV, 512, None),
    ("xa_wk", 0, 1024, 0), ("xa_wk", 0, 1024, 1), ("xa_wv", 0, 1024, 0), ("xa_wv", 0, 1024, 1),
    ("w_out", 0, 1024, 0), ("w_out", 0, 1024, 1), ("xa_wq", 0, 1024, 0), ("xa_wq", 0, 1024, 1),
    ("xa_wo", 0, 1024, 0), ("xa_wo", 0, 1024, 1),
]
N_ATT = len(ATTENTION_LOADS)
SLOTS = 6
G0, U0, G1, U1, D0, D1 = range(6)
ROLE_INPUT = ["exp_w_gate", "exp_w_up", "exp_w_gate", "exp_w_up", "exp_w_down", "exp_w_down"]
ROLE_SLOT = [(N_ATT + r) % SLOTS for r in range(SLOTS)]
ROLE_EARLIER = [sum(i % SLOTS == s for i in range(N_ATT)) for s in ROLE_SLOT]


def trunk_kernel(nc, d, out):
    ctx = ExitStack()
    with ctx:
        def sb(name, cols, dt=F32, rows=P):
            return ctx.enter_context(nc.sbuf_tensor(name, [rows, cols], dt))

        def sem(name):
            return ctx.enter_context(nc.semaphore(name))

        ring = sb("ring", SLOTS * 4 * D_MODEL)
        x_sb = sb("x_sb", TB * D_MODEL)
        xT_mem = sb("xT_mem", KC * SEQ)
        mem_mem = sb("mem_mem", TB * D_MODEL)
        memT_mem = sb("memT_mem", KC * SEQ)
        conv_in = sb("conv_in", CONV_CHUNKS * (SEQ + PAD))
        conv_out = sb("conv_out", CONV_CHUNKS * SEQ)
        gdn_mem = sb("gdn_mem", 6144)
        sz = sb("sz", TB * 512)
        dqk = sb("dqk", KC * SEQ)
        dv = sb("dv", TB * 512)
        km = sb("km", KC * SEQ)
        vm = sb("vm", TB * D_MODEL)
        ln_mem = sb("ln_mem", 2 * D_MODEL)
        kst = sb("kst", N_CONST)
        small = sb("small", 640)
        itab = sb("itab", 160, I32)

        slots = [ring[:, s * 4096:(s + 1) * 4096].rearrange("p (k n) -> p k n", k=4) for s in range(SLOTS)]
        x3 = x_sb[:, :].rearrange("p (b n) -> p b n", b=TB)
        xT = xT_mem[:, :].rearrange("p (k t) -> p k t", k=KC)
        mem3 = mem_mem[:, :].rearrange("p (b n) -> p b n", b=TB)
        memT = memT_mem[:, :].rearrange("p (k t) -> p k t", k=KC)
        cin = conv_in[:, :].rearrange("p (c t) -> p c t", c=CONV_CHUNKS)
        cout = conv_out[:, :].rearrange("p (c t) -> p c t", c=CONV_CHUNKS)
        qn, kn, vT = cout[:, 0:4, :], cout[:, 4:8, :], cout[:, 8:12, :]

        def pairs(mem, at, n=PAIRS):
            return mem[:, at:at + n * P].rearrange("p (g s) -> p g s", g=n)

        Dm, DT, L = pairs(conv_in, 0), pairs(conv_in, 1024), pairs(conv_in, 2048)
        X, XT, u_sb = Dm, DT, L
        wT, S_sb = pairs(conv_in, 0, 4), pairs(conv_in, 512, 4)
        BT = pairs(conv_out, 2048)
        LT, M1, AT, kbg, vbeta = (pairs(gdn_mem, 1024 * i) for i in range(5))
        ktail, qd = pairs(gdn_mem, 5120, 4), pairs(gdn_mem, 5632, 4)
        gB, diff, vnew, o_sb = M1, LT, pairs(gdn_mem, 0, 4), M1
        sq_mem = gdn_mem[:, 3072:5120]
        sq = sq_mem.rearrange("p (c t) -> p c t", c=8)
        sz3 = sz[:, :].rearrange("p (b n) -> p b n", b=TB)
        dqk3 = dqk[:, :].rearrange("p (k t) -> p k t", k=KC)
        dv3 = dv[:, :].rearrange("p (b n) -> p b n", b=TB)
        km3 = km[:, :].rearrange("p (k t) -> p k t", k=KC)
        vm3 = vm[:, :].rearrange("p (b n) -> p b n", b=TB)
        dp = [gdn_mem[:, 3072 + 768 * i:3840 + 768 * i].rearrange("p (c n) -> p c n", c=2) for i in range(2)]
        aT = xT_mem[:, 0:4 * 384].rearrange("p (h n) -> p h n", h=4)
        od_sb = conv_out[:, 2048:3072]
        o_sq = conv_in[:, 2048:3072]
        xp = gdn_mem[:, 3072:5120].rearrange("p (h b m) -> p h b m", h=4, b=TB)
        pT = mem_mem[:, :].rearrange("p (h m t) -> p h m t", h=4, m=TB)
        oT = conv_in[:, 0:2048].rearrange("p (k t) -> p k t", k=KC)

        ident = kst[:, K_ID:K_ID + P]
        upper = kst[:, K_UT:K_UT + P]
        strict = kst[:, K_US:K_US + P]
        ones = kst[:, K_ONE:K_ONE + P]
        causal = kst[:, K_CM:K_CM + 3 * P]
        iota2 = gdn_mem[:, 2432:2432 + P]
        niota = gdn_mem[:, 2432 + P:2432 + P + 64]
        lev0 = ln_mem[:, 0:P]
        levT = [ln_mem[:, P * (1 + i):P * (2 + i)] for i in range(LEVELS)]
        ln_g, ln_b = ln_mem[:, 0:D_MODEL], ln_mem[:, D_MODEL:2 * D_MODEL]

        at = [0]

        def take(n):
            at[0] += n
            return small[:, at[0] - n:at[0]]

        convw = take(48)
        ba = take(16)
        beta = take(8)
        g_log = take(8)
        gcum = take(8)
        eg = take(8)
        begs = take(8)
        tails = take(8)
        sp_a, sp_b, sp_c = take(8), take(8), take(8)
        a_log, dt_b = take(4), take(4)
        lamv = take(4)
        neglam = take(1)
        rs8 = take(8)
        stat_mx, stat_nb, stat_l, stat_r = take(8), take(8), take(8), take(8)
        bn = take(12)
        mv = take(2)
        rstd = take(1)
        top8 = take(16)
        gsum = take(2)
        nblk, cumc = take(2), take(2)
        rb = take(32)
        eps_rms = take(1)
        minus_half = take(4)
        logit, expl, M, G, pos = (take(64) for _ in range(5))
        assert at[0] <= 640

        def row_b(v, n, k):
            return v.unsqueeze(2).broadcast_to([P, n, k])

        def tile_b(v, n, k):
            return v.unsqueeze(1).broadcast_to([P, n, k])

        convw_raw = sz[0:48, 0:128]
        lam_raw = vm[:, 0:256]
        gnw = vm[:, 256:384]
        dnw = km[:, 0:128]
        dnw_keep = sb("dnw_keep", 128)

        yacc = vm3
        xgT = km[:, 0:512].rearrange("p (k s) -> p k s", k=4)
        gu = km[:, 512:1536].rearrange("p (f n) -> p f n", f=2)
        hT = km[:, 1536:2048].rearrange("p (k s) -> p k s", k=KC)
        mg, mu, sig, tmp = (conv_in[:, 512 * i:512 * (i + 1)].rearrange("p (f k s) -> p f k s", f=2, k=4) for i in range(4))
        y_sb = conv_in[:, 2048:2560]
        xg_sb = conv_in[:, 2560:3072]
        selw = gdn_mem[:, 0:256].rearrange("p (b s) -> p b s", b=TB)
        gsel = gdn_mem[:, 256:512].rearrange("p (b s) -> p b s", b=TB)
        gselT = gdn_mem[:, 512:768]
        ebias = gdn_mem[:, 768:1280].rearrange("p (w n) -> p w n", w=2)
        GT = gdn_mem[0:N_EXPERTS, 1280:1536]
        emask = gdn_mem[0:N_EXPERTS, 1536:1600]
        erow = gdn_mem[0:1, 1600:1664]
        crow = gdn_mem[0:1, 1664:1696]
        bias_raw = gdn_mem[:, 1792:2304].rearrange("p (w b n) -> p w b n", w=2, b=2)
        bdown = dqk[0:N_EXPERTS, 0:D_MODEL]
        T_E, T_E16, T_CUM = 0, 64, 128
        rtmp = gdn_mem[:, 2304:2368]
        rtmp2 = gdn_mem[:, 2368:2432]

        banks = [ctx.enter_context(nc.psum_tensor(f"bank{i}", [P, 512], F32)) for i in range(8)]

        def bank(name):
            return banks[UNIT_AT[name] % 8]

        unit_filled = sem("unit_filled")
        act_emptied = sem("act_emptied")
        dve_emptied = sem("dve_emptied")
        ring_full = [sem(f"ring_full{s}") for s in range(SLOTS)]
        ring_used = sem("ring_used")
        ld_x, ld_const, ld_lev, ld_mem, ld_vec, ld_ba = (sem(n) for n in ("ld_x", "ld_const", "ld_lev", "ld_mem", "ld_vec", "ld_ba"))
        ld_ln = sem("ld_ln")
        ld_iota = sem("ld_iota")
        ld_rt, ld_bias, ld_bdown = sem("ld_rt"), sem("ld_bias"), sem("ld_bdown")
        pad_zero = sem("pad_zero")
        conv_ready = sem("conv_ready")
        silu_ready = sem("silu_ready")
        sq_ready = sem("sq_ready")
        exp_ready = sem("exp_ready")
        gate_step = sem("gate_step")
        qk_normed = sem("qk_normed")
        dec_in, dec_exp, dec_ready = sem("dec_in"), sem("dec_exp"), sem("dec_ready")
        qd_exp = sem("qd_exp")
        l2_exp = sem("l2_exp")
        eps_set = sem("eps_set")
        var_in, var_out = sem("var_in"), sem("var_out")
        lmat_ready = sem("lmat_ready")
        x_init = sem("x_init")
        xt_init = sem("xt_init")
        bt_ready = sem("bt_ready")
        vnew_ready = sem("vnew_ready")
        lam_in, lam_exp = sem("lam_in"), sem("lam_exp")
        sm_in, sm_exp = sem("sm_in"), sem("sm_exp")
        a_ready = sem("a_ready")
        mix_ready = sem("mix_ready")
        o_square = sem("o_square")
        ln_ready = sem("ln_ready")
        xsm_in, xsm_exp, xp_ready = sem("xsm_in"), sem("xsm_exp"), sem("xp_ready")
        rt_in, rt_exp = sem("rt_in"), sem("rt_exp")
        route_ready = sem("route_ready")
        cnt_ready = sem("cnt_ready")
        tab_ready = sem("tab_ready")
        zsilu = sem("zsilu")
        sel_ready = sem("sel_ready")
        gsel_ready = sem("gsel_ready")
        xg_done, xg_copied = sem("xg_done"), sem("xg_copied")
        xgT_done, xgT_ready = sem("xgT_done"), sem("xgT_ready")
        gu0_used = sem("gu0_used")
        gu_done, gu_copied = sem("gu_done"), sem("gu_copied")
        guT_done = sem("guT_done")
        gselT_done, gselT_ready = sem("gselT_done"), sem("gselT_ready")
        mg_ready, sig_ready, hT_ready = sem("mg_ready"), sem("sig_ready"), sem("hT_ready")
        d0_used = sem("d0_used")
        y_done, y_copied = sem("y_done"), sem("y_copied")
        scat_done, acc_done = sem("scat_done"), sem("acc_done")
        bias_done, out_ready, out_stored = sem("bias_done"), sem("out_ready"), sem("out_stored")

        def wait_emptied(eng, name):
            engine, count = emptied(name)
            eng.wait_ge(act_emptied if engine == "A" else dve_emptied, count)

        block = ctx.enter_context(nc.Block())

        @block.sync
        def _(sp):
            for i, (name, col, cols, half) in enumerate(ATTENTION_LOADS):
                if i >= SLOTS:
                    sp.wait_ge(ring_used, i - SLOTS + 1)
                src = d[name][0, :, col:col + cols].rearrange("(k p) n -> p k n", p=P)
                if half is None:
                    dst = ring[:, (i % SLOTS) * 4096:(i % SLOTS + 1) * 4096].rearrange("p (k n) -> p k n", k=KC)
                else:
                    dst, src = slots[i % SLOTS], src[:, 4 * half:4 * half + 4, :]
                sp.dma_start(dst, src).then_inc(ring_full[i % SLOTS], 16)

            def load_role(role, e):
                w = d[ROLE_INPUT[role]][0].rearrange("e (k p) n -> e p k n", p=P)
                h = (0, 0, 1, 1, 0, 1)[role]
                src = w[bass.ds(e, 1), :, 4 * h:4 * h + 4, :].rearrange("e p k n -> p (e k) n")
                sp.dma_start(slots[ROLE_SLOT[role]], src).then_inc(ring_full[ROLE_SLOT[role]], 16)

            for role in range(SLOTS):
                sp.wait_ge(ring_used, N_ATT + role - SLOTS + 1)
                load_role(role, 0)
            sp.wait_ge(tab_ready, 1)
            with sp.Fori(1, N_EXPERTS) as e:
                done = sp.value_load(itab[0:1, bass.ds(e + (T_CUM - 1), 1)], min_val=1, max_val=MAX_BLOCKS)
                sp.wait_ge(gu0_used, done)
                load_role(G0, e)
                load_role(U0, e)
                sp.wait_ge(gu_done, done * 2)
                load_role(G1, e)
                load_role(U1, e)
                sp.wait_ge(d0_used, done)
                load_role(D0, e)
                sp.wait_ge(y_done, done)
                load_role(D1, e)

            sp.wait_ge(out_ready, 1)
            sp.dma_start(out[0, 0:P, :], x3[:, 0, :]).then_inc(out_stored, 16)
            sp.wait_ge(out_ready, 2)
            sp.dma_start(out[0, P:SEQ, :], x3[:, 1, :]).then_inc(out_stored, 16)
            sp.wait_ge(out_stored, 32)

        @block.gpsimd
        def _(pool):
            pool.memset(cin[:, :, 0:PAD], 0.0).then_inc(pad_zero, 1)
            pool.memset(eps_rms, RMS_EPS).then_inc(eps_set, 1)
            pool.memset(minus_half, -0.5)
            for j in range(4):
                pool.wait_ge(silu_ready, j + 1)
                pool.tensor_tensor(sq[:, 2 * j:2 * j + 2, :], cout[:, 2 * j:2 * j + 2, :], cout[:, 2 * j:2 * j + 2, :],
                                   ALU.mult).then_inc(sq_ready, 1)
            pool.wait_ge(dec_exp, 1)
            pool.affine_select(out=Dm, in_=Dm, pattern=[[0, PAIRS], [-1, P]], compare_op=ALU.is_gt, fill=0.0,
                               base=0, channel_multiplier=1).then_inc(dec_ready, 1)
            pool.wait_ge(dec_exp, 2)
            pool.affine_select(out=DT, in_=DT, pattern=[[0, PAIRS], [1, P]], compare_op=ALU.is_ge, fill=0.0,
                               base=0, channel_multiplier=-1).then_inc(dec_ready, 1)
            wait_emptied(pool, "LT1")
            wait_emptied(pool, "KQ1")
            pool.wait_ge(ld_lev, 16)
            pool.tensor_tensor(XT, LT, tile_b(levT[0], PAIRS, P), ALU.mult)
            pool.drain()
            pool.tensor_tensor(XT, tile_b(ident, PAIRS, P), XT, ALU.subtract).then_inc(xt_init, 1)
            for level in range(1, LEVELS):
                if level == 1:
                    wait_emptied(pool, "vtok1")
                else:
                    pool.wait_ge(unit_filled, UNIT_AT[f"M{level - 1}_1"] + 1)
                pool.tensor_tensor(BT, LT, tile_b(levT[level], PAIRS, P), ALU.mult).then_inc(bt_ready, 1)
            for i in range(4 + 3 * TB):
                pool.wait_ge(var_in, i + 1)
                v = rs8[:, 0:4] if i < 4 else rstd
                pool.tensor_tensor(v, v, minus_half[:, 0:4 if i < 4 else 1], ALU.pow).then_inc(var_out, 1)

        @block.scalar
        def _(act):
            act.dma_start(x3, d["x"][0].rearrange("(b p) n -> p b n", p=P)).then_inc(ld_x, 16)
            act.dma_start(kst[:, :], d["consts"][:, 0:N_CONST]).then_inc(ld_const, 16)
            act.dma_start(convw_raw, d["gdn_conv_w"][0].rearrange("t o (c p) -> (t o c) p", p=P)).then_inc(ld_const, 16)
            ba_dst = dnw_keep[:, 0:64].rearrange("p (k n) -> p k n", k=KC)
            act.dma_start(ba_dst, d["w_in"][0, :, C_BA:C_BA + 8].rearrange("(k p) n -> p k n", p=P)).then_inc(ld_ba, 16)
            for i, name in enumerate(["diff_lq1", "diff_lk1", "diff_lq2", "diff_lk2"]):
                act.dma_start(lam_raw[:, 64 * i:64 * i + 64], d[name][0:1, :].partition_broadcast(P)).then_inc(ld_vec, 16)
            for dst, name in ((gnw, "gdn_norm_w"), (a_log, "gdn_a_log"), (dt_b, "gdn_dt_bias"), (dnw, "diff_norm_w")):
                act.dma_start(dst, d[name][0:1, :].partition_broadcast(P)).then_inc(ld_vec, 16)
            act.dma_start(mem3, d["mem"][0].rearrange("(b p) n -> p b n", p=P)).then_inc(ld_mem, 16)
            act.dma_start(ln_mem[:, 0:N_LEVEL_MASKS], d["consts"][:, K_LEV0:K_LEV0 + N_LEVEL_MASKS]).then_inc(ld_lev, 16)
            act.dma_start(rb, d["router_b"][0:1, :].partition_broadcast(P)).then_inc(ld_rt, 16)

            def load_gains(name):
                act.dma_start(ln_g, d[name + "_g"][0:1, :].partition_broadcast(P)).then_inc(ld_ln, 16)
                act.dma_start(ln_b, d[name + "_b"][0:1, :].partition_broadcast(P)).then_inc(ld_ln, 16)

            def filled(name):
                act.wait_ge(unit_filled, UNIT_AT[name] + 1)
                return bank(name)

            def empty(name, dst, src=None, func=ACT.Copy, **kw):
                ps = filled(name)
                act.activation(dst, ps[:, :] if src is None else src(ps), func, **kw).then_inc(act_emptied, 1)

            def as3(n):
                return lambda ps: ps[:, :].rearrange("p (g s) -> p g s", g=n)

            for i in (0, 2):
                empty(f"xT{i}", xT[:, 0:4, (i // 2) * P:(i // 2 + 1) * P], as3(4))
            act.wait_ge(pad_zero, 1)
            for i in range(4):
                empty(f"qk{i}", cin[:, 2 * i:2 * i + 2, PAD:], as3(2))
            for i in range(2):
                empty(f"v{i}", cin[:, 8 + 2 * i:10 + 2 * i, PAD:], as3(2))
            for b in range(TB):
                empty(f"z{b}", sz3[:, b, :], func=ACT.Silu)
            zs_done = emptied("z1")[1]
            act.wait_ge(act_emptied, zs_done)

            for j in range(6):
                act.wait_ge(conv_ready, j + 1)
                act.activation(cout[:, 2 * j:2 * j + 2, :], cout[:, 2 * j:2 * j + 2, :], ACT.Silu).then_inc(silu_ready, 1)
            for i in range(4):
                empty(f"dqk{i}", dqk3[:, 2 * i:2 * i + 2, :], as3(2))
            for b in range(TB):
                empty(f"dv{b}", dv3[:, b, :])
            for i in range(4):
                empty(f"memT{i}", memT[:, 4 * (i % 2):4 * (i % 2) + 4, (i // 2) * P:(i // 2 + 1) * P], as3(4))

            act.wait_ge(eps_set, 1)
            act.wait_ge(gate_step, 1)
            act.activation(sp_a, sp_a, ACT.Exp, scale=-1.0).then_inc(exp_ready, 1)
            act.activation(sp_b, sp_b, ACT.Exp, scale=-1.0).then_inc(exp_ready, 1)
            act.activation(a_log, a_log, ACT.Exp).then_inc(exp_ready, 1)
            act.activation(lamv[:, 0:2], lamv[:, 0:2], ACT.Exp).then_inc(lam_exp, 1)
            act.wait_ge(exp_ready, 2)
            act.activation(sp_b, sp_b, ACT.Ln, bias=1.0).then_inc(exp_ready, 1)
            for i in range(4):
                empty(f"ss{i}", sq_mem[:, 512 * i:512 * (i + 1)], func=ACT.Ln, bias=eps_rms)
            act.wait_ge(act_emptied, emptied("ss3")[1])
            for i in range(4):
                part = sq_mem[:, 512 * i:512 * (i + 1)]
                act.activation(part, part, ACT.Exp, scale=-0.5).then_inc(l2_exp, 1)
            act.wait_ge(gate_step, 3)
            act.activation(eg, gcum, ACT.Exp).then_inc(exp_ready, 1)
            act.wait_ge(dec_in, 1)
            act.activation(tails[:, 0:4], tails[:, 0:4], ACT.Exp).then_inc(exp_ready, 1)
            act.activation(qd, bank("R1")[:, :].rearrange("p (g s) -> p g s", g=4), ACT.Exp).then_inc(qd_exp, 1)
            act.wait_ge(dec_in, 2)
            act.activation(Dm, Dm, ACT.Exp, scale=-1.0).then_inc(dec_exp, 1)
            act.wait_ge(dec_in, 3)
            act.activation(DT, DT, ACT.Exp).then_inc(dec_exp, 1)

            empty("km0", km3[:, 0:2, :], as3(2))
            empty("km1", km3[:, 2:4, :], as3(2))
            for g in range(TB):
                empty(f"LT{g}", LT[:, 4 * g:4 * g + 4, :], as3(4))
            for level in range(1, LEVELS):
                for g in range(TB):
                    empty(f"M{level}_{g}", M1[:, 4 * g:4 * g + 4, :], as3(4))
                if level <= 2:
                    empty(f"km{level + 1}", km3[:, 2 * level + 2:2 * level + 4, :], as3(2))
                else:
                    v = level - 3
                    empty(f"vm{v}", vm3[:, v // 2, (v % 2) * HALF:(v % 2 + 1) * HALF])
            for g in range(TB):
                empty(f"U{g}", u_sb[:, 4 * g:4 * g + 4, :], as3(4))
            empty("WT", wT, as3(4))
            act.wait_ge(bt_ready, LEVELS - 1)
            act.wait_ge(x_init, 1)
            load_gains("ln1")

            def diff_exp(h, c):
                i = 2 * h + c
                act.wait_ge(sm_in, i + 1)
                for q, (a, b) in enumerate(((0, P), (P, 3 * P))):
                    act.activation(dp[h % 2][:, c, a:b], dp[h % 2][:, c, a:b], ACT.Exp, scale=DIFF_SCALE,
                                   bias=stat_nb[:, 4 * (h % 2) + 2 * c + q:4 * (h % 2) + 2 * c + q + 1],
                                   accum_out=stat_l[:, 4 * (h % 2) + 2 * c + q:4 * (h % 2) + 2 * c + q + 1]).then_inc(sm_exp, 1)

            def empty_aT(h):
                empty(f"aT{h}", aT[:, h, :], lambda ps: ps[:, 0:384])

            diff_exp(0, 0)
            diff_exp(0, 1)
            empty("S", S_sb, as3(4))
            empty("O0", o_sb[:, 0:4, :], as3(4))
            diff_exp(1, 0)
            diff_exp(1, 1)
            empty_aT(0)
            diff_exp(2, 0)
            diff_exp(2, 1)
            empty("O1", o_sb[:, 4:8, :], as3(4))
            empty_aT(1)
            diff_exp(3, 0)
            diff_exp(3, 1)
            empty_aT(2)
            empty_aT(3)
            empty("OD0", od_sb[:, 0:512])
            empty("OD1", od_sb[:, 512:1024])

            act.wait_ge(mix_ready, 2)
            for w, n in enumerate(["exp_b_gate", "exp_b_up"]):
                act.dma_start(bias_raw[:, w, :, :], d[n][0].rearrange("(b e) (c f) -> (e c) b f", b=2, f=P)).then_inc(ld_bias, 16)
            act.dma_start(gdn_mem[:, 2432:2432 + P + 64], d["consts"][:, K_IOTA:K_END]).then_inc(ld_iota, 16)
            for i in range(4):
                empty(f"mixT{i}", xT[:, 4 * (i % 2):4 * (i % 2) + 4, (i // 2) * P:(i // 2 + 1) * P], as3(4))
            for i in range(4):
                empty(f"x1T{i}", memT[:, 4 * (i % 2):4 * (i % 2) + 4, (i // 2) * P:(i // 2 + 1) * P], as3(4))
            for i in range(4):
                empty(f"xq{i}", dqk3[:, 2 * i:2 * i + 2, :], as3(2))

            def cross_exp(h):
                act.wait_ge(xsm_in, h + 1)
                for b in range(TB):
                    act.activation(xp[:, h, b, :], bank(f"xs{h}")[:, b * 256:(b + 1) * 256], ACT.Exp, scale=XA_SCALE,
                                   bias=stat_nb[:, 2 * h + b:2 * h + b + 1],
                                   accum_out=stat_l[:, 2 * h + b:2 * h + b + 1]).then_inc(xsm_exp, 1)

            def empty_pT(h):
                empty(f"pT{h}", pT[:, h, :, :], as3(2))

            def empty_oT(h):
                empty(f"oT{h}", oT[:, 2 * h:2 * h + 2, :], as3(2))

            act.wait_ge(ln_ready, 2)
            load_gains("ln2")
            for h in range(4):
                cross_exp(h)
            act.dma_start(bdown, d["exp_b_down"][0]).then_inc(ld_bdown, 16)
            act.dma_start(dv[:, 0:KC * N_EXPERTS].rearrange("p (k e) -> p k e", k=KC),
                          d["router_w"][0].rearrange("(k p) e -> p k e", p=P)).then_inc(ld_rt, 16)
            empty_pT(0)
            empty_pT(1)
            empty_oT(0)
            empty_pT(2)
            empty_oT(1)
            empty_pT(3)
            empty_oT(2)
            empty_oT(3)
            empty("bT", ebias, as3(2))
            for i in range(4):
                empty(f"x2T{i}", xT[:, 4 * (i % 2):4 * (i % 2) + 4, (i // 2) * P:(i // 2 + 1) * P], as3(4))
            act.wait_ge(ln_ready, 4)
            load_gains("ln3")
            act.wait_ge(rt_in, 1)
            act.activation(expl, expl, ACT.Exp).then_inc(rt_exp, 1)
            empty("GT", GT, lambda ps: ps[0:N_EXPERTS, 0:256])

            def copy_xg():
                act.activation(xg_sb, banks[5][:, :], ACT.Copy).then_inc(xg_copied, 1)

            act.wait_ge(xg_done, 1)
            copy_xg()
            act.wait_ge(tab_ready, 1)
            blocks = act.value_load(itab[0:1, T_CUM + N_EXPERTS - 1:T_CUM + N_EXPERTS], min_val=N_EXPERTS, max_val=MAX_BLOCKS)
            with act.Fori(0, blocks) as n:
                for f in range(2):
                    act.wait_ge(gu_done, n * 2 + (f + 1))
                    act.activation(gu[:, f, :], banks[f][:, :], ACT.Copy).then_inc(gu_copied, 1)
                act.wait_ge(xg_done, n + 2)
                copy_xg()
                act.wait_ge(gselT_done, n + 1)
                act.activation(gselT, banks[4][:, 0:256], ACT.Copy).then_inc(gselT_ready, 1)
                for f in range(2):
                    act.wait_ge(mg_ready, n * 2 + (f + 1))
                    act.activation(sig[:, f, :, :], mg[:, f, :, :], ACT.Sigmoid, scale=SWIGLU_ALPHA).then_inc(sig_ready, 1)
                act.wait_ge(y_done, n + 1)
                act.activation(y_sb, banks[4][:, :], ACT.Copy).then_inc(y_copied, 1)

        @block.tensor
        def _(pe):
            def begin(name):
                u = UNIT_AT[name]
                if u >= 8:
                    wait_emptied(pe, UNITS[u - 8][0])
                return bank(name)

            def need(*names):
                for name in names:
                    wait_emptied(pe, name)

            def arrived(i):
                pe.wait_ge(ring_full[i % SLOTS], 16 * (i // SLOTS + 1))

            def transpose_block(name, src, chunks, out_ps=None, rows=P):
                ps = begin(name)
                for j, c in enumerate(chunks):
                    last = pe.transpose(ps[:, j * P:(j + 1) * P], src[:, c * P:(c + 1) * P], ident)
                last.then_inc(unit_filled, 1)

            def channel_major(name, w, chunks, src, signal=None):
                ps = begin(name)
                for j, c in enumerate(chunks):
                    for k in range(KC):
                        last = pe.matmul(ps[:, j * SEQ:(j + 1) * SEQ], w(k)[:, c * P:(c + 1) * P], src[:, k, :],
                                         start=(k == 0), stop=(k == KC - 1))
                last.then_inc(unit_filled, 1)

            def token_major(name, srcT, b, w, col):
                ps = begin(name)
                for k in range(KC):
                    last = pe.matmul(ps[:, :], srcT[:, k, b * P:(b + 1) * P], w(k)[:, col:col + 512],
                                     start=(k == 0), stop=(k == KC - 1))
                last.then_inc(unit_filled, 1)

            def through(*loads):
                return lambda k: slots[loads[k // 4] % SLOTS][:, k % 4, :]

            def used_up(n, after):
                pe.wait_ge(unit_filled, UNIT_AT[after] + 1)
                pe.sem_inc(ring_used, n)

            pe.wait_ge(ld_const, 32)
            ps = begin("convw")
            pe.transpose(ps[:, 0:48], convw_raw, ident[0:48, 0:48]).then_inc(unit_filled, 1)
            pe.wait_ge(ld_x, 16)
            for i in range(4):
                transpose_block(f"xT{i}", x3[:, i // 2, :], range(4 * (i % 2), 4 * (i % 2) + 4))
            need("xT2", "xT3")
            arrived(0)
            arrived(1)
            for i in range(4):
                channel_major(f"qk{i}", through(0, 1), (2 * i, 2 * i + 1), xT)
            arrived(2)
            arrived(3)
            for i in range(2):
                channel_major(f"v{i}", through(2, 3), (2 * i, 2 * i + 1), xT)
            used_up(2, "qk3")
            pe.wait_ge(ld_ba, 16)
            ps = begin("ba")
            for b in range(TB):
                for k in range(KC):
                    last = pe.matmul(ps[:, 8 * b:8 * b + 8], xT[:, k, b * P:(b + 1) * P], dnw_keep[:, 8 * k:8 * k + 8],
                                     start=(k == 0), stop=(k == KC - 1))
            last.then_inc(unit_filled, 1)
            for b in range(TB):
                token_major(f"z{b}", xT, b, through(2, 3), 512)
            arrived(4)
            arrived(5)
            channel_major("dqk0", through(4, 5), (0, 1), xT)
            used_up(2, "z1")
            for i in range(1, 4):
                channel_major(f"dqk{i}", through(4, 5), (2 * i, 2 * i + 1), xT)
            arrived(6)
            dv_w = ring[:, 0:4096].rearrange("p (k n) -> p k n", k=KC)
            for b in range(TB):
                token_major(f"dv{b}", xT, b, lambda k: dv_w[:, k, :], 0)
            pe.wait_ge(ld_mem, 16)
            for i in range(4):
                transpose_block(f"memT{i}", mem3[:, i // 2, :], range(4 * (i % 2), 4 * (i % 2) + 4))
            used_up(3, "dv1")

            for i in range(4):
                pe.wait_ge(sq_ready, i + 1)
                ps = begin(f"ss{i}")
                pe.matmul(ps[:, :], ones, sq_mem[:, 512 * i:512 * (i + 1)], start=True, stop=True).then_inc(unit_filled, 1)
            pe.wait_ge(gate_step, 2)
            ps = begin("gcum")
            pe.matmul(ps[:, 0:PAIRS], upper, g_log, start=True, stop=True).then_inc(unit_filled, 1)
            for g in range(TB):
                ps = begin(f"R{g}")
                for h in range(HEADS):
                    last = pe.matmul(ps[:, h * P:(h + 1) * P], gB[:, 4 * g + h, :], upper, start=True, stop=True)
                last.then_inc(unit_filled, 1)
            pe.wait_ge(silu_ready, 6)
            for b in range(TB):
                transpose_heads = begin(f"vtok{b}")
                for h in range(HEADS):
                    last = pe.transpose(transpose_heads[:, h * P:(h + 1) * P], vT[:, h, b * P:(b + 1) * P], ident)
                last.then_inc(unit_filled, 1)

            need("memT3")
            arrived(7)
            arrived(8)

            def km_unit(i):
                channel_major(f"km{i}", through(7, 8), (2 * i, 2 * i + 1), memT)

            def vm_unit(i):
                token_major(f"vm{i}", memT, i // 2, through(9, 10), (i % 2) * HALF)

            km_unit(0)
            pe.wait_ge(qk_normed, 4)
            for name, other in (("KK", kn), ("KQ", qn)):
                for b in range(TB):
                    ps = begin(f"{name}{b}")
                    for h in range(HEADS):
                        tok = slice(b * P, (b + 1) * P)
                        last = pe.matmul(ps[:, h * P:(h + 1) * P], kn[:, h, tok], other[:, h, tok], start=True, stop=True)
                    last.then_inc(unit_filled, 1)
            for b in range(TB):
                ps = begin(f"ktok{b}")
                for h in range(HEADS):
                    last = pe.transpose(ps[:, h * P:(h + 1) * P], kn[:, h, b * P:(b + 1) * P], ident)
                last.then_inc(unit_filled, 1)
            km_unit(1)
            for g in range(TB):
                pe.wait_ge(lmat_ready, g + 1)
                ps = begin(f"LT{g}")
                for h in range(HEADS):
                    last = pe.transpose(ps[:, h * P:(h + 1) * P], L[:, 4 * g + h, :], ident)
                last.then_inc(unit_filled, 1)

            pe.wait_ge(x_init, 1)
            pe.wait_ge(xt_init, 1)
            fill = [lambda: km_unit(2), lambda: km_unit(3)] + [lambda i=i: vm_unit(i) for i in range(4)]
            for level in range(1, LEVELS):
                pe.wait_ge(bt_ready, level)
                for g in range(TB):
                    if level > 1:
                        need(f"X{level - 1}_{g}", f"XT{level - 1}_{g}")
                    ps = begin(f"M{level}_{g}")
                    for h in range(HEADS):
                        i = 4 * g + h
                        last = pe.matmul(ps[:, h * P:(h + 1) * P], BT[:, i, :], X[:, i, :], start=True, stop=True)
                    last.then_inc(unit_filled, 1)
                for g in range(TB):
                    need(f"M{level}_{g}")
                    if level < LEVELS - 1:
                        ps = begin(f"X{level}_{g}")
                        for h in range(HEADS):
                            i = 4 * g + h
                            last = pe.matmul(ps[:, h * P:(h + 1) * P], XT[:, i, :], M1[:, i, :], start=True, stop=True)
                        last.then_inc(unit_filled, 1)
                    ps = begin(f"XT{level}_{g}")
                    for h in range(HEADS):
                        i = 4 * g + h
                        last = pe.matmul(ps[:, h * P:(h + 1) * P], M1[:, i, :], XT[:, i, :], start=True, stop=True)
                    last.then_inc(unit_filled, 1)
                if level == 3:
                    arrived(9)
                    arrived(10)
                fill[level - 1]()
            used_up(4, "vm3")

            for g in range(TB):
                need(f"XT{LEVELS - 1}_{g}")
                ps = begin(f"U{g}")
                for h in range(HEADS):
                    i = 4 * g + h
                    last = pe.matmul(ps[:, h * P:(h + 1) * P], XT[:, i, :], vbeta[:, i, :], start=True, stop=True)
                last.then_inc(unit_filled, 1)
            ps = begin("WT")
            for h in range(HEADS):
                last = pe.matmul(ps[:, h * P:(h + 1) * P], kbg[:, 4 + h, :], XT[:, 4 + h, :], start=True, stop=True)
            last.then_inc(unit_filled, 1)

            def scores(h):
                ps2 = [begin(f"sc{h}_0"), begin(f"sc{h}_1")]
                for q, (a, b) in enumerate(((0, P), (P, 3 * P))):
                    for c in range(2):
                        rows = slice(DIFF_D * c, DIFF_D * (c + 1))
                        last = pe.matmul(ps2[c][:, a:b], dqk3[rows, h, q * P:(q + 1) * P], dqk3[rows, 4 + h, 0:b - a],
                                         start=True, stop=True)
                        if q == 1:
                            last.then_inc(unit_filled, 1)

            def attention_T(h):
                pe.wait_ge(a_ready, h + 1)
                ps = begin(f"aT{h}")
                for j in range(3):
                    last = pe.transpose(ps[:, j * P:(j + 1) * P], dp[h % 2][:, 0, j * P:(j + 1) * P], ident)
                last.then_inc(unit_filled, 1)

            need("dqk3")
            scores(0)
            need("U0")
            ps = begin("S")
            for h in range(HEADS):
                last = pe.matmul(ps[:, h * P:(h + 1) * P], ktail[:, h, :], u_sb[:, h, :], start=True, stop=True)
            last.then_inc(unit_filled, 1)
            ps = begin("O0")
            for h in range(HEADS):
                last = pe.matmul(ps[:, h * P:(h + 1) * P], AT[:, h, :], u_sb[:, h, :], start=True, stop=True)
            last.then_inc(unit_filled, 1)
            scores(1)
            need("WT", "S")
            ps = begin("WS")
            for h in range(HEADS):
                last = pe.matmul(ps[:, h * P:(h + 1) * P], wT[:, h, :], S_sb[:, h, :], start=True, stop=True)
            last.then_inc(unit_filled, 1)
            attention_T(0)
            scores(2)
            pe.wait_ge(vnew_ready, 1)
            ps = begin("O1")
            for h in range(HEADS):
                pe.matmul(ps[:, h * P:(h + 1) * P], qd[:, h, :], S_sb[:, h, :], start=True, stop=False)
                last = pe.matmul(ps[:, h * P:(h + 1) * P], AT[:, 4 + h, :], vnew[:, h, :], start=False, stop=True)
            last.then_inc(unit_filled, 1)
            attention_T(1)
            scores(3)
            attention_T(2)
            attention_T(3)
            need("aT3", "dv1")
            ps = begin("OD0")
            for h in range(HEADS):
                last = pe.matmul(ps[:, h * P:(h + 1) * P], aT[:, h, 0:P], dv3[:, 0, h * P:(h + 1) * P], start=True, stop=True)
            last.then_inc(unit_filled, 1)
            ps = begin("OD1")
            for h in range(HEADS):
                for j in range(2):
                    last = pe.matmul(ps[:, h * P:(h + 1) * P], aT[:, h, (1 + j) * P:(2 + j) * P], dv3[:, j, h * P:(h + 1) * P],
                                     start=(j == 0), stop=(j == 1))
            last.then_inc(unit_filled, 1)

            for i in range(4):
                if i % 2 == 0:
                    pe.wait_ge(mix_ready, 3 + i // 2)
                transpose_block(f"mixT{i}", mem3[:, i // 2, :], range(4 * (i % 2), 4 * (i % 2) + 4))
            arrived(11)
            arrived(12)
            for i in range(4):
                need(f"mixT{2 * (i // 2) + 1}")
                token_major(f"h{i}", xT, i // 2, through(11, 12), (i % 2) * HALF)
            for i in range(4):
                pe.wait_ge(ln_ready, 1 + i // 2)
                transpose_block(f"x1T{i}", x3[:, i // 2, :], range(4 * (i % 2), 4 * (i % 2) + 4))
            used_up(2, "h3")
            need("x1T3")
            arrived(13)
            arrived(14)
            for i in range(4):
                channel_major(f"xq{i}", through(13, 14), (2 * i, 2 * i + 1), memT)
            for h in range(HEADS):
                need(f"xq{h}")
                if h == 0:
                    need("km3")
                ps = begin(f"xs{h}")
                for b in range(TB):
                    for j in range(2):
                        last = pe.matmul(ps[:, b * 256:(b + 1) * 256], dqk3[:, 2 * h + j, b * P:(b + 1) * P], km3[:, 2 * h + j, :],
                                         start=(j == 0), stop=(j == 1))
                last.then_inc(unit_filled, 1)
            used_up(2, "xq3")

            def probs_T(h):
                pe.wait_ge(xp_ready, h + 1)
                ps = begin(f"pT{h}")
                for m in range(2):
                    for b in range(TB):
                        last = pe.transpose(ps[:, (2 * m + b) * P:(2 * m + b + 1) * P], xp[:, h, b, m * P:(m + 1) * P], ident)
                last.then_inc(unit_filled, 1)

            def cross_out(h):
                need(f"pT{h}")
                if h == 0:
                    need("vm3")
                ps = begin(f"oT{h}")
                for j in range(2):
                    for m in range(2):
                        c = 2 * h + j
                        last = pe.matmul(ps[:, j * SEQ:(j + 1) * SEQ], vm3[:, m, c * P:(c + 1) * P], pT[:, h, m, :],
                                         start=(m == 0), stop=(m == 1))
                last.then_inc(unit_filled, 1)

            probs_T(0)
            probs_T(1)
            cross_out(0)
            probs_T(2)
            cross_out(1)
            probs_T(3)
            cross_out(2)
            cross_out(3)
            need("oT3")
            arrived(15)
            arrived(16)
            for i in range(4):
                token_major(f"wo{i}", oT, i // 2, through(15, 16), (i % 2) * HALF)
            pe.wait_ge(ld_bias, 32)
            ps = begin("bT")
            for w in range(2):
                for b in range(2):
                    last = pe.transpose(ps[:, (2 * w + b) * P:(2 * w + b + 1) * P], bias_raw[:, w, b, :], ident)
            last.then_inc(unit_filled, 1)
            for i in range(4):
                pe.wait_ge(ln_ready, 3 + i // 2)
                transpose_block(f"x2T{i}", x3[:, i // 2, :], range(4 * (i % 2), 4 * (i % 2) + 4))
            used_up(2, "wo3")
            need("x2T3")
            pe.wait_ge(ld_rt, 32)
            ps = begin("router")
            for b in range(TB):
                for k in range(KC):
                    last = pe.matmul(ps[:, 32 * b:32 * b + 32], xT[:, k, b * P:(b + 1) * P], dv[:, 32 * k:32 * k + 32],
                                     start=(k == 0), stop=(k == KC - 1))
            last.then_inc(unit_filled, 1)
            pe.wait_ge(route_ready, 1)
            ps = begin("pos")
            pe.matmul(ps[:, 0:32], strict, M[:, 0:32], start=True, stop=True)
            pe.matmul(ps[:, 32:64], strict, M[:, 32:64], start=True, stop=False)
            pe.matmul(ps[:, 32:64], ones, M[:, 0:32], start=False, stop=True)
            pe.matmul(ps[0:32, 64:65], M[:, 0:32], ones[:, 0:1], start=True, stop=False)
            pe.matmul(ps[0:32, 64:65], M[:, 32:64], ones[:, 0:1], start=False, stop=True).then_inc(unit_filled, 1)
            pe.wait_ge(cnt_ready, 1)
            ps = begin("cum")
            pe.matmul(ps[0:32, 0:1], upper[0:32, 0:32], nblk[0:32, 0:1], start=True, stop=True)
            pe.matmul(ps[0:1, 32:64], nblk[0:32, 0:1], upper[0:32, 0:32], start=True, stop=True).then_inc(unit_filled, 1)
            pe.wait_ge(cnt_ready, 2)
            ps = begin("etab")
            pe.matmul(ps[0:1, 0:64], ones[0:32, 0:1], emask, start=True, stop=True).then_inc(unit_filled, 1)
            ps = begin("GT")
            for b in range(TB):
                last = pe.transpose(ps[0:32, b * P:(b + 1) * P], G[:, 32 * b:32 * b + 32], ident)
            last.then_inc(unit_filled, 1)

            def gather():
                for b in range(TB):
                    for h in range(2):
                        last = pe.matmul(banks[5][64 * h:64 * h + 64, :], selw[:, b, 0:CAP], x3[:, b, h * HALF:(h + 1) * HALF],
                                         start=(b == 0), stop=(b == 1))
                last.then_inc(xg_done, 1)

            def gathered_T():
                for j in range(4):
                    last = pe.transpose(banks[6][:, j * P:(j + 1) * P], xg_sb[:, j * P:(j + 1) * P], ident)
                last.then_inc(xgT_done, 1)

            def xg_chunk(k):
                return xgT[:, k % 4, 64 * (k // 4):64 * (k // 4) + 64]

            wait_emptied(pe, "GT")
            wait_emptied(pe, "etab")
            pe.wait_ge(sel_ready, 1)
            gather()
            pe.wait_ge(xg_copied, 1)
            gathered_T()
            pe.wait_ge(tab_ready, 1)
            blocks = pe.value_load(itab[0:1, T_CUM + N_EXPERTS - 1:T_CUM + N_EXPERTS], min_val=N_EXPERTS, max_val=MAX_BLOCKS)
            with pe.Fori(0, blocks) as n:
                e16 = pe.value_load(itab[0:1, bass.ds(n + T_E16, 1)], min_val=0, max_val=16 * (N_EXPERTS - 1))

                def weights(role):
                    pe.wait_ge(ring_full[ROLE_SLOT[role]], e16 + 16 * (ROLE_EARLIER[role] + 1))

                def gate_up(f, k):
                    for side, role in ((0, (G0, G1)[k // 4]), (1, (U0, U1)[k // 4])):
                        last = pe.matmul(banks[f][64 * side:64 * side + 64, :], xg_chunk(k),
                                         slots[ROLE_SLOT[role]][:, k % 4, f * HALF:(f + 1) * HALF],
                                         start=(k == 0), stop=(k == KC - 1))
                    return last

                pe.wait_ge(xgT_ready, n + 1)
                weights(G0)
                weights(U0)
                for k in range(4):
                    for f in range(2):
                        last = gate_up(f, k)
                last.then_inc(gu0_used, 1)
                weights(G1)
                weights(U1)
                for f in range(2):
                    for k in range(4, KC):
                        last = gate_up(f, k)
                    last.then_inc(gu_done, 1)
                pe.wait_ge(acc_done, n + 1)
                pe.wait_ge(gsel_ready, n + 1)
                for b in range(TB):
                    last = pe.transpose(banks[4][:, b * P:(b + 1) * P], gsel[:, b, :], ident)
                last.then_inc(gselT_done, 1)
                pe.wait_ge(sel_ready, n + 2)
                gather()
                for f in range(2):
                    pe.wait_ge(gu_copied, n * 2 + (f + 1))
                    for j in range(4):
                        last = pe.transpose(banks[2 + f][:, j * P:(j + 1) * P], gu[:, f, j * P:(j + 1) * P], ident)
                    last.then_inc(guT_done, 1)
                pe.wait_ge(xg_copied, n + 2)
                gathered_T()
                pe.wait_ge(gselT_ready, n + 1)
                for f in range(2):
                    weights((D0, D1)[f])
                    pe.wait_ge(hT_ready, n * 2 + (f + 1))
                    for k in range(4 * f, 4 * f + 4):
                        for h in range(2):
                            last = pe.matmul(banks[4][64 * h:64 * h + 64, :], hT[:, k, :],
                                             slots[ROLE_SLOT[(D0, D1)[f]]][:, k % 4, h * HALF:(h + 1) * HALF],
                                             start=(k == 0), stop=(k == KC - 1))
                    last.then_inc((d0_used, y_done)[f], 1)
                pe.wait_ge(y_copied, n + 1)
                pe.wait_ge(xgT_ready, n + 2)
                for b, targets in enumerate(((7, 5), (6, 4))):
                    for h in range(2):
                        last = pe.matmul(banks[targets[h]][:, :], gselT[64 * h:64 * h + 64, b * P:(b + 1) * P],
                                         y_sb[64 * h:64 * h + 64, :], start=True, stop=True)
                    last.then_inc(scat_done, 1)
            pe.wait_ge(ld_bdown, 16)
            for b in range(TB):
                for h in range(2):
                    last = pe.matmul(banks[2 * b + h][:, :], GT[:, b * P:(b + 1) * P], bdown[:, h * HALF:(h + 1) * HALF],
                                     start=True, stop=True)
                last.then_inc(bias_done, 1)

        @block.vector
        def _(dve):
            tt, ts, stt = dve.tensor_tensor, dve.tensor_scalar, dve.scalar_tensor_tensor

            def filled(name):
                dve.wait_ge(unit_filled, UNIT_AT[name] + 1)
                return bank(name)

            def as3(ps, n):
                return ps[:, :].rearrange("p (g s) -> p g s", g=n)

            dve.tensor_copy(convw, filled("convw")[:, 0:48]).then_inc(dve_emptied, 1)
            for i in (1, 3):
                dve.tensor_copy(xT[:, 4:8, (i // 2) * P:(i // 2 + 1) * P], as3(filled(f"xT{i}"), 4)).then_inc(dve_emptied, 1)
            dve.wait_ge(ld_vec, 16 * 8)
            for i in range(2):
                tt(lam_raw[:, 128 * i:128 * i + 64], lam_raw[:, 128 * i:128 * i + 64], lam_raw[:, 128 * i + 64:128 * i + 128], ALU.mult)
            dve.drain()
            for i in range(2):
                dve.reduce_sum(lamv[:, i:i + 1], lam_raw[:, 128 * i:128 * i + 64], AX_X)

            names = {0: "qk0", 1: "qk1", 2: "qk2", 3: "qk3", 4: "v0", 5: "v1"}
            dve.wait_ge(pad_zero, 1)
            for j in range(6):
                wait_emptied(dve, names[j])
                for tap in range(GDN_TAPS):
                    for c in (2 * j, 2 * j + 1):
                        w = convw[:, 12 * tap + c:12 * tap + c + 1]
                        if tap == 0:
                            last = ts(cout[:, c, :], cin[:, c, 0:SEQ], w, None, ALU.mult)
                        else:
                            last = stt(cout[:, c, :], cin[:, c, tap:tap + SEQ], w, cout[:, c, :], ALU.mult, ALU.add)
                    if tap < GDN_TAPS - 1:
                        dve.drain()
                last.then_inc(conv_ready, 1)

            ps = filled("ba")
            dve.tensor_copy(ba, ps[:, 0:16]).then_inc(dve_emptied, 1)
            dve.drain()
            ba3 = ba.rearrange("p (b n) -> p b n", b=2)
            dt3 = dt_b.unsqueeze(1).broadcast_to([P, 2, 4])
            s3 = [v.rearrange("p (b n) -> p b n", b=2) for v in (sp_a, sp_b, sp_c)]
            dve.tensor_copy(s3[0], ba3[:, :, 0:4])
            tt(s3[2], ba3[:, :, 4:8], dt3, ALU.add)
            dve.drain()
            stt(sp_b, sp_c, -1.0, sp_c, ALU.mult, ALU.max).then_inc(gate_step, 1)
            ts(sp_c, sp_c, 0.0, None, ALU.max)
            dve.drain()
            dve.wait_ge(exp_ready, 4)
            ts(beta, sp_a, 1.0, None, ALU.add)
            tt(sp_c, sp_c, sp_b, ALU.add)
            dve.drain()
            dve.reciprocal(beta, beta)
            tt(sp_c.rearrange("p (b n) -> p b n", b=2), sp_c.rearrange("p (b n) -> p b n", b=2),
               a_log.unsqueeze(1).broadcast_to([P, 2, 4]), ALU.mult)
            dve.drain()
            ts(g_log, sp_c, -1.0, None, ALU.mult)
            dve.drain()
            dve.tensor_copy(gB, row_b(g_log, PAIRS, P))
            dve.wait_ge(lam_exp, 1)
            tt(neglam, lamv[:, 1:2], lamv[:, 0:1], ALU.subtract)
            dve.drain()
            ts(neglam, neglam, LAMBDA_INIT, None, ALU.subtract)
            wait_emptied(dve, "z1")
            tt(sz[:, :].rearrange("p (g s) -> p g s", g=PAIRS), sz[:, :].rearrange("p (g s) -> p g s", g=PAIRS),
               tile_b(gnw, PAIRS, P), ALU.mult)
            dve.wait_ge(unit_filled, UNIT_AT["ba"] + 1)
            ts(dnw_keep[:, :], dnw, 1.0 - LAMBDA_INIT, None, ALU.mult)
            dve.drain()
            dve.sem_inc(gate_step, 1)

            for i in range(4):
                rs = sq_mem[:, 512 * i:512 * (i + 1)]
                dve.wait_ge(l2_exp, i + 1)
                part = conv_out[:, 512 * i:512 * (i + 1)]
                stt(part, part, GDN_DK ** -0.5 if i < 2 else 1.0, rs, ALU.mult, ALU.mult).then_inc(qk_normed, 1)

            dve.tensor_copy(gcum, filled("gcum")[:, 0:PAIRS]).then_inc(dve_emptied, 1)
            dve.drain()
            dve.sem_inc(gate_step, 1)
            for g in range(TB):
                ps = as3(filled(f"R{g}"), 4)
                if g == 0:
                    tt(tails[:, 0:4], ps[:, :, P - 1:P].rearrange("p g s -> p (g s)"), gcum[:, 0:4], ALU.subtract)
                tt(diff[:, 4 * g:4 * g + 4, :], ps, row_b(gcum[:, 4 * g:4 * g + 4], 4, P), ALU.subtract)
            dve.drain()
            dve.sem_inc(dec_in, 1)
            dve.wait_ge(qd_exp, 1)
            dve.sem_inc(dve_emptied, 2)
            ts(Dm, diff, 0.0, None, ALU.max).then_inc(dec_in, 1)
            ts(DT, diff, 0.0, None, ALU.min).then_inc(dec_in, 1)
            dve.drain()
            tt(qd, qd, qn[:, :, P:SEQ], ALU.mult)
            dve.wait_ge(exp_ready, 6)
            tt(begs, beta, eg, ALU.mult)
            for g in range(TB):
                tt(vbeta[:, 4 * g:4 * g + 4, :], as3(filled(f"vtok{g}"), 4), row_b(beta[:, 4 * g:4 * g + 4], 4, P),
                   ALU.mult).then_inc(dve_emptied, 1)
            dve.wait_ge(dec_ready, 1)
            for g in range(TB):
                ps = as3(filled(f"KK{g}"), 4)
                for h in range(HEADS):
                    i = 4 * g + h
                    last = stt(L[:, i, :], ps[:, h, :], beta[:, i:i + 1], Dm[:, i, :], ALU.mult, ALU.mult)
                dve.drain()
                dve.sem_inc(dve_emptied, 1)
                dve.sem_inc(lmat_ready, 1)
            dve.wait_ge(dec_ready, 2)
            for g in range(TB):
                tt(AT[:, 4 * g:4 * g + 4, :], as3(filled(f"KQ{g}"), 4), DT[:, 4 * g:4 * g + 4, :], ALU.mult).then_inc(dve_emptied, 1)
            ps = as3(filled("ktok0"), 4)
            tt(ktail, ps, row_b(tails[:, 0:4], 4, P), ALU.mult)
            tt(kbg[:, 0:4, :], ps, row_b(begs[:, 0:4], 4, P), ALU.mult).then_inc(dve_emptied, 1)
            tt(kbg[:, 4:8, :], as3(filled("ktok1"), 4), row_b(begs[:, 4:8], 4, P), ALU.mult).then_inc(dve_emptied, 1)
            dve.wait_ge(ld_lev, 16)
            tt(X, L, tile_b(lev0, PAIRS, P), ALU.mult)
            dve.drain()
            tt(X, tile_b(ident, PAIRS, P), X, ALU.subtract).then_inc(x_init, 1)
            dve.wait_ge(xt_init, 1)
            dve.drain()
            for level in range(1, LEVELS):
                for g in range(TB):
                    gs = slice(4 * g, 4 * g + 4)
                    if level < LEVELS - 1:
                        ps = as3(filled(f"X{level}_{g}"), 4)
                        tt(X[:, gs, :], X[:, gs, :], ps, ALU.subtract).then_inc(dve_emptied, 1)
                    ps = as3(filled(f"XT{level}_{g}"), 4)
                    tt(XT[:, gs, :], XT[:, gs, :], ps, ALU.subtract).then_inc(dve_emptied, 1)
                dve.drain()

            def shifted(h, c):
                if h >= 2:
                    dve.wait_ge(unit_filled, UNIT_AT[f"aT{h - 2}"] + 1)
                s = 4 * (h % 2) + 2 * c
                ps = filled(f"sc{h}_{c}")
                p = dp[h % 2][:, c, :]
                tt(p, ps[:, 0:384], causal, ALU.add).then_inc(dve_emptied, 1)
                dve.drain()
                dve.reduce_max(stat_mx[:, s:s + 1], p[:, 0:P], AX_X)
                dve.reduce_max(stat_mx[:, s + 1:s + 2], p[:, P:384], AX_X)
                dve.drain()
                ts(stat_nb[:, s:s + 2], stat_mx[:, s:s + 2], -DIFF_SCALE, None, ALU.mult).then_inc(sm_in, 1)

            def combine(h):
                dve.wait_ge(sm_exp, 4 * h + 4)
                s = 4 * (h % 2)
                dve.reciprocal(stat_r[:, s:s + 4], stat_l[:, s:s + 4])
                dve.drain()
                ts(stat_r[:, s + 2:s + 4], stat_r[:, s + 2:s + 4], neglam, None, ALU.mult)
                for q, (a, b) in enumerate(((0, P), (P, 384))):
                    ts(dp[h % 2][:, 0, a:b], dp[h % 2][:, 0, a:b], stat_r[:, s + q:s + q + 1], None, ALU.mult)
                dve.drain()
                for q, (a, b) in enumerate(((0, P), (P, 384))):
                    last = stt(dp[h % 2][:, 0, a:b], dp[h % 2][:, 1, a:b], stat_r[:, s + 2 + q:s + 3 + q], dp[h % 2][:, 0, a:b],
                               ALU.mult, ALU.add)
                last.then_inc(a_ready, 1)

            roots = [0]

            def normed(src, b, col, weights, signal):
                s3 = src.rearrange("p (g s) -> p g s", g=4)
                q3 = o_sq[:, 0:512].rearrange("p (g s) -> p g s", g=4)
                tt(q3, s3, s3, ALU.mult)
                dve.drain()
                dve.tensor_reduce(rs8[:, 0:4], q3, AX_X, ALU.add)
                dve.drain()
                ts(rs8[:, 0:4], rs8[:, 0:4], 1.0 / P, RMS_EPS, ALU.mult, ALU.add).then_inc(var_in, 1)
                roots[0] += 1
                dve.wait_ge(var_out, roots[0])
                tt(s3, s3, row_b(rs8[:, 0:4], 4, P), ALU.mult)
                dve.drain()
                dst = mem3[:, b, col:col + 512].rearrange("p (g s) -> p g s", g=4)
                tt(dst, s3, weights, ALU.mult).then_inc(signal, 1)

            dve.wait_ge(unit_filled, UNIT_AT["WT"] + 1)
            shifted(0, 0)
            shifted(0, 1)
            shifted(1, 0)
            shifted(1, 1)
            combine(0)
            ps = as3(filled("WS"), 4)
            wait_emptied(dve, "U1")
            tt(vnew, u_sb[:, 4:8, :], ps, ALU.subtract).then_inc(vnew_ready, 1)
            dve.drain()
            dve.sem_inc(dve_emptied, 1)
            shifted(2, 0)
            shifted(2, 1)
            combine(1)
            shifted(3, 0)
            shifted(3, 1)
            combine(2)
            combine(3)
            wait_emptied(dve, "O1")
            o_flat = gdn_mem[:, 1024:2048]
            for b in range(TB):
                sz_b = sz3[:, b, :].rearrange("p (g s) -> p g s", g=4)
                normed(o_flat[:, 512 * b:512 * b + 512], b, 0, sz_b, mix_ready)
            for b in range(TB):
                wait_emptied(dve, f"OD{b}")
                normed(od_sb[:, 512 * b:512 * b + 512], b, 512, tile_b(dnw_keep[:, :], 4, P), mix_ready)

            def layer_norm(b, loads, signal):
                dve.wait_ge(ld_ln, loads)
                dve.drain()
                xb = x3[:, b, :]
                bn3 = bn.rearrange("p (a s) -> p a s", a=2)
                for h in range(2):
                    dve.bn_stats(bn3[:, h, :], xb[:, h * HALF:(h + 1) * HALF])
                dve.drain()
                dve.bn_aggr(mv, bn3)
                dve.drain()
                ts(rstd, mv[:, 1:2], LN_EPS, None, ALU.add).then_inc(var_in, 1)
                roots[0] += 1
                dve.wait_ge(var_out, roots[0])
                ts(xb, xb, mv[:, 0:1], rstd, ALU.subtract, ALU.mult)
                dve.drain()
                tt(xb, xb, ln_g, ALU.mult)
                dve.drain()
                tt(xb, xb, ln_b, ALU.add).then_inc(signal, 1)

            def residual(name, b, h):
                part = x3[:, b, h * HALF:(h + 1) * HALF]
                stt(part, part, ALPHA, filled(name)[:, :], ALU.mult, ALU.add).then_inc(dve_emptied, 1)

            for b in range(TB):
                residual(f"h{2 * b}", b, 0)
                residual(f"h{2 * b + 1}", b, 1)
                layer_norm(b, 32, ln_ready)

            for h in range(HEADS):
                ps = as3(filled(f"xs{h}"), 2)
                dve.reduce_max(stat_mx[:, 2 * h:2 * h + 2], ps, AX_X)
                dve.drain()
                ts(stat_nb[:, 2 * h:2 * h + 2], stat_mx[:, 2 * h:2 * h + 2], -XA_SCALE, None, ALU.mult).then_inc(xsm_in, 1)
            for h in range(HEADS):
                dve.wait_ge(xsm_exp, 2 * h + 2)
                dve.sem_inc(dve_emptied, 1)
                dve.reciprocal(stat_r[:, 2 * h:2 * h + 2], stat_l[:, 2 * h:2 * h + 2])
                dve.drain()
                tt(xp[:, h, :, :], xp[:, h, :, :], row_b(stat_r[:, 2 * h:2 * h + 2], 2, 256), ALU.mult).then_inc(xp_ready, 1)
            for b in range(TB):
                residual(f"wo{2 * b}", b, 0)
                residual(f"wo{2 * b + 1}", b, 1)
                layer_norm(b, 64, ln_ready)

            ps = filled("router")
            l3, e3, M3, G3 = (v.rearrange("p (b n) -> p b n", b=2) for v in (logit, expl, M, G))
            tt(l3, ps[:, 0:64].rearrange("p (b n) -> p b n", b=2), rb.unsqueeze(1).broadcast_to([P, 2, 32]), ALU.add)\
                .then_inc(dve_emptied, 1)
            dve.drain()
            for b in range(TB):
                dve.max(top8[:, 8 * b:8 * b + 8], l3[:, b, :])
            dve.drain()
            for b in range(TB):
                ts(e3[:, b, :], l3[:, b, :], top8[:, 8 * b:8 * b + 1], None, ALU.subtract)
            dve.drain()
            dve.sem_inc(rt_in, 1)
            t8 = top8.rearrange("p (b n) -> p b n", b=2)
            dve.memset(t8[:, :, TOP_K:8], NEG)
            dve.drain()
            for b in range(TB):
                dve.match_replace(M3[:, b, :], t8[:, b, :], l3[:, b, :], NEG)
            dve.drain()
            ts(M, M, NEG, None, ALU.is_equal)
            dve.wait_ge(rt_exp, 1)
            dve.drain()
            tt(G, expl, M, ALU.mult)
            dve.drain()
            dve.tensor_reduce(gsum, G3, AX_X, ALU.add)
            dve.drain()
            dve.reciprocal(gsum, gsum)
            dve.drain()
            tt(G3, G3, gsum.unsqueeze(2).broadcast_to([P, 2, 32]), ALU.mult)
            dve.drain()
            dve.sem_inc(route_ready, 1)
            dve.wait_ge(ld_iota, 16)
            ps = filled("pos")
            dve.tensor_copy(pos, ps[:, 0:64])
            dve.tensor_copy(cumc[0:32, 0:1], ps[0:32, 64:65])
            dve.drain()
            dve.sem_inc(dve_emptied, 1)
            ts(nblk[0:32, 0:1], cumc[0:32, 0:1], float(CAP), 1.0, ALU.is_gt, ALU.add)
            for r in range(2, SEQ // CAP):
                dve.drain()
                stt(nblk[0:32, 0:1], cumc[0:32, 0:1], float(r * CAP), nblk[0:32, 0:1], ALU.is_gt, ALU.add)
            dve.drain()
            dve.sem_inc(cnt_ready, 1)
            ps = filled("cum")
            dve.tensor_copy(cumc[0:32, 1:2], ps[0:32, 0:1])
            dve.tensor_copy(itab[0:1, T_CUM:T_CUM + 32], ps[0:1, 32:64])
            dve.drain()
            dve.sem_inc(dve_emptied, 1)
            ts(emask, niota[0:32, :], cumc[0:32, 1:2], None, ALU.is_ge).then_inc(cnt_ready, 1)
            ps = filled("etab")
            ts(erow, ps[0:1, 0:64], float(N_EXPERTS - 1), None, ALU.min).then_inc(dve_emptied, 1)
            dve.drain()
            dve.tensor_copy(itab[0:1, T_E:T_E + 64], erow)
            ts(itab[0:1, T_E16:T_E16 + 64], erow, 16.0, None, ALU.mult)
            dve.memset(yacc, 0.0).then_inc(acc_done, 1)
            dve.drain()
            dve.sem_inc(tab_ready, 1)

            M2, pos2, G2 = M3, pos.rearrange("p (b n) -> p b n", b=2), G3

            def select(e, first=False):
                for b in range(TB):
                    ts(selw[:, b, :], iota2, pos2[:, b, bass.ds(e, 1)], M2[:, b, bass.ds(e, 1)], ALU.is_equal, ALU.mult)
                dve.drain()
                for b in range(TB):
                    last = ts(pos2[:, b, bass.ds(e, 1)], pos2[:, b, bass.ds(e, 1)], float(CAP), None, ALU.subtract)
                last.then_inc(sel_ready, 1)

            def copy_xgT():
                dve.tensor_copy(xgT, banks[6][:, :].rearrange("p (k s) -> p k s", k=4)).then_inc(xgT_ready, 1)

            select(0)
            dve.wait_ge(xgT_done, 1)
            copy_xgT()
            blocks = dve.value_load(itab[0:1, T_CUM + N_EXPERTS - 1:T_CUM + N_EXPERTS], min_val=N_EXPERTS, max_val=MAX_BLOCKS)
            with dve.Fori(0, blocks) as n:
                e = dve.value_load(itab[0:1, bass.ds(n + T_E, 1)], min_val=0, max_val=N_EXPERTS - 1)
                e_next = dve.value_load(itab[0:1, bass.ds(n + (T_E + 1), 1)], min_val=0, max_val=N_EXPERTS - 1)
                dve.drain()
                for b in range(TB):
                    last = ts(gsel[:, b, :], selw[:, b, :], G2[:, b, bass.ds(e, 1)], None, ALU.mult)
                last.then_inc(gsel_ready, 1)
                dve.drain()
                select(e_next)
                bias4 = [ebias[:, w, :].rearrange("p (e k) -> p e k", k=KC) for w in range(2)]
                for f in range(2):
                    dve.wait_ge(guT_done, n * 2 + (f + 1))
                    gT = banks[2 + f][:, :].rearrange("p (k g s) -> p k g s", k=4, g=2)

                    def bias(w):
                        b = bias4[w][:, bass.ds(e, 1), 4 * f:4 * f + 4].rearrange("p e k -> p (e k)")
                        return b.unsqueeze(2).broadcast_to([P, 4, CAP])

                    tt(mg[:, f, :, :], gT[:, :, 0, :], bias(0), ALU.add)
                    tt(mu[:, f, :, :], gT[:, :, 1, :], bias(1), ALU.add)
                    dve.drain()
                    ts(mg[:, f, :, :], mg[:, f, :, :], SWIGLU_LIMIT, None, ALU.min).then_inc(mg_ready, 1)
                    ts(mu[:, f, :, :], mu[:, f, :, :], SWIGLU_LIMIT, -SWIGLU_LIMIT, ALU.min, ALU.max)
                    dve.drain()
                    stt(tmp[:, f, :, :], mu[:, f, :, :], 1.0, mg[:, f, :, :], ALU.add, ALU.mult)
                dve.drain()
                for f in range(2):
                    dve.wait_ge(sig_ready, n * 2 + (f + 1))
                    tt(hT[:, 4 * f:4 * f + 4, :], tmp[:, f, :, :], sig[:, f, :, :], ALU.mult).then_inc(hT_ready, 1)
                dve.wait_ge(xgT_done, n + 2)
                copy_xgT()
                for b, targets in enumerate(((7, 5), (6, 4))):
                    dve.wait_ge(scat_done, n * 2 + (b + 1))
                    for h in range(2):
                        part = yacc[:, b, h * HALF:(h + 1) * HALF]
                        last = tt(part, part, banks[targets[h]][:, :], ALU.add)
                last.then_inc(acc_done, 1)
            dve.drain()
            for b in range(TB):
                dve.wait_ge(bias_done, b + 1)
                for h in range(2):
                    part = yacc[:, b, h * HALF:(h + 1) * HALF]
                    tt(part, part, banks[2 * b + h][:, :], ALU.add)
                dve.drain()
                stt(x3[:, b, :], x3[:, b, :], ALPHA, yacc[:, b, :], ALU.mult, ALU.add)
                layer_norm(b, 96, out_ready)


_INS = ['x', 'mem', 'w_in', 'gdn_conv_w', 'gdn_a_log', 'gdn_dt_bias', 'gdn_norm_w', 'diff_lq1', 'diff_lk1', 'diff_lq2',
        'diff_lk2', 'diff_norm_w', 'w_out', 'ln1_g', 'ln1_b', 'xa_wq', 'xa_wk', 'xa_wv', 'xa_wo', 'ln2_g', 'ln2_b',
        'router_w', 'router_b', 'exp_w_gate', 'exp_b_gate', 'exp_w_up', 'exp_b_up', 'exp_w_down', 'exp_b_down',
        'ln3_g', 'ln3_b']


def kernel(**inputs):
    import numpy as _np
    import concourse.bacc as _bacc
    from concourse import mybir as _mybir
    from concourse.bass_utils import run_bass_kernel_spmd as _run

    nc = _bacc.Bacc("TRN2", target_bir_lowering=False, num_devices=1, dynamic_dma_scratch_size=256)
    arrays, args = {}, {}
    for name in _INS:
        a = _np.ascontiguousarray(inputs[name])
        arrays[f"in_{name}_dram"] = a
        args[name] = nc.dram_tensor(f"in_{name}_dram", a.shape, _mybir.dt.from_np(a.dtype), kind="ExternalInput").ap()
    a = constants()
    arrays["in_consts_dram"] = a
    args["consts"] = nc.dram_tensor("in_consts_dram", a.shape, _mybir.dt.from_np(a.dtype), kind="ExternalInput").ap()
    out = nc.dram_tensor("out_dram", (1, SEQ, D_MODEL), F32, kind="ExternalOutput").ap()
    trunk_kernel(nc, args, out)
    r = _run(nc, [arrays], core_ids=[0])
    return r.results[0]["out_dram"]
```

```python
from contextlib import ExitStack

import numpy as np

import concourse.bass as bass
from concourse import mybir

F32 = mybir.dt.float32
I32 = mybir.dt.int32
ALU = mybir.AluOpType
ACT = mybir.ActivationFunctionType
AX_X = mybir.AxisListType.X

P = 128
D_MODEL = 1024
SEQ = 256
TB = SEQ // P
KC = D_MODEL // P
HALF = D_MODEL // 2
DEPTH = 1
ALPHA = (2 * DEPTH) ** 0.25
LN_EPS = 1e-5
RMS_EPS = 1e-6

HEADS = 4
GDN_DK = 128
GDN_TAPS = 4
CONV_CHUNKS = 12
PAD = GDN_TAPS - 1
PAIRS = TB * HEADS
LEVELS = 7
DIFF_D = 64
DIFF_SCALE = DIFF_D ** -0.5
LAMBDA_INIT = 0.8 - 0.6
XA_SCALE = 256 ** -0.5
NEG = -3.0e38

N_EXPERTS = 32
TOP_K = 4
CAP = 64
MAX_BLOCKS = N_EXPERTS + SEQ * TOP_K // CAP
SWIGLU_ALPHA = 1.702
SWIGLU_LIMIT = 7.0

C_QK, C_VZ, C_BA, C_DQK, C_DV, IN_COLS = 0, 1024, 2048, 2056, 3080, 3592

K_ID, K_UT, K_US, K_ONE, K_CM, K_LEV0, K_LEVT = 0, 128, 256, 384, 512, 896, 1024
N_CONST = K_LEV0
N_LEVEL_MASKS = P * (LEVELS + 1)
K_IOTA = K_LEV0 + N_LEVEL_MASKS
K_NIOTA = K_IOTA + P
K_END = K_NIOTA + 64


def constants():
    r = np.arange(P)[:, None]
    c = np.arange(P)[None, :]
    out = np.zeros((P, K_END), np.float32)
    out[:, K_ID:K_ID + P] = r == c
    out[:, K_UT:K_UT + P] = r <= c
    out[:, K_US:K_US + P] = r < c
    out[:, K_ONE:K_ONE + P] = 1.0
    future = np.where(c > r, NEG, 0.0)
    out[:, K_CM:K_CM + P] = future
    out[:, K_CM + 2 * P:K_CM + 3 * P] = future
    out[:, K_IOTA:K_IOTA + P] = np.arange(P) % CAP
    out[:, K_NIOTA:K_NIOTA + 64] = np.arange(64)

    def below(t, s, size):
        return (t // (2 * size) == s // (2 * size)) & (t % (2 * size) >= size) & (s % (2 * size) < size)

    out[:, K_LEV0:K_LEV0 + P] = below(r, c, 1)
    for level in range(LEVELS):
        at = K_LEVT + P * level
        out[:, at:at + P] = below(c, r, 1 << level)
    return out


LEVEL_FILL = {
    1: [("dqk3", "A")],
    2: [("dv0", "A")],
    3: [("dv1", "A")] + [(f"memT{i}", "A") for i in range(4)],
    4: [("sc0_0", "D"), ("sc0_1", "D"), ("km0", "A")],
    5: [("sc1_0", "D"), ("sc1_1", "D"), ("aT0", "A"), ("km1", "A")],
    6: [("sc2_0", "D"), ("sc2_1", "D"), ("aT1", "A"), ("km2", "A")],
}


def unit_table():
    u = [(f"xT{i}", "D") for i in range(4)] + [("ba", "D"), ("columns", "D")]
    u += [(f"qk{i}", "A") for i in range(4)] + [(f"v{i}", "A") for i in range(2)]
    u += [("z0", "A"), ("gcum", "D"), ("R0", "D"), ("R1", "D"), ("z1", "A")]
    u += [(f"ss{i}", "A") for i in range(4)]
    u += [("dqk0", "A"), ("vtok0", "D"), ("vtok1", "D")]
    u += [("KK0", "D"), ("KK1", "D"), ("KQ0", "D"), ("KQ1", "D"), ("ktok0", "D"), ("ktok1", "D"), ("dqk1", "A")]
    u += [("LT0", "A"), ("LT1", "A"), ("dqk2", "A")]
    for level in range(1, LEVELS):
        u += [(f"M{level}_0", "A"), (f"M{level}_1", "A")]
        for g in range(TB):
            if level < LEVELS - 1:
                u += [(f"X{level}_{g}", "D")]
            u += [(f"XT{level}_{g}", "D")]
        u += LEVEL_FILL[level]
    u += [("U0", "A"), ("U1", "A"), ("WT", "A"), ("sc3_0", "D"), ("sc3_1", "D"), ("S", "A"), ("O0", "A"), ("aT2", "A")]
    u += [("WS", "D"), ("km3", "A"), ("O1", "A"), ("aT3", "A"), ("OD0", "A"), ("OD1", "A"), ("vm0", "A")]
    u += [("mixT0", "A"), ("mixT1", "A"), ("vm1", "A"), ("mixT2", "A"), ("mixT3", "A")]
    u += [("h0", "D"), ("h1", "D"), ("h2", "D"), ("x1T0", "A"), ("x1T1", "A"), ("h3", "D"), ("vm2", "A"), ("x1T2", "A"), ("x1T3", "A")] + [(f"xq{i}", "A") for i in range(4)]
    u += [(f"xs{i}", "D") for i in range(4)] + [("vm3", "A")]
    u += [("pT0", "A"), ("pT1", "A"), ("oT0", "A"), ("pT2", "A"), ("oT1", "A"), ("pT3", "A"), ("oT2", "A"), ("oT3", "A")]
    u += [("wo0", "D"), ("wo1", "D"), ("wo2", "D"), ("x2T0", "A"), ("x2T1", "A"), ("wo3", "D"), ("bT", "A")]
    u += [("x2T2", "A"), ("x2T3", "A"), ("router", "D")]
    u += [("pos", "D"), ("xg0", "A"), ("cum", "D"), ("xgT0", "D"), ("etab", "D"), ("GT", "A")]
    u += [(f"eb{i}", "D") for i in range(4)]
    return u


UNITS = unit_table()
UNIT_AT = {name: i for i, (name, _) in enumerate(UNITS)}
N_UNITS = len(UNITS)


def emptied(name):
    at = UNIT_AT[name]
    engine = UNITS[at][1]
    return engine, sum(e == engine for _, e in UNITS[:at + 1])


ATTENTION_LOADS = [
    ("w_in", C_QK, 1024, 0), ("w_in", C_QK, 1024, 1), ("w_in", C_VZ, 1024, 0), ("w_in", C_VZ, 1024, 1),
    ("w_in", C_DQK, 1024, 0), ("w_in", C_DQK, 1024, 1), ("w_in", C_DV, 512, None),
    ("xa_wk", 0, 1024, 0), ("xa_wk", 0, 1024, 1), ("w_out", 0, 1024, 0), ("w_out", 0, 1024, 1),
    ("xa_wv", 0, 1024, 0), ("xa_wv", 0, 1024, 1), ("xa_wq", 0, 1024, 0), ("xa_wq", 0, 1024, 1),
    ("xa_wo", 0, 1024, 0), ("xa_wo", 0, 1024, 1),
]
N_ATT = len(ATTENTION_LOADS)
SLOTS = 6
G0, U0, G1, U1, D0, D1 = range(6)
ROLE_INPUT = ["exp_w_gate", "exp_w_up", "exp_w_gate", "exp_w_up", "exp_w_down", "exp_w_down"]
ROLE_SLOT = [(N_ATT + r) % SLOTS for r in range(SLOTS)]
ROLE_EARLIER = [sum(i % SLOTS == s for i in range(N_ATT)) for s in ROLE_SLOT]


def trunk_kernel(nc, d, out):
    ctx = ExitStack()
    with ctx:
        def sb(name, cols, dt=F32, rows=P):
            return ctx.enter_context(nc.sbuf_tensor(name, [rows, cols], dt))

        def sem(name):
            return ctx.enter_context(nc.semaphore(name))

        ring = sb("ring", SLOTS * 4 * D_MODEL)
        x_sb = sb("x_sb", TB * D_MODEL)
        xT_mem = sb("xT_mem", KC * SEQ)
        mem_mem = sb("mem_mem", TB * D_MODEL)
        memT_mem = sb("memT_mem", KC * SEQ)
        conv_in = sb("conv_in", CONV_CHUNKS * (SEQ + PAD))
        conv_out = sb("conv_out", CONV_CHUNKS * SEQ)
        gdn_mem = sb("gdn_mem", 6144)
        sz = sb("sz", TB * 512)
        dqk = sb("dqk", KC * SEQ)
        dv = sb("dv", TB * 512)
        km = sb("km", KC * SEQ)
        vm = sb("vm", TB * D_MODEL)
        ln_mem = sb("ln_mem", 2 * D_MODEL)
        kst = sb("kst", N_CONST)
        small = sb("small", 672)
        itab = sb("itab", 160, I32)

        slots = [ring[:, s * 4096:(s + 1) * 4096].rearrange("p (k n) -> p k n", k=4) for s in range(SLOTS)]
        x3 = x_sb[:, :].rearrange("p (b n) -> p b n", b=TB)
        xT = xT_mem[:, :].rearrange("p (k t) -> p k t", k=KC)
        mem3 = mem_mem[:, :].rearrange("p (b n) -> p b n", b=TB)
        memT = memT_mem[:, :].rearrange("p (k t) -> p k t", k=KC)
        cin = conv_in[:, :].rearrange("p (c t) -> p c t", c=CONV_CHUNKS)
        cout = conv_out[:, :].rearrange("p (c t) -> p c t", c=CONV_CHUNKS)
        qn, kn, vT = cout[:, 0:4, :], cout[:, 4:8, :], cout[:, 8:12, :]

        def pairs(mem, at, n=PAIRS):
            return mem[:, at:at + n * P].rearrange("p (g s) -> p g s", g=n)

        Dm, DT, L = pairs(conv_in, 0), pairs(conv_in, 1024), pairs(conv_in, 2048)
        X, XT, u_sb = Dm, DT, L
        wT, S_sb = pairs(conv_in, 0, 4), pairs(conv_in, 512, 4)
        BT = pairs(conv_out, 2048)
        LT, M1, AT, kbg, vbeta = (pairs(gdn_mem, 1024 * i) for i in range(5))
        ktail, qd = pairs(gdn_mem, 5120, 4), pairs(gdn_mem, 5632, 4)
        gB, diff, vnew, o_sb = M1, LT, pairs(gdn_mem, 0, 4), M1
        sq_mem = gdn_mem[:, 3072:5120]
        sq = sq_mem.rearrange("p (c t) -> p c t", c=8)
        sz3 = sz[:, :].rearrange("p (b n) -> p b n", b=TB)
        dqk3 = dqk[:, :].rearrange("p (k t) -> p k t", k=KC)
        dv3 = dv[:, :].rearrange("p (b n) -> p b n", b=TB)
        km3 = km[:, :].rearrange("p (k t) -> p k t", k=KC)
        vm3 = vm[:, :].rearrange("p (b n) -> p b n", b=TB)
        dp = [vm[:, 768 * i:768 * (i + 1)].rearrange("p (c n) -> p c n", c=2) for i in range(2)]
        aT = xT_mem[:, 0:4 * 384].rearrange("p (h n) -> p h n", h=4)
        od_sb = conv_out[:, 2048:3072]
        o_sq = conv_in[:, 2048:3072]
        xp = gdn_mem[:, 3072:5120].rearrange("p (h b m) -> p h b m", h=4, b=TB)
        pT = mem_mem[:, :].rearrange("p (h m t) -> p h m t", h=4, m=TB)
        oT = conv_in[:, 0:2048].rearrange("p (k t) -> p k t", k=KC)

        ident = kst[:, K_ID:K_ID + P]
        upper = kst[:, K_UT:K_UT + P]
        strict = kst[:, K_US:K_US + P]
        ones = kst[:, K_ONE:K_ONE + P]
        causal = kst[:, K_CM:K_CM + 3 * P]
        iota2 = gdn_mem[:, 2432:2432 + P]
        niota = gdn_mem[:, 2432 + P:2432 + P + 64]
        lev0 = ln_mem[:, 0:P]
        levT = [ln_mem[:, P * (1 + i):P * (2 + i)] for i in range(LEVELS)]
        ln_g, ln_b = ln_mem[:, 0:D_MODEL], ln_mem[:, D_MODEL:2 * D_MODEL]

        at = [0]

        def take(n):
            at[0] += n
            return small[:, at[0] - n:at[0]]

        columns = take(80)
        convw = columns[:, 0:48]
        gcol1, bcol1, gcol2, bcol2 = (columns[:, 48 + 8 * i:56 + 8 * i] for i in range(4))
        ba = take(16)
        beta = take(8)
        g_log = take(8)
        gcum = take(8)
        eg = take(8)
        begs = take(8)
        tails = take(8)
        sp_a, sp_b, sp_c = take(8), take(8), take(8)
        a_log, dt_b = take(4), take(4)
        lamv = take(4)
        neglam = take(1)
        rs8 = take(8)
        stat_mx, stat_nb, stat_l, stat_r = take(8), take(8), take(8), take(8)
        bn = take(12)
        mv = take(2)
        rstd = take(1)
        top8 = take(16)
        gsum = take(2)
        nblk, cumc = take(2), take(2)
        rb = take(32)
        eps_rms = take(1)
        minus_half = take(4)
        logit, expl, M, G, pos = (take(64) for _ in range(5))
        assert at[0] <= 672

        def row_b(v, n, k):
            return v.unsqueeze(2).broadcast_to([P, n, k])

        def tile_b(v, n, k):
            return v.unsqueeze(1).broadcast_to([P, n, k])

        columns_raw = sz[0:80, 0:128]
        lam_raw = vm[:, 0:256]
        gnw = vm[:, 256:384]
        dnw = km[:, 0:128]
        dnw_keep = sb("dnw_keep", 128)

        yacc = vm3
        xgT = km[:, 0:512].rearrange("p (k s) -> p k s", k=4)
        gu = km[:, 512:1536].rearrange("p (f n) -> p f n", f=2)
        hT = km[:, 1536:2048].rearrange("p (k s) -> p k s", k=KC)
        mg, mu, sig, tmp = (conv_in[:, 512 * i:512 * (i + 1)].rearrange("p (f k s) -> p f k s", f=2, k=4) for i in range(4))
        y_sb = conv_in[:, 2048:2560]
        xg_sb = conv_in[:, 2560:3072]
        selw = gdn_mem[:, 0:256].rearrange("p (b s) -> p b s", b=TB)
        gsel = gdn_mem[:, 256:512].rearrange("p (b s) -> p b s", b=TB)
        gselT = gdn_mem[:, 512:768]
        ebias = gdn_mem[:, 768:1280].rearrange("p (w n) -> p w n", w=2)
        GT = gdn_mem[0:N_EXPERTS, 1280:1536]
        emask = gdn_mem[0:N_EXPERTS, 1536:1600]
        erow = gdn_mem[0:1, 1600:1664]
        crow = gdn_mem[0:1, 1664:1696]
        bias_raw = gdn_mem[:, 1792:2304].rearrange("p (w b n) -> p w b n", w=2, b=2)
        bdown = dqk[0:N_EXPERTS, 0:D_MODEL]
        T_E, T_E16, T_CUM = 0, 64, 128
        rtmp = gdn_mem[:, 2304:2368]
        rtmp2 = gdn_mem[:, 2368:2432]

        banks = [ctx.enter_context(nc.psum_tensor(f"bank{i}", [P, 512], F32)) for i in range(8)]

        def bank(name):
            return banks[UNIT_AT[name] % 8]

        unit_filled = sem("unit_filled")
        act_emptied = sem("act_emptied")
        dve_emptied = sem("dve_emptied")
        ring_full = [sem(f"ring_full{s}") for s in range(SLOTS)]
        ring_used = sem("ring_used")
        ld_x, ld_const, ld_lev, ld_mem, ld_vec, ld_ba = (sem(n) for n in ("ld_x", "ld_const", "ld_lev", "ld_mem", "ld_vec", "ld_ba"))
        ld_ln = sem("ld_ln")
        ld_iota = sem("ld_iota")
        ld_rt, ld_bias, ld_bdown = sem("ld_rt"), sem("ld_bias"), sem("ld_bdown")
        ld_cols = sem("ld_cols")
        pad_zero = sem("pad_zero")
        conv_ready = sem("conv_ready")
        silu_ready = sem("silu_ready")
        sq_ready = sem("sq_ready")
        exp_ready = sem("exp_ready")
        gate_step = sem("gate_step")
        qk_normed = sem("qk_normed")
        dec_in, dec_exp, dec_ready = sem("dec_in"), sem("dec_exp"), sem("dec_ready")
        qd_in, qd_exp = sem("qd_in"), sem("qd_exp")
        l2_exp = sem("l2_exp")
        eps_set = sem("eps_set")
        var_in, var_out = sem("var_in"), sem("var_out")
        lmat_ready = sem("lmat_ready")
        x_init = sem("x_init")
        xt_init = sem("xt_init")
        bt_ready = sem("bt_ready")
        vnew_ready = sem("vnew_ready")
        lam_in, lam_exp = sem("lam_in"), sem("lam_exp")
        sm_in, sm_exp = sem("sm_in"), sem("sm_exp")
        a_ready = sem("a_ready")
        mix_ready = sem("mix_ready")
        ln_ready = sem("ln_ready")
        xsm_in, xsm_exp, xp_ready = sem("xsm_in"), sem("xsm_exp"), sem("xp_ready")
        rt_in, rt_exp = sem("rt_in"), sem("rt_exp")
        route_ready = sem("route_ready")
        cnt_ready = sem("cnt_ready")
        tab_ready = sem("tab_ready")
        sel_ready = sem("sel_ready")
        gsel_ready = sem("gsel_ready")
        xg_done, xg_copied = sem("xg_done"), sem("xg_copied")
        xgT_done, xgT_ready = sem("xgT_done"), sem("xgT_ready")
        gu0_used = sem("gu0_used")
        gu_done, gu_copied = sem("gu_done"), sem("gu_copied")
        guT_done = sem("guT_done")
        gselT_done, gselT_ready = sem("gselT_done"), sem("gselT_ready")
        mg_ready, sig_ready, hT_ready = sem("mg_ready"), sem("sig_ready"), sem("hT_ready")
        d0_used = sem("d0_used")
        y_done, y_copied = sem("y_done"), sem("y_copied")
        scat_done, acc_done = sem("scat_done"), sem("acc_done")
        ln_applied = sem("ln_applied")
        fin_in, fin_out = sem("fin_in"), sem("fin_out")
        out_ready, out_stored = sem("out_ready"), sem("out_stored")

        def wait_emptied(eng, name):
            engine, count = emptied(name)
            eng.wait_ge(act_emptied if engine == "A" else dve_emptied, count)

        block = ctx.enter_context(nc.Block())

        @block.sync
        def _(sp):
            sp.dma_start(x3, d["x"][0].rearrange("(b p) n -> p b n", p=P)).then_inc(ld_x, 16)
            ba_dst = dnw_keep[:, 0:64].rearrange("p (k n) -> p k n", k=KC)
            sp.dma_start(ba_dst, d["w_in"][0, :, C_BA:C_BA + 8].rearrange("(k p) n -> p k n", p=P)).then_inc(ld_ba, 16)
            sp.dma_start(a_log, d["gdn_a_log"][0:1, :].partition_broadcast(P)).then_inc(ld_ba, 16)
            sp.dma_start(dt_b, d["gdn_dt_bias"][0:1, :].partition_broadcast(P)).then_inc(ld_ba, 16)
            for i, (name, col, cols, half) in enumerate(ATTENTION_LOADS):
                if i >= SLOTS:
                    sp.wait_ge(ring_used, i - SLOTS + 1)
                src = d[name][0, :, col:col + cols].rearrange("(k p) n -> p k n", p=P)
                if half is None:
                    dst = ring[:, (i % SLOTS) * 4096:(i % SLOTS + 1) * 4096].rearrange("p (k n) -> p k n", k=KC)
                else:
                    dst, src = slots[i % SLOTS], src[:, 4 * half:4 * half + 4, :]
                sp.dma_start(dst, src).then_inc(ring_full[i % SLOTS], 16)

            def load_role(role, e):
                w = d[ROLE_INPUT[role]][0].rearrange("e (k p) n -> e p k n", p=P)
                h = (0, 0, 1, 1, 0, 1)[role]
                src = w[bass.ds(e, 1), :, 4 * h:4 * h + 4, :].rearrange("e p k n -> p (e k) n")
                sp.dma_start(slots[ROLE_SLOT[role]], src).then_inc(ring_full[ROLE_SLOT[role]], 16)

            for role in range(SLOTS):
                sp.wait_ge(ring_used, N_ATT + role - SLOTS + 1)
                load_role(role, 0)
            sp.wait_ge(tab_ready, 1)
            with sp.Fori(1, N_EXPERTS) as e:
                done = sp.value_load(itab[0:1, bass.ds(e + (T_CUM - 1), 1)], min_val=1, max_val=MAX_BLOCKS)
                sp.wait_ge(gu0_used, done)
                load_role(G0, e)
                load_role(U0, e)
                sp.wait_ge(gu_done, done * 2)
                load_role(G1, e)
                load_role(U1, e)
                sp.wait_ge(d0_used, done)
                load_role(D0, e)
                sp.wait_ge(y_done, done)
                load_role(D1, e)

            sp.wait_ge(fin_out, 1)
            sp.dma_start(out[0, 0:P, :], x3[:, 0, :]).then_inc(out_stored, 16)
            sp.wait_ge(out_ready, 1)
            sp.dma_start(out[0, P:SEQ, :], x3[:, 1, :]).then_inc(out_stored, 16)
            sp.wait_ge(out_stored, 32)

        @block.gpsimd
        def _(pool):
            pool.memset(cin[:, :, 0:PAD], 0.0).then_inc(pad_zero, 1)
            pool.memset(eps_rms, RMS_EPS).then_inc(eps_set, 1)
            pool.memset(minus_half, -0.5)
            for j in range(4):
                pool.wait_ge(silu_ready, j + 1)
                pool.tensor_tensor(sq[:, 2 * j:2 * j + 2, :], cout[:, 2 * j:2 * j + 2, :], cout[:, 2 * j:2 * j + 2, :],
                                   ALU.mult).then_inc(sq_ready, 1)
            pool.wait_ge(dec_exp, 1)
            pool.affine_select(out=Dm, in_=Dm, pattern=[[0, PAIRS], [-1, P]], compare_op=ALU.is_gt, fill=0.0,
                               base=0, channel_multiplier=1).then_inc(dec_ready, 1)
            pool.wait_ge(dec_exp, 2)
            pool.affine_select(out=DT, in_=DT, pattern=[[0, PAIRS], [1, P]], compare_op=ALU.is_ge, fill=0.0,
                               base=0, channel_multiplier=-1).then_inc(dec_ready, 1)
            wait_emptied(pool, "LT1")
            wait_emptied(pool, "KQ1")
            pool.wait_ge(ld_lev, 16)
            pool.tensor_tensor(XT, LT, tile_b(levT[0], PAIRS, P), ALU.mult)
            pool.drain()
            pool.tensor_tensor(XT, tile_b(ident, PAIRS, P), XT, ALU.subtract).then_inc(xt_init, 1)
            for level in range(1, LEVELS):
                if level == 1:
                    wait_emptied(pool, "vtok1")
                else:
                    pool.wait_ge(unit_filled, UNIT_AT[f"M{level - 1}_1"] + 1)
                pool.tensor_tensor(BT, LT, tile_b(levT[level], PAIRS, P), ALU.mult).then_inc(bt_ready, 1)
            def root(i, v):
                pool.wait_ge(var_in, i + 1)
                pool.tensor_tensor(v, v, minus_half[:, 0:v.shape[1]], ALU.pow).then_inc(var_out, 1)

            for i in range(4):
                root(i, rs8[:, 0:4])
            for i, name in enumerate(("x1T3", "x2T3")):
                root(4 + 2 * i, rstd)
                root(5 + 2 * i, rstd)
                pool.wait_ge(unit_filled, UNIT_AT[name] + 1)
                pool.wait_ge(ld_ln, 32 * (i + 1))
                pool.tensor_tensor(x3[:, 1, :], x3[:, 1, :], ln_g, ALU.mult)
                pool.drain()
                pool.tensor_tensor(x3[:, 1, :], x3[:, 1, :], ln_b, ALU.add).then_inc(ln_ready, 1)
            pool.memset(y_sb, 0.0)
            pool.memset(gselT, 0.0)
            pool.drain()
            pool.sem_inc(y_copied, 1)
            pool.sem_inc(gselT_ready, 1)
            root(8, rstd)
            root(9, rstd)
            pool.wait_ge(fin_in, 1)
            pool.tensor_tensor(x3[:, 0, :], x3[:, 0, :], ln_b, ALU.add).then_inc(fin_out, 1)

        @block.scalar
        def _(act):
            act.dma_start(kst[:, :], d["consts"][:, 0:N_CONST]).then_inc(ld_const, 16)
            act.dma_start(columns_raw[0:48, :], d["gdn_conv_w"][0].rearrange("t o (c p) -> (t o c) p", p=P)).then_inc(ld_cols, 16)
            for i, name in enumerate(("ln1_g", "ln1_b", "ln2_g", "ln2_b")):
                act.dma_start(columns_raw[48 + 8 * i:56 + 8 * i, :], d[name][0].rearrange("(k p) -> k p", p=P)).then_inc(ld_cols, 16)
            for i, name in enumerate(["diff_lq1", "diff_lk1", "diff_lq2", "diff_lk2"]):
                act.dma_start(lam_raw[:, 64 * i:64 * i + 64], d[name][0:1, :].partition_broadcast(P)).then_inc(ld_vec, 16)
            for dst, name in ((gnw, "gdn_norm_w"), (dnw, "diff_norm_w")):
                act.dma_start(dst, d[name][0:1, :].partition_broadcast(P)).then_inc(ld_vec, 16)
            act.dma_start(mem3, d["mem"][0].rearrange("(b p) n -> p b n", p=P)).then_inc(ld_mem, 16)
            act.dma_start(ln_mem[:, 0:N_LEVEL_MASKS], d["consts"][:, K_LEV0:K_LEV0 + N_LEVEL_MASKS]).then_inc(ld_lev, 16)
            act.dma_start(rb, d["router_b"][0:1, :].partition_broadcast(P)).then_inc(ld_rt, 16)

            def load_gains(name):
                act.dma_start(ln_g, d[name + "_g"][0:1, :].partition_broadcast(P)).then_inc(ld_ln, 16)
                act.dma_start(ln_b, d[name + "_b"][0:1, :].partition_broadcast(P)).then_inc(ld_ln, 16)

            def filled(name):
                act.wait_ge(unit_filled, UNIT_AT[name] + 1)
                return bank(name)

            def empty(name, dst, src=None, func=ACT.Copy, **kw):
                ps = filled(name)
                act.activation(dst, ps[:, :] if src is None else src(ps), func, **kw).then_inc(act_emptied, 1)

            def as3(n):
                return lambda ps: ps[:, :].rearrange("p (g s) -> p g s", g=n)

            act.wait_ge(eps_set, 1)
            act.wait_ge(gate_step, 1)
            act.activation(sp_a, sp_a, ACT.Exp, scale=-1.0).then_inc(exp_ready, 1)
            act.activation(sp_b, sp_b, ACT.Exp, scale=-1.0).then_inc(exp_ready, 1)
            act.activation(a_log, a_log, ACT.Exp).then_inc(exp_ready, 1)
            act.wait_ge(exp_ready, 2)
            act.activation(sp_b, sp_b, ACT.Ln, bias=1.0).then_inc(exp_ready, 1)

            def silu(j):
                act.wait_ge(conv_ready, j + 1)
                act.activation(cout[:, 2 * j:2 * j + 2, :], cout[:, 2 * j:2 * j + 2, :], ACT.Silu).then_inc(silu_ready, 1)

            act.wait_ge(pad_zero, 1)
            empty("qk0", cin[:, 0:2, PAD:], as3(2))
            empty("qk1", cin[:, 2:4, PAD:], as3(2))
            silu(0)
            empty("qk2", cin[:, 4:6, PAD:], as3(2))
            silu(1)
            empty("qk3", cin[:, 6:8, PAD:], as3(2))
            silu(2)
            empty("v0", cin[:, 8:10, PAD:], as3(2))
            silu(3)
            empty("v1", cin[:, 10:12, PAD:], as3(2))
            silu(4)
            empty("z0", sz3[:, 0, :], func=ACT.Silu)
            silu(5)
            empty("z1", sz3[:, 1, :], func=ACT.Silu)
            for i in range(4):
                empty(f"ss{i}", sq_mem[:, 512 * i:512 * (i + 1)], func=ACT.Ln, bias=eps_rms)
            act.wait_ge(act_emptied, emptied("ss3")[1])
            for i in range(4):
                part = sq_mem[:, 512 * i:512 * (i + 1)]
                act.activation(part, part, ACT.Exp, scale=-0.5).then_inc(l2_exp, 1)
            act.wait_ge(lam_in, 1)
            act.activation(lamv[:, 0:2], lamv[:, 0:2], ACT.Exp).then_inc(lam_exp, 1)
            act.wait_ge(gate_step, 3)
            act.activation(eg, gcum, ACT.Exp).then_inc(exp_ready, 1)
            act.wait_ge(dec_in, 1)
            act.activation(tails[:, 0:4], tails[:, 0:4], ACT.Exp).then_inc(exp_ready, 1)
            act.wait_ge(qd_in, 1)
            act.activation(qd, qd, ACT.Exp).then_inc(qd_exp, 1)
            act.wait_ge(dec_in, 2)
            act.activation(Dm, Dm, ACT.Exp, scale=-1.0).then_inc(dec_exp, 1)
            act.wait_ge(dec_in, 3)
            act.activation(DT, DT, ACT.Exp).then_inc(dec_exp, 1)

            empty("dqk0", dqk3[:, 0:2, :], as3(2))
            empty("dqk1", dqk3[:, 2:4, :], as3(2))
            for g in range(TB):
                empty(f"LT{g}", LT[:, 4 * g:4 * g + 4, :], as3(4))
            empty("dqk2", dqk3[:, 4:6, :], as3(2))

            def empty_km(i):
                empty(f"km{i}", km3[:, 2 * i:2 * i + 2, :], as3(2))

            def empty_vm(i):
                empty(f"vm{i}", vm3[:, i // 2, (i % 2) * HALF:(i % 2 + 1) * HALF])

            def empty_T(name, i, dst, gains=None):
                ps = filled(f"{name}{i}")
                tok = slice((i // 2) * P, (i // 2 + 1) * P)
                if gains is None:
                    act.activation(dst[:, 4 * (i % 2):4 * (i % 2) + 4, tok], as3(4)(ps), ACT.Copy).then_inc(act_emptied, 1)
                    return
                for j in range(4):
                    k = 4 * (i % 2) + j
                    last = act.activation(dst[:, k, tok], ps[:, j * P:(j + 1) * P], ACT.Identity,
                                          scale=gains[0][:, k:k + 1], bias=gains[1][:, k:k + 1])
                last.then_inc(act_emptied, 1)

            def diff_exp(h, c):
                i = 2 * h + c
                act.wait_ge(sm_in, i + 1)
                for q, (a, b) in enumerate(((0, P), (P, 3 * P))):
                    act.activation(dp[h % 2][:, c, a:b], dp[h % 2][:, c, a:b], ACT.Exp, scale=DIFF_SCALE,
                                   bias=stat_nb[:, 4 * (h % 2) + 2 * c + q:4 * (h % 2) + 2 * c + q + 1],
                                   accum_out=stat_l[:, 4 * (h % 2) + 2 * c + q:4 * (h % 2) + 2 * c + q + 1]).then_inc(sm_exp, 1)

            def empty_aT(h):
                empty(f"aT{h}", aT[:, h, :], lambda ps: ps[:, 0:384])

            for level in range(1, LEVELS):
                for g in range(TB):
                    empty(f"M{level}_{g}", M1[:, 4 * g:4 * g + 4, :], as3(4))
                if level == 1:
                    empty("dqk3", dqk3[:, 6:8, :], as3(2))
                elif level <= 3:
                    empty(f"dv{level - 2}", dv3[:, level - 2, :])
                if level == 3:
                    for i in range(4):
                        empty_T("memT", i, memT)
                if level >= 4:
                    if level > 4:
                        empty_aT(level - 5)
                    diff_exp(level - 4, 0)
                    diff_exp(level - 4, 1)
                    empty_km(level - 4)
            for g in range(TB):
                empty(f"U{g}", u_sb[:, 4 * g:4 * g + 4, :], as3(4))
            empty("WT", wT, as3(4))
            empty("S", S_sb, as3(4))
            empty("O0", o_sb[:, 0:4, :], as3(4))
            empty_aT(2)
            diff_exp(3, 0)
            diff_exp(3, 1)
            empty_km(3)
            empty("O1", o_sb[:, 4:8, :], as3(4))
            empty_aT(3)
            load_gains("ln1")
            empty("OD0", od_sb[:, 0:512])
            empty("OD1", od_sb[:, 512:1024])
            empty_vm(0)

            act.wait_ge(mix_ready, 2)
            for w, n in enumerate(["exp_b_gate", "exp_b_up"]):
                act.dma_start(bias_raw[:, w, :, :], d[n][0].rearrange("(b e) (c f) -> (e c) b f", b=2, f=P)).then_inc(ld_bias, 16)
            act.dma_start(gdn_mem[:, 2432:2432 + P + 64], d["consts"][:, K_IOTA:K_END]).then_inc(ld_iota, 16)
            empty_T("mixT", 0, xT)
            empty_T("mixT", 1, xT)
            empty_vm(1)
            empty_T("mixT", 2, xT)
            empty_T("mixT", 3, xT)
            empty_T("x1T", 0, xT, (gcol1, bcol1))
            empty_T("x1T", 1, xT, (gcol1, bcol1))
            empty_vm(2)
            empty_T("x1T", 2, xT, (gcol1, bcol1))
            empty_T("x1T", 3, xT, (gcol1, bcol1))
            for i in range(4):
                empty(f"xq{i}", dqk3[:, 2 * i:2 * i + 2, :], as3(2))

            def cross_exp(h):
                act.wait_ge(xsm_in, h + 1)
                for b in range(TB):
                    act.activation(xp[:, h, b, :], bank(f"xs{h}")[:, b * 256:(b + 1) * 256], ACT.Exp, scale=XA_SCALE,
                                   bias=stat_nb[:, 2 * h + b:2 * h + b + 1],
                                   accum_out=stat_l[:, 2 * h + b:2 * h + b + 1]).then_inc(xsm_exp, 1)

            def empty_pT(h):
                empty(f"pT{h}", pT[:, h, :, :], as3(2))

            def empty_oT(h):
                empty(f"oT{h}", oT[:, 2 * h:2 * h + 2, :], as3(2))

            act.wait_ge(ln_ready, 2)
            load_gains("ln2")
            for h in range(4):
                cross_exp(h)
            act.dma_start(bdown, d["exp_b_down"][0]).then_inc(ld_bdown, 16)
            act.dma_start(dv[:, 0:KC * N_EXPERTS].rearrange("p (k e) -> p k e", k=KC),
                          d["router_w"][0].rearrange("(k p) e -> p k e", p=P)).then_inc(ld_rt, 16)
            empty_vm(3)
            empty_pT(0)
            empty_pT(1)
            empty_oT(0)
            empty_pT(2)
            empty_oT(1)
            empty_pT(3)
            empty_oT(2)
            empty_oT(3)
            for i in range(4):
                if i == 2:
                    empty("bT", ebias, as3(2))
                empty_T("x2T", i, xT, (gcol2, bcol2))
            act.wait_ge(rt_in, 1)
            act.activation(expl, expl, ACT.Exp).then_inc(rt_exp, 1)
            act.wait_ge(ln_ready, 4)
            load_gains("ln3")
            empty("xg0", xg_sb)
            empty("GT", GT, lambda ps: ps[0:N_EXPERTS, 0:256])

            act.wait_ge(tab_ready, 1)
            blocks = act.value_load(itab[0:1, T_CUM + N_EXPERTS - 1:T_CUM + N_EXPERTS], min_val=N_EXPERTS, max_val=MAX_BLOCKS)
            with act.Fori(0, blocks) as n:
                for f in range(2):
                    act.wait_ge(gu_done, n * 2 + (f + 1))
                    act.activation(gu[:, f, :], banks[f][:, :], ACT.Copy).then_inc(gu_copied, 1)
                act.wait_ge(xg_done, n + 1)
                act.activation(xg_sb, banks[5][:, :], ACT.Copy).then_inc(xg_copied, 1)
                for f in range(2):
                    act.wait_ge(mg_ready, n * 2 + (f + 1))
                    act.activation(sig[:, f, :, :], mg[:, f, :, :], ACT.Sigmoid, scale=SWIGLU_ALPHA).then_inc(sig_ready, 1)
                act.wait_ge(y_done, n + 1)
                act.activation(y_sb, banks[4][:, :], ACT.Copy).then_inc(y_copied, 1)
                act.wait_ge(gselT_done, n + 2)
                act.activation(gselT, banks[7][:, 0:256], ACT.Copy).then_inc(gselT_ready, 1)

        @block.tensor
        def _(pe):
            def begin(name):
                u = UNIT_AT[name]
                if u >= 8:
                    wait_emptied(pe, UNITS[u - 8][0])
                return bank(name)

            def need(*names):
                for name in names:
                    wait_emptied(pe, name)

            def arrived(i):
                pe.wait_ge(ring_full[i % SLOTS], 16 * (i // SLOTS + 1))

            dv_w = ring[:, 0:4096].rearrange("p (k n) -> p k n", k=KC)

            def transpose_block(name, src, chunks):
                ps = begin(name)
                for j, c in enumerate(chunks):
                    last = pe.transpose(ps[:, j * P:(j + 1) * P], src[:, c * P:(c + 1) * P], ident)
                last.then_inc(unit_filled, 1)

            def channel_major(name, w, chunks, src):
                ps = begin(name)
                for j, c in enumerate(chunks):
                    for k in range(KC):
                        last = pe.matmul(ps[:, j * SEQ:(j + 1) * SEQ], w(k)[:, c * P:(c + 1) * P], src[:, k, :],
                                         start=(k == 0), stop=(k == KC - 1))
                last.then_inc(unit_filled, 1)

            def token_major(name, srcT, b, w, col):
                ps = begin(name)
                for k in range(KC):
                    last = pe.matmul(ps[:, :], srcT[:, k, b * P:(b + 1) * P], w(k)[:, col:col + 512],
                                     start=(k == 0), stop=(k == KC - 1))
                last.then_inc(unit_filled, 1)

            def through(*loads):
                return lambda k: slots[loads[k // 4] % SLOTS][:, k % 4, :]

            def used_up(n, after):
                pe.wait_ge(unit_filled, UNIT_AT[after] + 1)
                pe.sem_inc(ring_used, n)

            pe.wait_ge(ld_const, 16)
            pe.wait_ge(ld_x, 16)
            for i in range(4):
                transpose_block(f"xT{i}", x3[:, i // 2, :], range(4 * (i % 2), 4 * (i % 2) + 4))
            need("xT2", "xT3")
            pe.wait_ge(ld_ba, 48)
            ps = begin("ba")
            for b in range(TB):
                for k in range(KC):
                    last = pe.matmul(ps[:, 8 * b:8 * b + 8], xT[:, k, b * P:(b + 1) * P], dnw_keep[:, 8 * k:8 * k + 8],
                                     start=(k == 0), stop=(k == KC - 1))
            last.then_inc(unit_filled, 1)
            w = through(0, 1)
            arrived(0)
            for i in range(4):
                ps = begin(f"qk{i}")
                for k in range(KC // 2):
                    pe.matmul(ps[:, 0:SEQ], w(k)[:, 2 * i * P:(2 * i + 1) * P], xT[:, k, :], start=(k == 0), stop=False)
            pe.wait_ge(ld_cols, 80)
            ps = begin("columns")
            pe.transpose(ps[:, 0:80], columns_raw, ident[0:80, 0:80]).then_inc(unit_filled, 1)
            arrived(1)
            for i in range(4):
                ps = bank(f"qk{i}")
                for k in range(KC // 2, KC):
                    pe.matmul(ps[:, 0:SEQ], w(k)[:, 2 * i * P:(2 * i + 1) * P], xT[:, k, :], start=False, stop=(k == KC - 1))
                for k in range(KC):
                    last = pe.matmul(ps[:, SEQ:2 * SEQ], w(k)[:, (2 * i + 1) * P:(2 * i + 2) * P], xT[:, k, :],
                                     start=(k == 0), stop=(k == KC - 1))
                last.then_inc(unit_filled, 1)
            arrived(2)
            arrived(3)
            for i in range(2):
                channel_major(f"v{i}", through(2, 3), (2 * i, 2 * i + 1), xT)
            used_up(2, "qk3")
            token_major("z0", xT, 0, through(2, 3), 512)
            pe.wait_ge(gate_step, 2)
            ps = begin("gcum")
            pe.matmul(ps[:, 0:PAIRS], upper, g_log, start=True, stop=True).then_inc(unit_filled, 1)
            for g in range(TB):
                ps = begin(f"R{g}")
                for h in range(HEADS):
                    last = pe.matmul(ps[:, h * P:(h + 1) * P], gB[:, 4 * g + h, :], upper, start=True, stop=True)
                last.then_inc(unit_filled, 1)
            token_major("z1", xT, 1, through(2, 3), 512)
            for i in range(4):
                pe.wait_ge(sq_ready, i + 1)
                ps = begin(f"ss{i}")
                pe.matmul(ps[:, :], ones, sq_mem[:, 512 * i:512 * (i + 1)], start=True, stop=True).then_inc(unit_filled, 1)
            arrived(4)
            arrived(5)

            def dqk_unit(i):
                channel_major(f"dqk{i}", through(4, 5), (2 * i, 2 * i + 1), xT)

            def dv_unit(b):
                token_major(f"dv{b}", xT, b, lambda k: dv_w[:, k, :], 0)

            def km_unit(i):
                channel_major(f"km{i}", through(7, 8), (2 * i, 2 * i + 1), memT)

            def vm_unit(i):
                token_major(f"vm{i}", memT, i // 2, through(11, 12), (i % 2) * HALF)

            def per_head(name, product):
                ps = begin(name)
                for h in range(HEADS):
                    last = product(ps[:, h * P:(h + 1) * P], h)
                last.then_inc(unit_filled, 1)

            dqk_unit(0)
            used_up(2, "z1")
            pe.wait_ge(silu_ready, 6)
            for b in range(TB):
                per_head(f"vtok{b}", lambda o, h: pe.transpose(o, vT[:, h, b * P:(b + 1) * P], ident))
            pe.wait_ge(qk_normed, 4)
            for name, other in (("KK", kn), ("KQ", qn)):
                for b in range(TB):
                    tok = slice(b * P, (b + 1) * P)
                    per_head(f"{name}{b}", lambda o, h: pe.matmul(o, kn[:, h, tok], other[:, h, tok], start=True, stop=True))
            for b in range(TB):
                per_head(f"ktok{b}", lambda o, h: pe.transpose(o, kn[:, h, b * P:(b + 1) * P], ident))
            dqk_unit(1)
            for g in range(TB):
                pe.wait_ge(lmat_ready, g + 1)
                per_head(f"LT{g}", lambda o, h: pe.transpose(o, L[:, 4 * g + h, :], ident))
            dqk_unit(2)

            def scores(h):
                ps2 = [begin(f"sc{h}_0"), begin(f"sc{h}_1")]
                for q, (a, b) in enumerate(((0, P), (P, 3 * P))):
                    for c in range(2):
                        rows = slice(DIFF_D * c, DIFF_D * (c + 1))
                        last = pe.matmul(ps2[c][:, a:b], dqk3[rows, h, q * P:(q + 1) * P], dqk3[rows, 4 + h, 0:b - a],
                                         start=True, stop=True)
                        if q == 1:
                            last.then_inc(unit_filled, 1)

            def attention_T(h):
                pe.wait_ge(a_ready, h + 1)
                ps = begin(f"aT{h}")
                for j in range(3):
                    last = pe.transpose(ps[:, j * P:(j + 1) * P], dp[h % 2][:, 0, j * P:(j + 1) * P], ident)
                last.then_inc(unit_filled, 1)

            pe.wait_ge(x_init, 1)
            pe.wait_ge(xt_init, 1)
            for level in range(1, LEVELS):
                pe.wait_ge(bt_ready, level)
                for g in range(TB):
                    if level > 1:
                        need(f"X{level - 1}_{g}", f"XT{level - 1}_{g}")
                    per_head(f"M{level}_{g}", lambda o, h: pe.matmul(o, BT[:, 4 * g + h, :], X[:, 4 * g + h, :],
                                                                   start=True, stop=True))
                for g in range(TB):
                    need(f"M{level}_{g}")
                    if level < LEVELS - 1:
                        per_head(f"X{level}_{g}", lambda o, h: pe.matmul(o, XT[:, 4 * g + h, :], M1[:, 4 * g + h, :],
                                                                       start=True, stop=True))
                    per_head(f"XT{level}_{g}", lambda o, h: pe.matmul(o, M1[:, 4 * g + h, :], XT[:, 4 * g + h, :],
                                                                    start=True, stop=True))
                if level == 1:
                    dqk_unit(3)
                elif level == 2:
                    arrived(6)
                    dv_unit(0)
                    used_up(2, "dqk3")
                elif level == 3:
                    dv_unit(1)
                    pe.wait_ge(ld_mem, 16)
                    for i in range(4):
                        transpose_block(f"memT{i}", mem3[:, i // 2, :], range(4 * (i % 2), 4 * (i % 2) + 4))
                else:
                    if level == 4:
                        need("memT3", "dqk3")
                        used_up(1, "dv1")
                        arrived(7)
                        arrived(8)
                    scores(level - 4)
                    if level > 4:
                        attention_T(level - 5)
                    km_unit(level - 4)

            for g in range(TB):
                need(f"XT{LEVELS - 1}_{g}")
                per_head(f"U{g}", lambda o, h: pe.matmul(o, XT[:, 4 * g + h, :], vbeta[:, 4 * g + h, :], start=True, stop=True))
            per_head("WT", lambda o, h: pe.matmul(o, kbg[:, 4 + h, :], XT[:, 4 + h, :], start=True, stop=True))
            scores(3)
            need("U0")
            per_head("S", lambda o, h: pe.matmul(o, ktail[:, h, :], u_sb[:, h, :], start=True, stop=True))
            per_head("O0", lambda o, h: pe.matmul(o, AT[:, h, :], u_sb[:, h, :], start=True, stop=True))
            attention_T(2)
            need("WT", "S")
            per_head("WS", lambda o, h: pe.matmul(o, wT[:, h, :], S_sb[:, h, :], start=True, stop=True))
            km_unit(3)
            pe.wait_ge(vnew_ready, 1)
            ps = begin("O1")
            for h in range(HEADS):
                pe.matmul(ps[:, h * P:(h + 1) * P], qd[:, h, :], S_sb[:, h, :], start=True, stop=False)
                last = pe.matmul(ps[:, h * P:(h + 1) * P], AT[:, 4 + h, :], vnew[:, h, :], start=False, stop=True)
            last.then_inc(unit_filled, 1)
            attention_T(3)
            used_up(2, "km3")
            need("aT3", "dv1")
            per_head("OD0", lambda o, h: pe.matmul(o, aT[:, h, 0:P], dv3[:, 0, h * P:(h + 1) * P], start=True, stop=True))
            ps = begin("OD1")
            for h in range(HEADS):
                for j in range(2):
                    last = pe.matmul(ps[:, h * P:(h + 1) * P], aT[:, h, (1 + j) * P:(2 + j) * P], dv3[:, j, h * P:(h + 1) * P],
                                     start=(j == 0), stop=(j == 1))
            last.then_inc(unit_filled, 1)
            arrived(11)
            arrived(12)
            vm_unit(0)

            def tokens_T(name, i, src):
                transpose_block(f"{name}{i}", src[:, i // 2, :], range(4 * (i % 2), 4 * (i % 2) + 4))

            pe.wait_ge(mix_ready, 3)
            tokens_T("mixT", 0, mem3)
            tokens_T("mixT", 1, mem3)
            vm_unit(1)
            pe.wait_ge(mix_ready, 4)
            tokens_T("mixT", 2, mem3)
            tokens_T("mixT", 3, mem3)
            arrived(9)
            arrived(10)
            for i in range(4):
                if i == 3:
                    pe.wait_ge(ln_applied, 1)
                    tokens_T("x1T", 0, x3)
                    tokens_T("x1T", 1, x3)
                need(f"mixT{2 * (i // 2) + 1}")
                token_major(f"h{i}", xT, i // 2, through(9, 10), (i % 2) * HALF)
            vm_unit(2)
            used_up(2, "h3")
            pe.wait_ge(ln_applied, 2)
            tokens_T("x1T", 2, x3)
            tokens_T("x1T", 3, x3)
            need("x1T3")
            arrived(13)
            arrived(14)
            for i in range(4):
                channel_major(f"xq{i}", through(13, 14), (2 * i, 2 * i + 1), xT)
            for h in range(HEADS):
                need(f"xq{h}")
                if h == 0:
                    need("km3")
                ps = begin(f"xs{h}")
                for b in range(TB):
                    for j in range(2):
                        last = pe.matmul(ps[:, b * 256:(b + 1) * 256], dqk3[:, 2 * h + j, b * P:(b + 1) * P], km3[:, 2 * h + j, :],
                                         start=(j == 0), stop=(j == 1))
                last.then_inc(unit_filled, 1)
            vm_unit(3)

            def probs_T(h):
                pe.wait_ge(xp_ready, h + 1)
                ps = begin(f"pT{h}")
                for m in range(2):
                    for b in range(TB):
                        last = pe.transpose(ps[:, (2 * m + b) * P:(2 * m + b + 1) * P], xp[:, h, b, m * P:(m + 1) * P], ident)
                last.then_inc(unit_filled, 1)

            def cross_out(h):
                need(f"pT{h}")
                if h == 0:
                    need("vm3")
                ps = begin(f"oT{h}")
                for j in range(2):
                    for m in range(2):
                        c = 2 * h + j
                        last = pe.matmul(ps[:, j * SEQ:(j + 1) * SEQ], vm3[:, m, c * P:(c + 1) * P], pT[:, h, m, :],
                                         start=(m == 0), stop=(m == 1))
                last.then_inc(unit_filled, 1)

            probs_T(0)
            used_up(4, "vm3")
            probs_T(1)
            cross_out(0)
            probs_T(2)
            cross_out(1)
            probs_T(3)
            cross_out(2)
            cross_out(3)
            need("oT3")
            arrived(15)
            arrived(16)
            for i in range(4):
                if i == 3:
                    pe.wait_ge(ln_applied, 3)
                    tokens_T("x2T", 0, x3)
                    tokens_T("x2T", 1, x3)
                token_major(f"wo{i}", oT, i // 2, through(15, 16), (i % 2) * HALF)
            pe.wait_ge(ld_bias, 32)
            ps = begin("bT")
            for w in range(2):
                for b in range(2):
                    last = pe.transpose(ps[:, (2 * w + b) * P:(2 * w + b + 1) * P], bias_raw[:, w, b, :], ident)
            last.then_inc(unit_filled, 1)
            pe.wait_ge(ld_rt, 32)
            router_ps = begin("router")

            def route_block(b):
                for k in range(KC):
                    last = pe.matmul(router_ps[:, 32 * b:32 * b + 32], xT[:, k, b * P:(b + 1) * P], dv[:, 32 * k:32 * k + 32],
                                     start=(k == 0), stop=(k == KC - 1))
                return last

            need("x2T1")
            route_block(0)
            used_up(2, "wo3")
            pe.wait_ge(ln_applied, 4)
            tokens_T("x2T", 2, x3)
            tokens_T("x2T", 3, x3)
            need("x2T3")
            route_block(1).then_inc(unit_filled, 1)
            pe.wait_ge(route_ready, 1)
            ps = begin("pos")
            pe.matmul(ps[:, 0:32], strict, M[:, 0:32], start=True, stop=True)
            pe.matmul(ps[:, 32:64], strict, M[:, 32:64], start=True, stop=False)
            pe.matmul(ps[:, 32:64], ones, M[:, 0:32], start=False, stop=True)
            pe.matmul(ps[0:32, 64:65], M[:, 0:32], ones[:, 0:1], start=True, stop=False)
            pe.matmul(ps[0:32, 64:65], M[:, 32:64], ones[:, 0:1], start=False, stop=True).then_inc(unit_filled, 1)

            def gather(ps):
                for b in range(TB):
                    for h in range(2):
                        last = pe.matmul(ps[64 * h:64 * h + 64, :], selw[:, b, 0:CAP], x3[:, b, h * HALF:(h + 1) * HALF],
                                         start=(b == 0), stop=(b == 1))
                return last

            def gathered_T(ps):
                for j in range(4):
                    last = pe.transpose(ps[:, j * P:(j + 1) * P], xg_sb[:, j * P:(j + 1) * P], ident)
                return last

            pe.wait_ge(ln_ready, 4)
            pe.wait_ge(sel_ready, 1)
            gather(begin("xg0")).then_inc(unit_filled, 1)
            pe.wait_ge(cnt_ready, 1)
            ps = begin("cum")
            pe.matmul(ps[0:32, 0:1], upper[0:32, 0:32], nblk[0:32, 0:1], start=True, stop=True)
            pe.matmul(ps[0:1, 32:64], nblk[0:32, 0:1], upper[0:32, 0:32], start=True, stop=True).then_inc(unit_filled, 1)
            need("xg0")
            gathered_T(begin("xgT0")).then_inc(unit_filled, 1)
            pe.wait_ge(cnt_ready, 2)
            ps = begin("etab")
            pe.matmul(ps[0:1, 0:64], ones[0:32, 0:1], emask, start=True, stop=True).then_inc(unit_filled, 1)
            ps = begin("GT")
            for b in range(TB):
                last = pe.transpose(ps[0:32, b * P:(b + 1) * P], G[:, 32 * b:32 * b + 32], ident)
            last.then_inc(unit_filled, 1)
            need("GT")
            pe.wait_ge(ld_bdown, 16)
            for i in range(4):
                ps = begin(f"eb{i}")
                pe.matmul(ps[:, :], GT[:, (i // 2) * P:(i // 2 + 1) * P], bdown[:, (i % 2) * HALF:(i % 2 + 1) * HALF],
                          start=True, stop=True).then_inc(unit_filled, 1)

            def xg_chunk(k):
                return xgT[:, k % 4, 64 * (k // 4):64 * (k // 4) + 64]

            def scatter():
                for b, targets in enumerate(((7, 5), (0, 1))):
                    for h in range(2):
                        last = pe.matmul(banks[targets[h]][:, :], gselT[64 * h:64 * h + 64, b * P:(b + 1) * P],
                                         y_sb[64 * h:64 * h + 64, :], start=True, stop=True)
                    last.then_inc(scat_done, 1)

            wait_emptied(pe, "eb3")
            pe.sem_inc(gselT_done, 1)
            pe.wait_ge(tab_ready, 1)
            blocks = pe.value_load(itab[0:1, T_CUM + N_EXPERTS - 1:T_CUM + N_EXPERTS], min_val=N_EXPERTS, max_val=MAX_BLOCKS)
            with pe.Fori(0, blocks) as n:
                e16 = pe.value_load(itab[0:1, bass.ds(n + T_E16, 1)], min_val=0, max_val=16 * (N_EXPERTS - 1))

                def weights(role):
                    pe.wait_ge(ring_full[ROLE_SLOT[role]], e16 + 16 * (ROLE_EARLIER[role] + 1))

                def gate_up(f, k):
                    for side, role in ((0, (G0, G1)[k // 4]), (1, (U0, U1)[k // 4])):
                        last = pe.matmul(banks[f][64 * side:64 * side + 64, :], xg_chunk(k),
                                         slots[ROLE_SLOT[role]][:, k % 4, f * HALF:(f + 1) * HALF],
                                         start=(k == 0), stop=(k == KC - 1))
                    return last

                pe.wait_ge(xgT_ready, n + 1)
                weights(G0)
                weights(U0)
                for k in range(4):
                    for f in range(2):
                        last = gate_up(f, k)
                last.then_inc(gu0_used, 1)
                weights(G1)
                weights(U1)
                for f in range(2):
                    for k in range(4, KC):
                        last = gate_up(f, k)
                    last.then_inc(gu_done, 1)
                pe.wait_ge(sel_ready, n + 2)
                gather(banks[5]).then_inc(xg_done, 1)
                for f in range(2):
                    pe.wait_ge(gu_copied, n * 2 + (f + 1))
                    for j in range(4):
                        last = pe.transpose(banks[2 + f][:, j * P:(j + 1) * P], gu[:, f, j * P:(j + 1) * P], ident)
                    last.then_inc(guT_done, 1)
                pe.wait_ge(xg_copied, n + 1)
                gathered_T(banks[6]).then_inc(xgT_done, 1)
                pe.wait_ge(y_copied, n + 1)
                pe.wait_ge(gselT_ready, n + 1)
                scatter()
                for f in range(2):
                    weights((D0, D1)[f])
                    pe.wait_ge(hT_ready, n * 2 + (f + 1))
                    for k in range(4 * f, 4 * f + 4):
                        for h in range(2):
                            last = pe.matmul(banks[4][64 * h:64 * h + 64, :], hT[:, k, :],
                                             slots[ROLE_SLOT[(D0, D1)[f]]][:, k % 4, h * HALF:(h + 1) * HALF],
                                             start=(k == 0), stop=(k == KC - 1))
                    last.then_inc((d0_used, y_done)[f], 1)
                pe.wait_ge(acc_done, n + 2)
                pe.wait_ge(gsel_ready, n + 1)
                for b in range(TB):
                    last = pe.transpose(banks[7][:, b * P:(b + 1) * P], gsel[:, b, :], ident)
                last.then_inc(gselT_done, 1)
            pe.wait_ge(y_copied, blocks + 1)
            pe.wait_ge(gselT_ready, blocks + 1)
            scatter()

        @block.vector
        def _(dve):
            tt, ts, stt = dve.tensor_tensor, dve.tensor_scalar, dve.scalar_tensor_tensor

            def filled(name):
                dve.wait_ge(unit_filled, UNIT_AT[name] + 1)
                return bank(name)

            def as3(ps, n):
                return ps[:, :].rearrange("p (g s) -> p g s", g=n)

            for i in range(4):
                dve.tensor_copy(xT[:, 4 * (i % 2):4 * (i % 2) + 4, (i // 2) * P:(i // 2 + 1) * P], as3(filled(f"xT{i}"), 4)).then_inc(dve_emptied, 1)
            ps = filled("ba")
            dve.tensor_copy(ba, ps[:, 0:16]).then_inc(dve_emptied, 1)
            dve.tensor_copy(columns, filled("columns")[:, 0:80]).then_inc(dve_emptied, 1)
            dve.drain()
            ba3 = ba.rearrange("p (b n) -> p b n", b=2)
            dt3 = dt_b.unsqueeze(1).broadcast_to([P, 2, 4])
            s3 = [v.rearrange("p (b n) -> p b n", b=2) for v in (sp_a, sp_b, sp_c)]
            dve.tensor_copy(s3[0], ba3[:, :, 0:4])
            tt(s3[2], ba3[:, :, 4:8], dt3, ALU.add)
            dve.drain()
            stt(sp_b, sp_c, -1.0, sp_c, ALU.mult, ALU.max).then_inc(gate_step, 1)
            ts(sp_c, sp_c, 0.0, None, ALU.max)
            dve.drain()
            dve.wait_ge(exp_ready, 4)
            ts(beta, sp_a, 1.0, None, ALU.add)
            tt(sp_c, sp_c, sp_b, ALU.add)
            dve.drain()
            dve.reciprocal(beta, beta)
            tt(s3[2], s3[2], a_log.unsqueeze(1).broadcast_to([P, 2, 4]), ALU.mult)
            dve.drain()
            ts(g_log, sp_c, -1.0, None, ALU.mult)
            dve.drain()
            dve.tensor_copy(gB, row_b(g_log, PAIRS, P))
            dve.drain()
            dve.sem_inc(gate_step, 1)

            names = {0: "qk0", 1: "qk1", 2: "qk2", 3: "qk3", 4: "v0", 5: "v1"}
            dve.wait_ge(pad_zero, 1)
            for j in range(6):
                wait_emptied(dve, names[j])
                for tap in range(GDN_TAPS):
                    for c in (2 * j, 2 * j + 1):
                        w = convw[:, 12 * tap + c:12 * tap + c + 1]
                        if tap == 0:
                            last = ts(cout[:, c, :], cin[:, c, 0:SEQ], w, None, ALU.mult)
                        else:
                            last = stt(cout[:, c, :], cin[:, c, tap:tap + SEQ], w, cout[:, c, :], ALU.mult, ALU.add)
                    if tap < GDN_TAPS - 1:
                        dve.drain()
                last.then_inc(conv_ready, 1)

            dve.wait_ge(ld_vec, 16 * 6)
            for i in range(2):
                tt(lam_raw[:, 128 * i:128 * i + 64], lam_raw[:, 128 * i:128 * i + 64], lam_raw[:, 128 * i + 64:128 * i + 128], ALU.mult)
            dve.drain()
            for i in range(2):
                dve.reduce_sum(lamv[:, i:i + 1], lam_raw[:, 128 * i:128 * i + 64], AX_X)
            dve.drain()
            dve.sem_inc(lam_in, 1)
            ts(dnw_keep[:, :], dnw, 1.0 - LAMBDA_INIT, None, ALU.mult)

            dve.tensor_copy(gcum, filled("gcum")[:, 0:PAIRS]).then_inc(dve_emptied, 1)
            dve.drain()
            dve.sem_inc(gate_step, 1)
            for g in range(TB):
                ps = as3(filled(f"R{g}"), 4)
                if g == 0:
                    tt(tails[:, 0:4], ps[:, :, P - 1:P].rearrange("p g s -> p (g s)"), gcum[:, 0:4], ALU.subtract)
                else:
                    dve.tensor_copy(qd, ps).then_inc(qd_in, 1)
                tt(diff[:, 4 * g:4 * g + 4, :], ps, row_b(gcum[:, 4 * g:4 * g + 4], 4, P), ALU.subtract).then_inc(dve_emptied, 1)
            dve.drain()
            dve.sem_inc(dec_in, 1)
            ts(Dm, diff, 0.0, None, ALU.max).then_inc(dec_in, 1)
            ts(DT, diff, 0.0, None, ALU.min).then_inc(dec_in, 1)
            wait_emptied(dve, "z1")
            tt(sz[:, :].rearrange("p (g s) -> p g s", g=PAIRS), sz[:, :].rearrange("p (g s) -> p g s", g=PAIRS),
               tile_b(gnw, PAIRS, P), ALU.mult)
            for i in range(4):
                dve.wait_ge(l2_exp, i + 1)
                part = conv_out[:, 512 * i:512 * (i + 1)]
                stt(part, part, GDN_DK ** -0.5 if i < 2 else 1.0, sq_mem[:, 512 * i:512 * (i + 1)],
                    ALU.mult, ALU.mult).then_inc(qk_normed, 1)
            dve.wait_ge(qd_exp, 1)
            dve.drain()
            tt(qd, qd, qn[:, :, P:SEQ], ALU.mult)
            dve.wait_ge(exp_ready, 6)
            tt(begs, beta, eg, ALU.mult)
            for g in range(TB):
                tt(vbeta[:, 4 * g:4 * g + 4, :], as3(filled(f"vtok{g}"), 4), row_b(beta[:, 4 * g:4 * g + 4], 4, P),
                   ALU.mult).then_inc(dve_emptied, 1)
            dve.wait_ge(dec_ready, 1)
            for g in range(TB):
                ps = as3(filled(f"KK{g}"), 4)
                for h in range(HEADS):
                    i = 4 * g + h
                    last = stt(L[:, i, :], ps[:, h, :], beta[:, i:i + 1], Dm[:, i, :], ALU.mult, ALU.mult)
                dve.drain()
                dve.sem_inc(dve_emptied, 1)
                dve.sem_inc(lmat_ready, 1)
            dve.wait_ge(dec_ready, 2)
            for g in range(TB):
                tt(AT[:, 4 * g:4 * g + 4, :], as3(filled(f"KQ{g}"), 4), DT[:, 4 * g:4 * g + 4, :], ALU.mult).then_inc(dve_emptied, 1)
            ps = as3(filled("ktok0"), 4)
            tt(ktail, ps, row_b(tails[:, 0:4], 4, P), ALU.mult)
            tt(kbg[:, 0:4, :], ps, row_b(begs[:, 0:4], 4, P), ALU.mult).then_inc(dve_emptied, 1)
            tt(kbg[:, 4:8, :], as3(filled("ktok1"), 4), row_b(begs[:, 4:8], 4, P), ALU.mult).then_inc(dve_emptied, 1)
            dve.wait_ge(ld_lev, 16)
            tt(X, L, tile_b(lev0, PAIRS, P), ALU.mult)
            dve.drain()
            tt(X, tile_b(ident, PAIRS, P), X, ALU.subtract).then_inc(x_init, 1)
            dve.wait_ge(xt_init, 1)
            dve.drain()
            dve.wait_ge(lam_exp, 1)
            tt(neglam, lamv[:, 1:2], lamv[:, 0:1], ALU.subtract)
            dve.drain()
            ts(neglam, neglam, LAMBDA_INIT, None, ALU.subtract)
            def shifted(h, c):
                if h >= 2:
                    dve.wait_ge(unit_filled, UNIT_AT[f"aT{h - 2}"] + 1)
                s = 4 * (h % 2) + 2 * c
                ps = filled(f"sc{h}_{c}")
                p = dp[h % 2][:, c, :]
                tt(p, ps[:, 0:384], causal, ALU.add).then_inc(dve_emptied, 1)
                dve.drain()
                dve.reduce_max(stat_mx[:, s:s + 1], p[:, 0:P], AX_X)
                dve.reduce_max(stat_mx[:, s + 1:s + 2], p[:, P:384], AX_X)
                dve.drain()
                ts(stat_nb[:, s:s + 2], stat_mx[:, s:s + 2], -DIFF_SCALE, None, ALU.mult).then_inc(sm_in, 1)

            def combine(h):
                dve.wait_ge(sm_exp, 4 * h + 4)
                s = 4 * (h % 2)
                dve.reciprocal(stat_r[:, s:s + 4], stat_l[:, s:s + 4])
                dve.drain()
                ts(stat_r[:, s + 2:s + 4], stat_r[:, s + 2:s + 4], neglam, None, ALU.mult)
                for q, (a, b) in enumerate(((0, P), (P, 384))):
                    ts(dp[h % 2][:, 0, a:b], dp[h % 2][:, 0, a:b], stat_r[:, s + q:s + q + 1], None, ALU.mult)
                dve.drain()
                for q, (a, b) in enumerate(((0, P), (P, 384))):
                    last = stt(dp[h % 2][:, 0, a:b], dp[h % 2][:, 1, a:b], stat_r[:, s + 2 + q:s + 3 + q], dp[h % 2][:, 0, a:b],
                               ALU.mult, ALU.add)
                last.then_inc(a_ready, 1)

            for level in range(1, LEVELS):
                for g in range(TB):
                    gs = slice(4 * g, 4 * g + 4)
                    if level < LEVELS - 1:
                        ps = as3(filled(f"X{level}_{g}"), 4)
                        tt(X[:, gs, :], X[:, gs, :], ps, ALU.subtract).then_inc(dve_emptied, 1)
                    ps = as3(filled(f"XT{level}_{g}"), 4)
                    tt(XT[:, gs, :], XT[:, gs, :], ps, ALU.subtract).then_inc(dve_emptied, 1)
                dve.drain()
                if level >= 4:
                    if level > 4:
                        combine(level - 5)
                    shifted(level - 4, 0)
                    shifted(level - 4, 1)

            roots = [0]

            def normed(src, b, col, weights, signal):
                s3 = src.rearrange("p (g s) -> p g s", g=4)
                q3 = o_sq[:, 0:512].rearrange("p (g s) -> p g s", g=4)
                tt(q3, s3, s3, ALU.mult)
                dve.drain()
                dve.tensor_reduce(rs8[:, 0:4], q3, AX_X, ALU.add)
                dve.drain()
                ts(rs8[:, 0:4], rs8[:, 0:4], 1.0 / P, RMS_EPS, ALU.mult, ALU.add).then_inc(var_in, 1)
                roots[0] += 1
                dve.wait_ge(var_out, roots[0])
                tt(s3, s3, row_b(rs8[:, 0:4], 4, P), ALU.mult)
                dve.drain()
                dst = mem3[:, b, col:col + 512].rearrange("p (g s) -> p g s", g=4)
                tt(dst, s3, weights, ALU.mult).then_inc(signal, 1)

            combine(2)
            shifted(3, 0)
            shifted(3, 1)
            ps = as3(filled("WS"), 4)
            wait_emptied(dve, "U1")
            tt(vnew, u_sb[:, 4:8, :], ps, ALU.subtract).then_inc(vnew_ready, 1)
            dve.drain()
            dve.sem_inc(dve_emptied, 1)
            combine(3)
            wait_emptied(dve, "O1")
            o_flat = gdn_mem[:, 1024:2048]
            for b in range(TB):
                sz_b = sz3[:, b, :].rearrange("p (g s) -> p g s", g=4)
                normed(o_flat[:, 512 * b:512 * b + 512], b, 0, sz_b, mix_ready)
            for b in range(TB):
                wait_emptied(dve, f"OD{b}")
                normed(od_sb[:, 512 * b:512 * b + 512], b, 512, tile_b(dnw_keep[:, :], 4, P), mix_ready)

            bn3 = bn.rearrange("p (a s) -> p a s", a=2)

            def standardise(b):
                xb = x3[:, b, :]
                dve.drain()
                dve.bn_aggr(mv, bn3)
                dve.drain()
                ts(rstd, mv[:, 1:2], LN_EPS, None, ALU.add).then_inc(var_in, 1)
                roots[0] += 1
                dve.wait_ge(var_out, roots[0])
                return ts(xb, xb, mv[:, 0:1], rstd, ALU.subtract, ALU.mult)

            def residual(name, b, h):
                part = x3[:, b, h * HALF:(h + 1) * HALF]
                stt(part, part, ALPHA, filled(name)[:, :], ALU.mult, ALU.add).then_inc(dve_emptied, 1)
                dve.drain()
                dve.bn_stats(bn3[:, h, :], part)

            def gains(b, loads):
                dve.wait_ge(ld_ln, loads)
                dve.drain()
                tt(x3[:, b, :], x3[:, b, :], ln_g, ALU.mult)
                dve.drain()
                return tt(x3[:, b, :], x3[:, b, :], ln_b, ALU.add)

            def norm_both(unit, transposed, loads):
                for b in range(TB):
                    residual(f"{unit}{2 * b}", b, 0)
                    residual(f"{unit}{2 * b + 1}", b, 1)
                    standardise(b).then_inc(ln_applied, 1)
                    if b == 0:
                        dve.wait_ge(unit_filled, UNIT_AT[transposed + "1"] + 1)
                        gains(0, loads).then_inc(ln_ready, 1)

            norm_both("h", "x1T", 32)

            for h in range(HEADS):
                ps = as3(filled(f"xs{h}"), 2)
                dve.reduce_max(stat_mx[:, 2 * h:2 * h + 2], ps, AX_X)
                dve.drain()
                ts(stat_nb[:, 2 * h:2 * h + 2], stat_mx[:, 2 * h:2 * h + 2], -XA_SCALE, None, ALU.mult).then_inc(xsm_in, 1)
            for h in range(HEADS):
                dve.wait_ge(xsm_exp, 2 * h + 2)
                dve.sem_inc(dve_emptied, 1)
                dve.reciprocal(stat_r[:, 2 * h:2 * h + 2], stat_l[:, 2 * h:2 * h + 2])
                dve.drain()
                tt(xp[:, h, :, :], xp[:, h, :, :], row_b(stat_r[:, 2 * h:2 * h + 2], 2, 256), ALU.mult).then_inc(xp_ready, 1)
            dve.wait_ge(ln_ready, 2)
            norm_both("wo", "x2T", 64)

            ps = filled("router")
            l3, e3, M3, G3 = (v.rearrange("p (b n) -> p b n", b=2) for v in (logit, expl, M, G))
            tt(l3, ps[:, 0:64].rearrange("p (b n) -> p b n", b=2), rb.unsqueeze(1).broadcast_to([P, 2, 32]), ALU.add)\
                .then_inc(dve_emptied, 1)
            dve.drain()
            for b in range(TB):
                dve.max(top8[:, 8 * b:8 * b + 8], l3[:, b, :])
            dve.drain()
            for b in range(TB):
                ts(e3[:, b, :], l3[:, b, :], top8[:, 8 * b:8 * b + 1], None, ALU.subtract)
            dve.drain()
            dve.sem_inc(rt_in, 1)
            t8 = top8.rearrange("p (b n) -> p b n", b=2)
            dve.memset(t8[:, :, TOP_K:8], NEG)
            dve.drain()
            for b in range(TB):
                dve.match_replace(M3[:, b, :], t8[:, b, :], l3[:, b, :], NEG)
            dve.drain()
            ts(M, M, NEG, None, ALU.is_equal)
            dve.wait_ge(rt_exp, 1)
            dve.drain()
            tt(G, expl, M, ALU.mult)
            dve.drain()
            dve.tensor_reduce(gsum, G3, AX_X, ALU.add)
            dve.drain()
            dve.reciprocal(gsum, gsum)
            dve.drain()
            tt(G3, G3, gsum.unsqueeze(2).broadcast_to([P, 2, 32]), ALU.mult)
            dve.drain()
            dve.sem_inc(route_ready, 1)
            dve.wait_ge(ld_iota, 16)
            ps = filled("pos")
            dve.tensor_copy(pos, ps[:, 0:64])
            dve.tensor_copy(cumc[0:32, 0:1], ps[0:32, 64:65])
            dve.drain()
            dve.sem_inc(dve_emptied, 1)
            M2, pos2, G2 = M3, pos.rearrange("p (b n) -> p b n", b=2), G3

            def select(e):
                for b in range(TB):
                    ts(selw[:, b, :], iota2, pos2[:, b, bass.ds(e, 1)], M2[:, b, bass.ds(e, 1)], ALU.is_equal, ALU.mult)
                dve.drain()
                for b in range(TB):
                    last = ts(pos2[:, b, bass.ds(e, 1)], pos2[:, b, bass.ds(e, 1)], float(CAP), None, ALU.subtract)
                last.then_inc(sel_ready, 1)

            select(0)
            ts(nblk[0:32, 0:1], cumc[0:32, 0:1], float(CAP), 1.0, ALU.is_gt, ALU.add)
            for r in range(2, SEQ // CAP):
                dve.drain()
                stt(nblk[0:32, 0:1], cumc[0:32, 0:1], float(r * CAP), nblk[0:32, 0:1], ALU.is_gt, ALU.add)
            dve.drain()
            dve.sem_inc(cnt_ready, 1)
            ps = filled("cum")
            dve.tensor_copy(cumc[0:32, 1:2], ps[0:32, 0:1])
            dve.tensor_copy(itab[0:1, T_CUM:T_CUM + 32], ps[0:1, 32:64])
            dve.drain()
            dve.sem_inc(dve_emptied, 1)
            ts(emask, niota[0:32, :], cumc[0:32, 1:2], None, ALU.is_ge).then_inc(cnt_ready, 1)
            dve.tensor_copy(xgT, filled("xgT0")[:, :].rearrange("p (k s) -> p k s", k=4)).then_inc(dve_emptied, 1)
            ps = filled("etab")
            ts(erow, ps[0:1, 0:64], float(N_EXPERTS - 1), None, ALU.min).then_inc(dve_emptied, 1)
            dve.drain()
            dve.tensor_copy(itab[0:1, T_E:T_E + 64], erow)
            ts(itab[0:1, T_E16:T_E16 + 64], erow, 16.0, None, ALU.mult)
            dve.drain()
            dve.sem_inc(tab_ready, 1)
            dve.sem_inc(xgT_ready, 1)
            for i in range(4):
                b, cols = i // 2, slice((i % 2) * HALF, (i % 2 + 1) * HALF)
                last = stt(yacc[:, b, cols], x3[:, b, cols], ALPHA, filled(f"eb{i}")[:, :], ALU.mult, ALU.add)
                last.then_inc(dve_emptied, 1)
            dve.drain()
            dve.sem_inc(acc_done, 1)

            def copy_xgT():
                dve.tensor_copy(xgT, banks[6][:, :].rearrange("p (k s) -> p k s", k=4)).then_inc(xgT_ready, 1)

            def accumulate(b):
                for h in range(2):
                    part = yacc[:, b, h * HALF:(h + 1) * HALF]
                    last = tt(part, part, banks[((7, 5), (0, 1))[b][h]][:, :], ALU.add)
                return last

            blocks = dve.value_load(itab[0:1, T_CUM + N_EXPERTS - 1:T_CUM + N_EXPERTS], min_val=N_EXPERTS, max_val=MAX_BLOCKS)
            with dve.Fori(0, blocks) as n:
                e = dve.value_load(itab[0:1, bass.ds(n + T_E, 1)], min_val=0, max_val=N_EXPERTS - 1)
                e_next = dve.value_load(itab[0:1, bass.ds(n + (T_E + 1), 1)], min_val=0, max_val=N_EXPERTS - 1)
                dve.drain()
                dve.wait_ge(gselT_done, n + 1)
                for b in range(TB):
                    last = ts(gsel[:, b, :], selw[:, b, :], G2[:, b, bass.ds(e, 1)], None, ALU.mult)
                last.then_inc(gsel_ready, 1)
                dve.drain()
                select(e_next)
                bias4 = [ebias[:, w, :].rearrange("p (e k) -> p e k", k=KC) for w in range(2)]
                for f in range(2):
                    dve.wait_ge(guT_done, n * 2 + (f + 1))
                    gT = banks[2 + f][:, :].rearrange("p (k g s) -> p k g s", k=4, g=2)

                    def bias(w):
                        b = bias4[w][:, bass.ds(e, 1), 4 * f:4 * f + 4].rearrange("p e k -> p (e k)")
                        return b.unsqueeze(2).broadcast_to([P, 4, CAP])

                    tt(mg[:, f, :, :], gT[:, :, 0, :], bias(0), ALU.add)
                    tt(mu[:, f, :, :], gT[:, :, 1, :], bias(1), ALU.add)
                    dve.drain()
                    ts(mg[:, f, :, :], mg[:, f, :, :], SWIGLU_LIMIT, None, ALU.min).then_inc(mg_ready, 1)
                    ts(mu[:, f, :, :], mu[:, f, :, :], SWIGLU_LIMIT, -SWIGLU_LIMIT, ALU.min, ALU.max)
                    dve.drain()
                    stt(tmp[:, f, :, :], mu[:, f, :, :], 1.0, mg[:, f, :, :], ALU.add, ALU.mult)
                dve.drain()
                for f in range(2):
                    dve.wait_ge(sig_ready, n * 2 + (f + 1))
                    tt(hT[:, 4 * f:4 * f + 4, :], tmp[:, f, :, :], sig[:, f, :, :], ALU.mult).then_inc(hT_ready, 1)
                dve.wait_ge(xgT_done, n + 1)
                copy_xgT()
                for b in range(TB):
                    dve.wait_ge(scat_done, n * 2 + (b + 1))
                    last = accumulate(b)
                last.then_inc(acc_done, 1)
            dve.drain()
            for b in range(TB):
                dve.wait_ge(scat_done, blocks * 2 + (b + 1))
                for h in range(2):
                    part = yacc[:, b, h * HALF:(h + 1) * HALF]
                    tt(x3[:, b, h * HALF:(h + 1) * HALF], part, banks[((7, 5), (0, 1))[b][h]][:, :], ALU.add)
                    dve.drain()
                    dve.bn_stats(bn3[:, h, :], x3[:, b, h * HALF:(h + 1) * HALF])
                standardise(b)
                dve.wait_ge(ld_ln, 96)
                dve.drain()
                if b == 0:
                    tt(x3[:, 0, :], x3[:, 0, :], ln_g, ALU.mult).then_inc(fin_in, 1)
                else:
                    gains(1, 96).then_inc(out_ready, 1)


_INS = ['x', 'mem', 'w_in', 'gdn_conv_w', 'gdn_a_log', 'gdn_dt_bias', 'gdn_norm_w', 'diff_lq1', 'diff_lk1', 'diff_lq2',
        'diff_lk2', 'diff_norm_w', 'w_out', 'ln1_g', 'ln1_b', 'xa_wq', 'xa_wk', 'xa_wv', 'xa_wo', 'ln2_g', 'ln2_b',
        'router_w', 'router_b', 'exp_w_gate', 'exp_b_gate', 'exp_w_up', 'exp_b_up', 'exp_w_down', 'exp_b_down',
        'ln3_g', 'ln3_b']


def kernel(**inputs):
    import numpy as _np
    import concourse.bacc as _bacc
    from concourse import mybir as _mybir
    from concourse.bass_utils import run_bass_kernel_spmd as _run

    nc = _bacc.Bacc("TRN2", target_bir_lowering=False, num_devices=1, dynamic_dma_scratch_size=256)
    arrays, args = {}, {}
    for name in _INS:
        a = _np.ascontiguousarray(inputs[name])
        arrays[f"in_{name}_dram"] = a
        args[name] = nc.dram_tensor(f"in_{name}_dram", a.shape, _mybir.dt.from_np(a.dtype), kind="ExternalInput").ap()
    a = constants()
    arrays["in_consts_dram"] = a
    args["consts"] = nc.dram_tensor("in_consts_dram", a.shape, _mybir.dt.from_np(a.dtype), kind="ExternalInput").ap()
    out = nc.dram_tensor("out_dram", (1, SEQ, D_MODEL), F32, kind="ExternalOutput").ap()
    trunk_kernel(nc, args, out)
    r = _run(nc, [arrays], core_ids=[0])
    return r.results[0]["out_dram"]
```

```python
from contextlib import ExitStack

import numpy as np

import concourse.bass as bass
from concourse import mybir

F32 = mybir.dt.float32
I32 = mybir.dt.int32
ALU = mybir.AluOpType
ACT = mybir.ActivationFunctionType
AX_X = mybir.AxisListType.X

P = 128
D_MODEL = 1024
SEQ = 256
TB = SEQ // P
KC = D_MODEL // P
HALF = D_MODEL // 2
DEPTH = 1
ALPHA = (2 * DEPTH) ** 0.25
LN_EPS = 1e-5
RMS_EPS = 1e-6

HEADS = 4
GDN_DK = 128
GDN_TAPS = 4
CONV_CHUNKS = 12
PAD = GDN_TAPS - 1
PAIRS = TB * HEADS
LEVELS = 7
DIFF_D = 64
DIFF_SCALE = DIFF_D ** -0.5
LAMBDA_INIT = 0.8 - 0.6
XA_SCALE = 256 ** -0.5
NEG = -3.0e38

N_EXPERTS = 32
TOP_K = 4
CAP = 64
MAX_BLOCKS = N_EXPERTS + SEQ * TOP_K // CAP
SWIGLU_ALPHA = 1.702
SWIGLU_LIMIT = 7.0

C_QK, C_VZ, C_BA, C_DQK, C_DV, IN_COLS = 0, 1024, 2048, 2056, 3080, 3592

K_ID, K_UT, K_US, K_ONE, K_CM, K_LEV0, K_LEVT = 0, 128, 256, 384, 512, 896, 1024
N_CONST = K_LEV0
N_LEVEL_MASKS = P * (LEVELS + 1)
K_IOTA = K_LEV0 + N_LEVEL_MASKS
K_NIOTA = K_IOTA + P
K_END = K_NIOTA + 64


def constants():
    r = np.arange(P)[:, None]
    c = np.arange(P)[None, :]
    out = np.zeros((P, K_END), np.float32)
    out[:, K_ID:K_ID + P] = r == c
    out[:, K_UT:K_UT + P] = r <= c
    out[:, K_US:K_US + P] = r < c
    out[:, K_ONE:K_ONE + P] = 1.0
    future = np.where(c > r, NEG, 0.0)
    out[:, K_CM:K_CM + P] = future
    out[:, K_CM + 2 * P:K_CM + 3 * P] = future
    out[:, K_IOTA:K_IOTA + P] = np.arange(P) % CAP
    out[:, K_NIOTA:K_NIOTA + 64] = np.arange(64)

    def below(t, s, size):
        return (t // (2 * size) == s // (2 * size)) & (t % (2 * size) >= size) & (s % (2 * size) < size)

    out[:, K_LEV0:K_LEV0 + P] = below(r, c, 1)
    for level in range(LEVELS):
        at = K_LEVT + P * level
        out[:, at:at + P] = below(c, r, 1 << level)
    return out


LEVEL_FILL = {
    1: [("dqk3", "A")],
    2: [("dv0", "A")],
    3: [("dv1", "A")] + [(f"memT{i}", "A") for i in range(4)],
    4: [("sc0_0", "D"), ("sc0_1", "D"), ("km0", "A")],
    5: [("sc1_0", "D"), ("sc1_1", "D"), ("aT0", "A"), ("km1", "A")],
    6: [("sc2_0", "D"), ("sc2_1", "D"), ("aT1", "A"), ("km2", "A")],
}


def unit_table():
    u = [(f"xT{i}", "D") for i in range(4)] + [("ba", "D"), ("columns", "D")]
    u += [(f"qk{i}", "A") for i in range(4)] + [(f"v{i}", "A") for i in range(2)]
    u += [("z0", "A"), ("gcum", "D"), ("R0", "D"), ("R1", "D"), ("z1", "A")]
    u += [(f"ss{i}", "A") for i in range(4)]
    u += [("dqk0", "A"), ("vtok0", "D"), ("vtok1", "D")]
    u += [("KK0", "D"), ("KK1", "D"), ("KQ0", "D"), ("KQ1", "D"), ("ktok0", "D"), ("ktok1", "D"), ("dqk1", "A")]
    u += [("LT0", "A"), ("LT1", "A"), ("dqk2", "A")]
    for level in range(1, LEVELS):
        u += [(f"M{level}_0", "A"), (f"M{level}_1", "A")]
        for g in range(TB):
            if level < LEVELS - 1:
                u += [(f"X{level}_{g}", "D")]
            u += [(f"XT{level}_{g}", "D")]
        u += LEVEL_FILL[level]
    u += [("U0", "A"), ("U1", "A"), ("WT", "A"), ("sc3_0", "D"), ("sc3_1", "D"), ("S", "A"), ("O0", "A"), ("aT2", "A")]
    u += [("WS", "D"), ("km3", "A"), ("O1", "A"), ("aT3", "A"), ("vm0", "A"), ("OD0", "A"), ("OD1", "A"), ("vm1", "A")]
    u += [("mixT0", "A"), ("mixT1", "D"), ("mixT2", "A"), ("mixT3", "D")]
    u += [("h0", "D"), ("h1", "D"), ("h2", "D"), ("x1T0", "A"), ("x1T1", "A"), ("h3", "D"), ("x1T2", "A"), ("x1T3", "D")]
    u += [("xq0", "A"), ("xq1", "A"), ("xs0", "D"), ("xq2", "A"), ("xs1", "D"), ("xq3", "A"), ("xs2", "D")]
    u += [("xs3", "D"), ("vm2", "A"), ("pT0", "A"), ("pT1", "A"), ("vm3", "A"), ("pT2", "A"), ("oT0", "A"), ("oT1", "A")]
    u += [("pT3", "A"), ("oT2", "A"), ("oT3", "A")]
    u += [("wo0", "D"), ("wo1", "D"), ("wo2", "D"), ("x2T0", "A"), ("x2T1", "A"), ("wo3", "D"), ("bT", "A")]
    u += [("x2T2", "A"), ("x2T3", "D"), ("router", "D"), ("pos", "D"), ("GT", "A")]
    u += [("eb0", "D"), ("xg0", "A"), ("cum", "D"), ("eb1", "D"), ("xgT0", "D"), ("etab", "D"), ("eb2", "D"), ("eb3", "D")]
    return u


UNITS = unit_table()
UNIT_AT = {name: i for i, (name, _) in enumerate(UNITS)}
N_UNITS = len(UNITS)


def emptied(name):
    at = UNIT_AT[name]
    engine = UNITS[at][1]
    return engine, sum(e == engine for _, e in UNITS[:at + 1])


ATTENTION_LOADS = [
    ("w_in", C_QK, 1024, 0), ("w_in", C_QK, 1024, 1), ("w_in", C_VZ, 1024, 0), ("w_in", C_VZ, 1024, 1),
    ("w_in", C_DQK, 1024, 0), ("w_in", C_DQK, 1024, 1), ("w_in", C_DV, 512, None),
    ("xa_wk", 0, 1024, 0), ("xa_wk", 0, 1024, 1), ("w_out", 0, 1024, 0), ("w_out", 0, 1024, 1),
    ("xa_wv", 0, 1024, 0), ("xa_wv", 0, 1024, 1), ("xa_wq", 0, 1024, 0), ("xa_wq", 0, 1024, 1),
    ("xa_wo", 0, 1024, 0), ("xa_wo", 0, 1024, 1),
]
N_ATT = len(ATTENTION_LOADS)
SLOTS = 6
G0, U0, G1, U1, D0, D1 = range(6)
ROLE_INPUT = ["exp_w_gate", "exp_w_up", "exp_w_gate", "exp_w_up", "exp_w_down", "exp_w_down"]
ROLE_SLOT = [(N_ATT + r) % SLOTS for r in range(SLOTS)]
TWO_SLOT_ROLES = (U1, D0, D1)
SLOT_COLS = 4 * D_MODEL
ROLE_EARLIER = [sum(i % SLOTS == s for i in range(N_ATT)) for s in ROLE_SLOT]


def trunk_kernel(nc, d, out):
    ctx = ExitStack()
    with ctx:
        def sb(name, cols, dt=F32, rows=P):
            return ctx.enter_context(nc.sbuf_tensor(name, [rows, cols], dt))

        def sem(name):
            return ctx.enter_context(nc.semaphore(name))

        main_cols = [("ring", SLOTS * SLOT_COLS),
                     ("conv_out", CONV_CHUNKS * SEQ),
                     ("sz", TB * 512),
                     ("memT_mem", KC * SEQ),
                     ("mem_mem", TB * D_MODEL),
                     ("km", KC * SEQ), ("vm", TB * D_MODEL), ("x_sb", TB * D_MODEL),
                     ("ln_mem", 2 * D_MODEL),
                     ("gdn_mem", 6144),
                     ("xT_mem", KC * SEQ)]
        main = sb("main", sum(cols for _, cols in main_cols))
        region, start = {}, {}
        for name, cols in main_cols:
            start[name] = sum(region[n].shape[1] for n in region)
            region[name] = main[:, start[name]:start[name] + cols]
        ring, conv_out, sz, memT_mem, mem_mem, km, vm, x_sb, ln_mem, gdn_mem, xT_mem = (region[n] for n, _ in main_cols)
        odd_slot = {U1: start["conv_out"], D0: start["memT_mem"], D1: start["gdn_mem"] + 6144 - TB * D_MODEL}

        def weights_at(role, odd):
            return odd_slot[role] if odd and role in TWO_SLOT_ROLES else ROLE_SLOT[role] * SLOT_COLS

        conv_in = sb("conv_in", CONV_CHUNKS * (SEQ + PAD))
        dqk = sb("dqk", KC * SEQ)
        dv = sb("dv", TB * 512)
        kst = sb("kst", N_CONST)
        small = sb("small", 680)
        itab = sb("itab", 96, I32)

        slots = [ring[:, s * 4096:(s + 1) * 4096].rearrange("p (k n) -> p k n", k=4) for s in range(SLOTS)]
        x3 = x_sb[:, :].rearrange("p (b n) -> p b n", b=TB)
        xT = xT_mem[:, :].rearrange("p (k t) -> p k t", k=KC)
        mem3 = mem_mem[:, :].rearrange("p (b n) -> p b n", b=TB)
        memT = memT_mem[:, :].rearrange("p (k t) -> p k t", k=KC)
        cin = conv_in[:, :].rearrange("p (c t) -> p c t", c=CONV_CHUNKS)
        cout = conv_out[:, :].rearrange("p (c t) -> p c t", c=CONV_CHUNKS)
        qn, kn, vT = cout[:, 0:4, :], cout[:, 4:8, :], cout[:, 8:12, :]

        def pairs(mem, at, n=PAIRS):
            return mem[:, at:at + n * P].rearrange("p (g s) -> p g s", g=n)

        Dm, DT, L = pairs(conv_in, 0), pairs(conv_in, 1024), pairs(conv_in, 2048)
        X, XT, u_sb = Dm, DT, L
        wT, S_sb = pairs(conv_in, 0, 4), pairs(conv_in, 512, 4)
        BT = pairs(conv_out, 2048)
        LT, M1, AT, kbg, vbeta = (pairs(gdn_mem, 1024 * i) for i in range(5))
        ktail, qd = pairs(gdn_mem, 5120, 4), pairs(gdn_mem, 5632, 4)
        gB, diff, vnew, o_sb = M1, LT, pairs(gdn_mem, 0, 4), M1
        sq_mem = gdn_mem[:, 3072:5120]
        sq = sq_mem.rearrange("p (c t) -> p c t", c=8)
        sz3 = sz[:, :].rearrange("p (b n) -> p b n", b=TB)
        dqk3 = dqk[:, :].rearrange("p (k t) -> p k t", k=KC)
        dv3 = dv[:, :].rearrange("p (b n) -> p b n", b=TB)
        km3 = km[:, :].rearrange("p (k t) -> p k t", k=KC)
        vm3 = vm[:, :].rearrange("p (b n) -> p b n", b=TB)
        dp = [vm[:, 768 * i:768 * (i + 1)].rearrange("p (c n) -> p c n", c=2) for i in range(2)]
        aT = xT_mem[:, 0:4 * 384].rearrange("p (h n) -> p h n", h=4)
        o_flat = gdn_mem[:, 1024:2048]
        od_sb = conv_out[:, 2048:3072]
        xp = gdn_mem[:, 3072:5120].rearrange("p (h b m) -> p h b m", h=4, b=TB)
        pT = mem_mem[:, :].rearrange("p (h m t) -> p h m t", h=4, m=TB)
        oT = conv_in[:, 0:2048].rearrange("p (k t) -> p k t", k=KC)

        ident = kst[:, K_ID:K_ID + P]
        upper = kst[:, K_UT:K_UT + P]
        strict = kst[:, K_US:K_US + P]
        ones = kst[:, K_ONE:K_ONE + P]
        causal = kst[:, K_CM:K_CM + 3 * P]
        iota2 = gdn_mem[:, 2432:2432 + P]
        niota = gdn_mem[:, 2432 + P:2432 + P + 64]
        lev0 = ln_mem[:, 0:P]
        levT = [ln_mem[:, P * (1 + i):P * (2 + i)] for i in range(LEVELS)]
        ln_g, ln_b = ln_mem[:, 0:D_MODEL], ln_mem[:, D_MODEL:2 * D_MODEL]

        at = [0]

        def take(n):
            at[0] += n
            return small[:, at[0] - n:at[0]]

        columns = take(80)
        convw = columns[:, 0:48]
        gcol1, bcol1, gcol2, bcol2 = (columns[:, 48 + 8 * i:56 + 8 * i] for i in range(4))
        ba = take(16)
        beta = take(8)
        g_log = take(8)
        gcum = take(8)
        eg = take(8)
        begs = take(8)
        tails = take(8)
        sp_a, sp_b, sp_c = take(8), take(8), take(8)
        a_log, dt_b = take(4), take(4)
        lamv = take(4)
        neglam = take(1)
        rs16 = take(16)
        stat_mx, stat_nb, stat_l, stat_r = take(8), take(8), take(8), take(8)
        bn = take(12)
        mv = take(2)
        rstd = take(1)
        top8 = take(16)
        gsum = take(2)
        nblk, cumc = take(2), take(2)
        rb = take(32)
        eps_rms = take(1)
        minus_half = take(4)
        logit, expl, M, G, pos = (take(64) for _ in range(5))
        assert at[0] <= 680

        def row_b(v, n, k):
            return v.unsqueeze(2).broadcast_to([P, n, k])

        def tile_b(v, n, k):
            return v.unsqueeze(1).broadcast_to([P, n, k])

        columns_raw = sz[0:80, 0:128]
        lam_raw = vm[:, 0:256]
        gnw = vm[:, 256:384]
        dnw = km[:, 0:128]
        dnw_keep = sb("dnw_keep", 128)

        yacc = vm3
        xgT = km[:, 0:512].rearrange("p (k s) -> p k s", k=4)
        gu = km[:, 512:1536].rearrange("p (f n) -> p f n", f=2)
        hT = km[:, 1536:2048].rearrange("p (k s) -> p k s", k=KC)
        mg, mu, sig, tmp = (conv_in[:, 512 * i:512 * (i + 1)].rearrange("p (f k s) -> p f k s", f=2, k=4) for i in range(4))
        y_sb = conv_in[:, 2048:2560]
        xg_sb = conv_in[:, 2560:3072]
        selw = gdn_mem[:, 0:256].rearrange("p (b s) -> p b s", b=TB)
        gsel = gdn_mem[:, 256:512].rearrange("p (b s) -> p b s", b=TB)
        gselT = gdn_mem[:, 512:768]
        ebias = gdn_mem[:, 768:1280].rearrange("p (w n) -> p w n", w=2)
        GT = gdn_mem[0:N_EXPERTS, 1280:1536]
        emask = gdn_mem[0:N_EXPERTS, 1536:1600]
        erow = gdn_mem[0:1, 1600:1664]
        crow = gdn_mem[0:1, 1664:1696]
        bias_raw = gdn_mem[:, 1792:2304].rearrange("p (w b n) -> p w b n", w=2, b=2)
        bdown = dqk[0:N_EXPERTS, 0:D_MODEL]
        T_E, T_CUM = 0, 64
        rtmp = gdn_mem[:, 2304:2368]
        rtmp2 = gdn_mem[:, 2368:2432]

        banks = [ctx.enter_context(nc.psum_tensor(f"bank{i}", [P, 512], F32)) for i in range(8)]

        def bank(name):
            return banks[UNIT_AT[name] % 8]

        moe_bank = [banks[(UNIT_AT["xg0"] + i) % 8] for i in range(8)]

        unit_filled = sem("unit_filled")
        act_emptied = sem("act_emptied")
        dve_emptied = sem("dve_emptied")
        ring_full = [sem(f"ring_full{s}") for s in range(SLOTS)]
        odd_full = {role: sem(f"odd_full{role}") for role in TWO_SLOT_ROLES}
        ring_used = sem("ring_used")
        ld_x, ld_const, ld_lev, ld_mem, ld_vec, ld_ba = (sem(n) for n in ("ld_x", "ld_const", "ld_lev", "ld_mem", "ld_vec", "ld_ba"))
        ld_ln = sem("ld_ln")
        ld_iota = sem("ld_iota")
        ld_rt, ld_bias, ld_bdown = sem("ld_rt"), sem("ld_bias"), sem("ld_bdown")
        ld_cols = sem("ld_cols")
        gu0_used = sem("gu0_used")
        pad_zero = sem("pad_zero")
        conv_ready = sem("conv_ready")
        silu_ready = sem("silu_ready")
        sq_ready = sem("sq_ready")
        exp_ready = sem("exp_ready")
        gate_step = sem("gate_step")
        qk_normed = sem("qk_normed")
        dec_in, dec_exp, dec_ready = sem("dec_in"), sem("dec_exp"), sem("dec_ready")
        qd_in, qd_exp = sem("qd_in"), sem("qd_exp")
        l2_exp = sem("l2_exp")
        eps_set = sem("eps_set")
        var_in, var_out = sem("var_in"), sem("var_out")
        lmat_ready = sem("lmat_ready")
        x_init = sem("x_init")
        xt_init = sem("xt_init")
        bt_ready = sem("bt_ready")
        vnew_ready = sem("vnew_ready")
        lam_in, lam_exp = sem("lam_in"), sem("lam_exp")
        sm_in, sm_exp = sem("sm_in"), sem("sm_exp")
        a_ready = sem("a_ready")
        mix_ready = sem("mix_ready")
        ln_ready = sem("ln_ready")
        xsm_in, xsm_exp, xp_ready = sem("xsm_in"), sem("xsm_exp"), sem("xp_ready")
        rt_in, rt_exp = sem("rt_in"), sem("rt_exp")
        route_ready = sem("route_ready")
        cnt_ready = sem("cnt_ready")
        tab_ready = sem("tab_ready")
        sel_ready = sem("sel_ready")
        gsel_ready = sem("gsel_ready")
        xg_done, xg_copied = sem("xg_done"), sem("xg_copied")
        xgT_done, xgT_ready = sem("xgT_done"), sem("xgT_ready")
        gu_done, gu_copied = sem("gu_done"), sem("gu_copied")
        guT_done = sem("guT_done")
        gselT_done, gselT_ready = sem("gselT_done"), sem("gselT_ready")
        mg_ready, sig_ready, hT_ready = sem("mg_ready"), sem("sig_ready"), sem("hT_ready")
        d0_used = sem("d0_used")
        y_done, y_copied = sem("y_done"), sem("y_copied")
        scat_done, acc_done = sem("scat_done"), sem("acc_done")
        ln_applied = sem("ln_applied")
        fin_in, fin_out = sem("fin_in"), sem("fin_out")
        out_ready, out_stored = sem("out_ready"), sem("out_stored")

        def wait_emptied(eng, name):
            engine, count = emptied(name)
            eng.wait_ge(act_emptied if engine == "A" else dve_emptied, count)

        block = ctx.enter_context(nc.Block())

        @block.sync
        def _(sp):
            sp.dma_start(x3, d["x"][0].rearrange("(b p) n -> p b n", p=P)).then_inc(ld_x, 16)
            ba_dst = dnw_keep[:, 0:64].rearrange("p (k n) -> p k n", k=KC)
            sp.dma_start(ba_dst, d["w_in"][0, :, C_BA:C_BA + 8].rearrange("(k p) n -> p k n", p=P)).then_inc(ld_ba, 16)
            sp.dma_start(a_log, d["gdn_a_log"][0:1, :].partition_broadcast(P)).then_inc(ld_ba, 16)
            sp.dma_start(dt_b, d["gdn_dt_bias"][0:1, :].partition_broadcast(P)).then_inc(ld_ba, 16)
            for i, (name, col, cols, half) in enumerate(ATTENTION_LOADS):
                if i >= SLOTS:
                    sp.wait_ge(ring_used, i - SLOTS + 1)
                src = d[name][0, :, col:col + cols].rearrange("(k p) n -> p k n", p=P)
                if half is None:
                    dst = ring[:, (i % SLOTS) * 4096:(i % SLOTS + 1) * 4096].rearrange("p (k n) -> p k n", k=KC)
                else:
                    dst, src = slots[i % SLOTS], src[:, 4 * half:4 * half + 4, :]
                sp.dma_start(dst, src).then_inc(ring_full[i % SLOTS], 16)

            def load_role(role, e, odd, ahead=0):
                w = d[ROLE_INPUT[role]][0, ahead:].rearrange("e (k p) n -> e p k n", p=P)
                h = (0, 0, 1, 1, 0, 1)[role]
                at = weights_at(role, odd)
                dst = main[:, at:at + SLOT_COLS].rearrange("p (k n) -> p k n", k=4)
                src = w[bass.ds(e, 1), :, 4 * h:4 * h + 4, :].rearrange("e p k n -> p (e k) n")
                own = odd and role in TWO_SLOT_ROLES
                sp.dma_start(dst, src).then_inc(odd_full[role] if own else ring_full[ROLE_SLOT[role]], 16)

            def load_first(role):
                sp.wait_ge(ring_used, N_ATT + role - SLOTS + 1)
                load_role(role, 0, odd=False)

            for role in (G0, U0, G1, U1):
                load_first(role)
            sp.wait_ge(mix_ready, 4)
            load_role(U1, 1, odd=True)
            sp.wait_ge(unit_filled, UNIT_AT["oT3"] + 1)
            load_role(D0, 1, odd=True)
            load_first(D0)
            load_first(D1)
            sp.wait_ge(unit_filled, UNIT_AT["router"] + 1)
            load_role(D1, 1, odd=True)
            sp.wait_ge(tab_ready, 1)

            def blocks_before(e, ahead=0):
                return sp.value_load(itab[0:1, bass.ds(e + (T_CUM + ahead - 1), 1)], min_val=1, max_val=MAX_BLOCKS)

            def load_one_slot_roles(done, e, odd, ahead=0):
                sp.wait_ge(gu0_used, done)
                load_role(G0, e, odd, ahead)
                load_role(U0, e, odd, ahead)
                sp.wait_ge(gu_done, done * 2)
                load_role(G1, e, odd, ahead)

            def load_down(done, e, odd, ahead=0):
                sp.wait_ge(d0_used, done)
                load_role(D0, e, odd, ahead)
                sp.wait_ge(y_done, done)
                load_role(D1, e, odd, ahead)

            def load_expert(e, ahead, odd):
                done = blocks_before(e, ahead)
                load_one_slot_roles(done, e, odd, ahead)
                load_role(U1, e, not odd, ahead + 1)
                load_down(done, e, not odd, ahead + 1)

            with sp.Fori(0, (N_EXPERTS - 4) // 2) as pair:
                load_expert(pair * 2, 1, odd=True)
                load_expert(pair * 2, 2, odd=False)
            for e in range(N_EXPERTS - 3, N_EXPERTS):
                if e == N_EXPERTS - 3:
                    done = blocks_before(e)
                    load_one_slot_roles(done, e, odd=True)
                else:
                    load_role(U1, e, odd=(e % 2 == 1))
                    load_one_slot_roles(blocks_before(e), e, odd=(e % 2 == 1))
                    load_down(blocks_before(e - 1), e, odd=(e % 2 == 1))

            sp.wait_ge(fin_out, 1)
            sp.dma_start(out[0, 0:P, :], x3[:, 0, :]).then_inc(out_stored, 16)
            sp.wait_ge(out_ready, 1)
            sp.dma_start(out[0, P:SEQ, :], x3[:, 1, :]).then_inc(out_stored, 16)
            sp.wait_ge(out_stored, 32)

        @block.gpsimd
        def _(pool):
            pool.memset(cin[:, :, 0:PAD], 0.0).then_inc(pad_zero, 1)
            pool.memset(eps_rms, RMS_EPS).then_inc(eps_set, 1)
            pool.memset(minus_half, -0.5)
            for j in range(4):
                pool.wait_ge(silu_ready, j + 1)
                pool.tensor_tensor(sq[:, 2 * j:2 * j + 2, :], cout[:, 2 * j:2 * j + 2, :], cout[:, 2 * j:2 * j + 2, :],
                                   ALU.mult).then_inc(sq_ready, 1)
            pool.wait_ge(dec_exp, 1)
            pool.affine_select(out=Dm, in_=Dm, pattern=[[0, PAIRS], [-1, P]], compare_op=ALU.is_gt, fill=0.0,
                               base=0, channel_multiplier=1).then_inc(dec_ready, 1)
            pool.wait_ge(dec_exp, 2)
            pool.affine_select(out=DT, in_=DT, pattern=[[0, PAIRS], [1, P]], compare_op=ALU.is_ge, fill=0.0,
                               base=0, channel_multiplier=-1).then_inc(dec_ready, 1)
            wait_emptied(pool, "LT1")
            wait_emptied(pool, "KQ1")
            pool.wait_ge(ld_lev, 16)
            pool.tensor_tensor(XT, LT, tile_b(levT[0], PAIRS, P), ALU.mult)
            pool.drain()
            pool.tensor_tensor(XT, tile_b(ident, PAIRS, P), XT, ALU.subtract).then_inc(xt_init, 1)
            for level in range(1, LEVELS):
                if level == 1:
                    wait_emptied(pool, "vtok1")
                else:
                    pool.wait_ge(unit_filled, UNIT_AT[f"M{level - 1}_1"] + 1)
                pool.tensor_tensor(BT, LT, tile_b(levT[level], PAIRS, P), ALU.mult).then_inc(bt_ready, 1)
            def root(i, v):
                pool.wait_ge(var_in, i + 1)
                pool.tensor_tensor(v, v, minus_half[:, 0:v.shape[1]], ALU.pow).then_inc(var_out, 1)

            for i in range(4):
                root(i, rs16[:, 4 * i:4 * i + 4])
            for i, name in enumerate(("x1T3", "x2T3")):
                root(4 + 2 * i, rstd)
                root(5 + 2 * i, rstd)
                pool.wait_ge(unit_filled, UNIT_AT[name] + 1)
                pool.wait_ge(ld_ln, 32 * (i + 1))
                pool.tensor_tensor(x3[:, 1, :], x3[:, 1, :], ln_g, ALU.mult)
                pool.drain()
                pool.tensor_tensor(x3[:, 1, :], x3[:, 1, :], ln_b, ALU.add).then_inc(ln_ready, 1)
            pool.memset(y_sb, 0.0)
            pool.memset(gselT, 0.0)
            pool.drain()
            pool.sem_inc(y_copied, 1)
            pool.sem_inc(gselT_ready, 1)
            root(8, rstd)
            root(9, rstd)
            pool.wait_ge(fin_in, 1)
            pool.tensor_tensor(x3[:, 0, :], x3[:, 0, :], ln_b, ALU.add).then_inc(fin_out, 1)

        @block.scalar
        def _(act):
            act.dma_start(kst[:, :], d["consts"][:, 0:N_CONST]).then_inc(ld_const, 16)
            act.dma_start(columns_raw[0:48, :], d["gdn_conv_w"][0].rearrange("t o (c p) -> (t o c) p", p=P)).then_inc(ld_cols, 16)
            for i, name in enumerate(("ln1_g", "ln1_b", "ln2_g", "ln2_b")):
                act.dma_start(columns_raw[48 + 8 * i:56 + 8 * i, :], d[name][0].rearrange("(k p) -> k p", p=P)).then_inc(ld_cols, 16)
            for i, name in enumerate(["diff_lq1", "diff_lk1", "diff_lq2", "diff_lk2"]):
                act.dma_start(lam_raw[:, 64 * i:64 * i + 64], d[name][0:1, :].partition_broadcast(P)).then_inc(ld_vec, 16)
            for dst, name in ((gnw, "gdn_norm_w"), (dnw, "diff_norm_w")):
                act.dma_start(dst, d[name][0:1, :].partition_broadcast(P)).then_inc(ld_vec, 16)
            act.dma_start(mem3, d["mem"][0].rearrange("(b p) n -> p b n", p=P)).then_inc(ld_mem, 16)
            act.dma_start(ln_mem[:, 0:N_LEVEL_MASKS], d["consts"][:, K_LEV0:K_LEV0 + N_LEVEL_MASKS]).then_inc(ld_lev, 16)
            act.dma_start(rb, d["router_b"][0:1, :].partition_broadcast(P)).then_inc(ld_rt, 16)

            def load_gains(name):
                act.dma_start(ln_g, d[name + "_g"][0:1, :].partition_broadcast(P)).then_inc(ld_ln, 16)
                act.dma_start(ln_b, d[name + "_b"][0:1, :].partition_broadcast(P)).then_inc(ld_ln, 16)

            def filled(name):
                act.wait_ge(unit_filled, UNIT_AT[name] + 1)
                return bank(name)

            def empty(name, dst, src=None, func=ACT.Copy, **kw):
                ps = filled(name)
                act.activation(dst, ps[:, :] if src is None else src(ps), func, **kw).then_inc(act_emptied, 1)

            def as3(n):
                return lambda ps: ps[:, :].rearrange("p (g s) -> p g s", g=n)

            act.wait_ge(eps_set, 1)
            act.wait_ge(gate_step, 1)
            act.activation(sp_a, sp_a, ACT.Exp, scale=-1.0).then_inc(exp_ready, 1)
            act.activation(sp_b, sp_b, ACT.Exp, scale=-1.0).then_inc(exp_ready, 1)
            act.activation(a_log, a_log, ACT.Exp).then_inc(exp_ready, 1)
            act.wait_ge(exp_ready, 2)
            act.activation(sp_b, sp_b, ACT.Ln, bias=1.0).then_inc(exp_ready, 1)

            def silu(j):
                act.wait_ge(conv_ready, j + 1)
                act.activation(cout[:, 2 * j:2 * j + 2, :], cout[:, 2 * j:2 * j + 2, :], ACT.Silu).then_inc(silu_ready, 1)

            act.wait_ge(pad_zero, 1)
            empty("qk0", cin[:, 0:2, PAD:], as3(2))
            empty("qk1", cin[:, 2:4, PAD:], as3(2))
            silu(0)
            empty("qk2", cin[:, 4:6, PAD:], as3(2))
            silu(1)
            empty("qk3", cin[:, 6:8, PAD:], as3(2))
            silu(2)
            empty("v0", cin[:, 8:10, PAD:], as3(2))
            silu(3)
            empty("v1", cin[:, 10:12, PAD:], as3(2))
            silu(4)
            empty("z0", sz3[:, 0, :], func=ACT.Silu)
            silu(5)
            empty("z1", sz3[:, 1, :], func=ACT.Silu)
            for i in range(4):
                empty(f"ss{i}", sq_mem[:, 512 * i:512 * (i + 1)], func=ACT.Ln, bias=eps_rms)
            act.wait_ge(act_emptied, emptied("ss3")[1])
            for i in range(4):
                part = sq_mem[:, 512 * i:512 * (i + 1)]
                act.activation(part, part, ACT.Exp, scale=-0.5).then_inc(l2_exp, 1)
            act.wait_ge(lam_in, 1)
            act.activation(lamv[:, 0:2], lamv[:, 0:2], ACT.Exp).then_inc(lam_exp, 1)
            act.wait_ge(gate_step, 3)
            act.activation(eg, gcum, ACT.Exp).then_inc(exp_ready, 1)
            act.wait_ge(dec_in, 1)
            act.activation(tails[:, 0:4], tails[:, 0:4], ACT.Exp).then_inc(exp_ready, 1)
            act.wait_ge(qd_in, 1)
            act.activation(qd, qd, ACT.Exp).then_inc(qd_exp, 1)
            act.wait_ge(dec_in, 2)
            act.activation(Dm, Dm, ACT.Exp, scale=-1.0).then_inc(dec_exp, 1)
            act.wait_ge(dec_in, 3)
            act.activation(DT, DT, ACT.Exp).then_inc(dec_exp, 1)

            empty("dqk0", dqk3[:, 0:2, :], as3(2))
            empty("dqk1", dqk3[:, 2:4, :], as3(2))
            for g in range(TB):
                empty(f"LT{g}", LT[:, 4 * g:4 * g + 4, :], as3(4))
            empty("dqk2", dqk3[:, 4:6, :], as3(2))

            def empty_km(i):
                empty(f"km{i}", km3[:, 2 * i:2 * i + 2, :], as3(2))

            def empty_vm(i):
                empty(f"vm{i}", vm3[:, i // 2, (i % 2) * HALF:(i % 2 + 1) * HALF])

            def empty_T(name, i, dst, gains=None):
                ps = filled(f"{name}{i}")
                tok = slice((i // 2) * P, (i // 2 + 1) * P)
                if gains is None:
                    act.activation(dst[:, 4 * (i % 2):4 * (i % 2) + 4, tok], as3(4)(ps), ACT.Copy).then_inc(act_emptied, 1)
                    return
                for j in range(4):
                    k = 4 * (i % 2) + j
                    last = act.activation(dst[:, k, tok], ps[:, j * P:(j + 1) * P], ACT.Identity,
                                          scale=gains[0][:, k:k + 1], bias=gains[1][:, k:k + 1])
                last.then_inc(act_emptied, 1)

            def diff_exp(h, c):
                i = 2 * h + c
                act.wait_ge(sm_in, i + 1)
                for q, (a, b) in enumerate(((0, P), (P, 3 * P))):
                    act.activation(dp[h % 2][:, c, a:b], dp[h % 2][:, c, a:b], ACT.Exp, scale=DIFF_SCALE,
                                   bias=stat_nb[:, 4 * (h % 2) + 2 * c + q:4 * (h % 2) + 2 * c + q + 1],
                                   accum_out=stat_l[:, 4 * (h % 2) + 2 * c + q:4 * (h % 2) + 2 * c + q + 1]).then_inc(sm_exp, 1)

            def empty_aT(h):
                empty(f"aT{h}", aT[:, h, :], lambda ps: ps[:, 0:384])

            def empty_head_out(name, dst, i, b, col):
                ps = filled(name)
                for h in range(HEADS):
                    act.activation(mem3[:, b, col + h * P:col + (h + 1) * P], ps[:, h * P:(h + 1) * P], ACT.Square,
                                   accum_out=rs16[:, 4 * i + h:4 * i + h + 1])
                act.activation(dst, ps[:, :], ACT.Copy).then_inc(act_emptied, 1)

            for level in range(1, LEVELS):
                for g in range(TB):
                    empty(f"M{level}_{g}", M1[:, 4 * g:4 * g + 4, :], as3(4))
                if level == 1:
                    empty("dqk3", dqk3[:, 6:8, :], as3(2))
                elif level <= 3:
                    empty(f"dv{level - 2}", dv3[:, level - 2, :])
                if level == 3:
                    for i in range(4):
                        empty_T("memT", i, memT)
                if level >= 4:
                    if level > 4:
                        empty_aT(level - 5)
                    diff_exp(level - 4, 0)
                    diff_exp(level - 4, 1)
                    empty_km(level - 4)
            for g in range(TB):
                empty(f"U{g}", u_sb[:, 4 * g:4 * g + 4, :], as3(4))
            empty("WT", wT, as3(4))
            empty("S", S_sb, as3(4))
            empty_head_out("O0", o_flat[:, 0:512], 0, 0, 0)
            empty_aT(2)
            diff_exp(3, 0)
            diff_exp(3, 1)
            empty_km(3)
            empty_head_out("O1", o_flat[:, 512:1024], 1, 1, 0)
            empty_aT(3)
            load_gains("ln1")
            empty_vm(0)
            empty_head_out("OD0", od_sb[:, 0:512], 2, 0, 512)
            empty_head_out("OD1", od_sb[:, 512:1024], 3, 1, 512)
            empty_vm(1)

            act.wait_ge(mix_ready, 2)
            for w, n in enumerate(["exp_b_gate", "exp_b_up"]):
                act.dma_start(bias_raw[:, w, :, :], d[n][0].rearrange("(b e) (c f) -> (e c) b f", b=2, f=P)).then_inc(ld_bias, 16)
            act.dma_start(gdn_mem[:, 2432:2432 + P + 64], d["consts"][:, K_IOTA:K_END]).then_inc(ld_iota, 16)
            empty_T("mixT", 0, xT)
            empty_T("mixT", 2, xT)
            for i in range(3):
                empty_T("x1T", i, xT, (gcol1, bcol1))

            def cross_exp(h):
                act.wait_ge(xsm_in, h + 1)
                for b in range(TB):
                    act.activation(xp[:, h, b, :], bank(f"xs{h}")[:, b * 256:(b + 1) * 256], ACT.Exp, scale=XA_SCALE,
                                   bias=stat_nb[:, 2 * h + b:2 * h + b + 1],
                                   accum_out=stat_l[:, 2 * h + b:2 * h + b + 1]).then_inc(xsm_exp, 1)

            def empty_pT(h):
                empty(f"pT{h}", pT[:, h, :, :], as3(2))

            def empty_oT(h):
                empty(f"oT{h}", oT[:, 2 * h:2 * h + 2, :], as3(2))

            empty("xq0", dqk3[:, 0:2, :], as3(2))
            empty("xq1", dqk3[:, 2:4, :], as3(2))
            cross_exp(0)
            empty("xq2", dqk3[:, 4:6, :], as3(2))
            cross_exp(1)
            empty("xq3", dqk3[:, 6:8, :], as3(2))
            cross_exp(2)
            act.wait_ge(ln_ready, 2)
            load_gains("ln2")
            cross_exp(3)
            act.dma_start(bdown, d["exp_b_down"][0]).then_inc(ld_bdown, 16)
            act.dma_start(dv[:, 0:KC * N_EXPERTS].rearrange("p (k e) -> p k e", k=KC),
                          d["router_w"][0].rearrange("(k p) e -> p k e", p=P)).then_inc(ld_rt, 16)
            empty_vm(2)
            empty_pT(0)
            empty_pT(1)
            empty_vm(3)
            empty_pT(2)
            empty_oT(0)
            empty_oT(1)
            empty_pT(3)
            empty_oT(2)
            empty_oT(3)
            for i in range(3):
                if i == 2:
                    empty("bT", ebias, as3(2))
                empty_T("x2T", i, xT, (gcol2, bcol2))
            act.wait_ge(rt_in, 1)
            act.activation(expl, expl, ACT.Exp).then_inc(rt_exp, 1)
            empty("GT", GT, lambda ps: ps[0:N_EXPERTS, 0:256])
            act.wait_ge(ln_ready, 4)
            load_gains("ln3")
            empty("xg0", xg_sb)

            act.wait_ge(tab_ready, 1)
            blocks = act.value_load(itab[0:1, T_CUM + N_EXPERTS - 1:T_CUM + N_EXPERTS], min_val=N_EXPERTS, max_val=MAX_BLOCKS)
            with act.Fori(0, blocks) as n:
                for f in range(2):
                    act.wait_ge(gu_done, n * 2 + (f + 1))
                    act.activation(gu[:, f, :], moe_bank[f][:, :], ACT.Copy).then_inc(gu_copied, 1)
                act.wait_ge(xg_done, n + 1)
                act.activation(xg_sb, moe_bank[5][:, :], ACT.Copy).then_inc(xg_copied, 1)
                for f in range(2):
                    act.wait_ge(mg_ready, n * 2 + (f + 1))
                    act.activation(sig[:, f, :, :], mg[:, f, :, :], ACT.Sigmoid, scale=SWIGLU_ALPHA).then_inc(sig_ready, 1)
                act.wait_ge(y_done, n + 1)
                act.activation(y_sb, moe_bank[4][:, :], ACT.Copy).then_inc(y_copied, 1)
                act.wait_ge(gselT_done, n + 2)
                act.activation(gselT, moe_bank[7][:, 0:256], ACT.Copy).then_inc(gselT_ready, 1)

        @block.tensor
        def _(pe):
            def begin(name):
                u = UNIT_AT[name]
                if u >= 8:
                    wait_emptied(pe, UNITS[u - 8][0])
                return bank(name)

            def need(*names):
                for name in names:
                    wait_emptied(pe, name)

            def arrived(i):
                pe.wait_ge(ring_full[i % SLOTS], 16 * (i // SLOTS + 1))

            dv_w = ring[:, 0:4096].rearrange("p (k n) -> p k n", k=KC)

            def transpose_block(name, src, chunks):
                ps = begin(name)
                for j, c in enumerate(chunks):
                    last = pe.transpose(ps[:, j * P:(j + 1) * P], src[:, c * P:(c + 1) * P], ident)
                last.then_inc(unit_filled, 1)

            def channel_major(name, w, chunks, src):
                ps = begin(name)
                for j, c in enumerate(chunks):
                    for k in range(KC):
                        last = pe.matmul(ps[:, j * SEQ:(j + 1) * SEQ], w(k)[:, c * P:(c + 1) * P], src[:, k, :],
                                         start=(k == 0), stop=(k == KC - 1))
                last.then_inc(unit_filled, 1)

            def token_major(name, srcT, b, w, col, parts=()):
                ps = begin(name)
                for k in range(KC):
                    if k in dict(parts):
                        need(dict(parts)[k])
                    last = pe.matmul(ps[:, :], srcT[:, k, b * P:(b + 1) * P], w(k)[:, col:col + 512],
                                     start=(k == 0), stop=(k == KC - 1))
                last.then_inc(unit_filled, 1)

            def through(*loads):
                return lambda k: slots[loads[k // 4] % SLOTS][:, k % 4, :]

            def used_up(n, after):
                pe.wait_ge(unit_filled, UNIT_AT[after] + 1)
                pe.sem_inc(ring_used, n)

            pe.wait_ge(ld_const, 16)
            pe.wait_ge(ld_x, 16)
            for i in range(4):
                transpose_block(f"xT{i}", x3[:, i // 2, :], range(4 * (i % 2), 4 * (i % 2) + 4))
            need("xT2", "xT3")
            pe.wait_ge(ld_ba, 48)
            ps = begin("ba")
            for b in range(TB):
                for k in range(KC):
                    last = pe.matmul(ps[:, 8 * b:8 * b + 8], xT[:, k, b * P:(b + 1) * P], dnw_keep[:, 8 * k:8 * k + 8],
                                     start=(k == 0), stop=(k == KC - 1))
            last.then_inc(unit_filled, 1)
            w = through(0, 1)
            arrived(0)
            for i in range(4):
                ps = begin(f"qk{i}")
                for k in range(KC // 2):
                    pe.matmul(ps[:, 0:SEQ], w(k)[:, 2 * i * P:(2 * i + 1) * P], xT[:, k, :], start=(k == 0), stop=False)
            pe.wait_ge(ld_cols, 80)
            ps = begin("columns")
            pe.transpose(ps[:, 0:80], columns_raw, ident[0:80, 0:80]).then_inc(unit_filled, 1)
            arrived(1)
            for i in range(4):
                ps = bank(f"qk{i}")
                for k in range(KC // 2, KC):
                    pe.matmul(ps[:, 0:SEQ], w(k)[:, 2 * i * P:(2 * i + 1) * P], xT[:, k, :], start=False, stop=(k == KC - 1))
                for k in range(KC):
                    last = pe.matmul(ps[:, SEQ:2 * SEQ], w(k)[:, (2 * i + 1) * P:(2 * i + 2) * P], xT[:, k, :],
                                     start=(k == 0), stop=(k == KC - 1))
                last.then_inc(unit_filled, 1)
            arrived(2)
            arrived(3)
            for i in range(2):
                channel_major(f"v{i}", through(2, 3), (2 * i, 2 * i + 1), xT)
            used_up(2, "qk3")
            token_major("z0", xT, 0, through(2, 3), 512)
            pe.wait_ge(gate_step, 2)
            ps = begin("gcum")
            pe.matmul(ps[:, 0:PAIRS], upper, g_log, start=True, stop=True).then_inc(unit_filled, 1)
            for g in range(TB):
                ps = begin(f"R{g}")
                for h in range(HEADS):
                    last = pe.matmul(ps[:, h * P:(h + 1) * P], gB[:, 4 * g + h, :], upper, start=True, stop=True)
                last.then_inc(unit_filled, 1)
            token_major("z1", xT, 1, through(2, 3), 512)
            for i in range(4):
                pe.wait_ge(sq_ready, i + 1)
                ps = begin(f"ss{i}")
                pe.matmul(ps[:, :], ones, sq_mem[:, 512 * i:512 * (i + 1)], start=True, stop=True).then_inc(unit_filled, 1)
            arrived(4)
            arrived(5)

            def dqk_unit(i):
                channel_major(f"dqk{i}", through(4, 5), (2 * i, 2 * i + 1), xT)

            def dv_unit(b):
                token_major(f"dv{b}", xT, b, lambda k: dv_w[:, k, :], 0)

            def km_unit(i):
                channel_major(f"km{i}", through(7, 8), (2 * i, 2 * i + 1), memT)

            def vm_unit(i):
                token_major(f"vm{i}", memT, i // 2, through(11, 12), (i % 2) * HALF)

            def per_head(name, product):
                ps = begin(name)
                for h in range(HEADS):
                    last = product(ps[:, h * P:(h + 1) * P], h)
                last.then_inc(unit_filled, 1)

            dqk_unit(0)
            used_up(2, "z1")
            pe.wait_ge(silu_ready, 6)
            for b in range(TB):
                per_head(f"vtok{b}", lambda o, h: pe.transpose(o, vT[:, h, b * P:(b + 1) * P], ident))
            pe.wait_ge(qk_normed, 4)
            for name, other in (("KK", kn), ("KQ", qn)):
                for b in range(TB):
                    tok = slice(b * P, (b + 1) * P)
                    per_head(f"{name}{b}", lambda o, h: pe.matmul(o, kn[:, h, tok], other[:, h, tok], start=True, stop=True))
            for b in range(TB):
                per_head(f"ktok{b}", lambda o, h: pe.transpose(o, kn[:, h, b * P:(b + 1) * P], ident))
            dqk_unit(1)
            for g in range(TB):
                pe.wait_ge(lmat_ready, g + 1)
                per_head(f"LT{g}", lambda o, h: pe.transpose(o, L[:, 4 * g + h, :], ident))
            dqk_unit(2)

            def scores(h):
                ps2 = [begin(f"sc{h}_0"), begin(f"sc{h}_1")]
                for q, (a, b) in enumerate(((0, P), (P, 3 * P))):
                    for c in range(2):
                        rows = slice(DIFF_D * c, DIFF_D * (c + 1))
                        last = pe.matmul(ps2[c][:, a:b], dqk3[rows, h, q * P:(q + 1) * P], dqk3[rows, 4 + h, 0:b - a],
                                         start=True, stop=True)
                        if q == 1:
                            last.then_inc(unit_filled, 1)

            def attention_T(h):
                pe.wait_ge(a_ready, h + 1)
                ps = begin(f"aT{h}")
                for j in range(3):
                    last = pe.transpose(ps[:, j * P:(j + 1) * P], dp[h % 2][:, 0, j * P:(j + 1) * P], ident)
                last.then_inc(unit_filled, 1)

            pe.wait_ge(x_init, 1)
            pe.wait_ge(xt_init, 1)
            for level in range(1, LEVELS):
                pe.wait_ge(bt_ready, level)
                for g in range(TB):
                    if level > 1:
                        need(f"X{level - 1}_{g}", f"XT{level - 1}_{g}")
                    per_head(f"M{level}_{g}", lambda o, h: pe.matmul(o, BT[:, 4 * g + h, :], X[:, 4 * g + h, :],
                                                                   start=True, stop=True))
                for g in range(TB):
                    need(f"M{level}_{g}")
                    if level < LEVELS - 1:
                        per_head(f"X{level}_{g}", lambda o, h: pe.matmul(o, XT[:, 4 * g + h, :], M1[:, 4 * g + h, :],
                                                                       start=True, stop=True))
                    per_head(f"XT{level}_{g}", lambda o, h: pe.matmul(o, M1[:, 4 * g + h, :], XT[:, 4 * g + h, :],
                                                                    start=True, stop=True))
                if level == 1:
                    dqk_unit(3)
                elif level == 2:
                    arrived(6)
                    dv_unit(0)
                    used_up(2, "dqk3")
                elif level == 3:
                    dv_unit(1)
                    pe.wait_ge(ld_mem, 16)
                    for i in range(4):
                        transpose_block(f"memT{i}", mem3[:, i // 2, :], range(4 * (i % 2), 4 * (i % 2) + 4))
                else:
                    if level == 4:
                        need("memT3", "dqk3")
                        used_up(1, "dv1")
                        arrived(7)
                        arrived(8)
                    scores(level - 4)
                    if level > 4:
                        attention_T(level - 5)
                    km_unit(level - 4)

            for g in range(TB):
                need(f"XT{LEVELS - 1}_{g}")
                per_head(f"U{g}", lambda o, h: pe.matmul(o, XT[:, 4 * g + h, :], vbeta[:, 4 * g + h, :], start=True, stop=True))
            per_head("WT", lambda o, h: pe.matmul(o, kbg[:, 4 + h, :], XT[:, 4 + h, :], start=True, stop=True))
            scores(3)
            need("U0")
            per_head("S", lambda o, h: pe.matmul(o, ktail[:, h, :], u_sb[:, h, :], start=True, stop=True))
            per_head("O0", lambda o, h: pe.matmul(o, AT[:, h, :], u_sb[:, h, :], start=True, stop=True))
            attention_T(2)
            need("WT", "S")
            per_head("WS", lambda o, h: pe.matmul(o, wT[:, h, :], S_sb[:, h, :], start=True, stop=True))
            km_unit(3)
            pe.wait_ge(vnew_ready, 1)
            ps = begin("O1")
            for h in range(HEADS):
                pe.matmul(ps[:, h * P:(h + 1) * P], qd[:, h, :], S_sb[:, h, :], start=True, stop=False)
                last = pe.matmul(ps[:, h * P:(h + 1) * P], AT[:, 4 + h, :], vnew[:, h, :], start=False, stop=True)
            last.then_inc(unit_filled, 1)
            attention_T(3)
            used_up(2, "km3")
            arrived(11)
            arrived(12)
            vm_unit(0)
            need("aT3", "dv1")
            per_head("OD0", lambda o, h: pe.matmul(o, aT[:, h, 0:P], dv3[:, 0, h * P:(h + 1) * P], start=True, stop=True))
            ps = begin("OD1")
            for h in range(HEADS):
                for j in range(2):
                    last = pe.matmul(ps[:, h * P:(h + 1) * P], aT[:, h, (1 + j) * P:(2 + j) * P], dv3[:, j, h * P:(h + 1) * P],
                                     start=(j == 0), stop=(j == 1))
            last.then_inc(unit_filled, 1)
            vm_unit(1)

            def tokens_T(name, i, src):
                transpose_block(f"{name}{i}", src[:, i // 2, :], range(4 * (i % 2), 4 * (i % 2) + 4))

            pe.wait_ge(mix_ready, 4)
            for i in range(4):
                tokens_T("mixT", i, mem3)
            arrived(9)
            arrived(10)
            for i in range(4):
                if i == 3:
                    pe.wait_ge(ln_applied, 1)
                    tokens_T("x1T", 0, x3)
                    tokens_T("x1T", 1, x3)
                b = i // 2
                token_major(f"h{i}", xT, b, through(9, 10), (i % 2) * HALF, ((0, f"mixT{2 * b}"), (4, f"mixT{2 * b + 1}")))
            def xq_part(i, b):
                w = through(13, 14)
                ps = bank(f"xq{i}")
                for j in range(2):
                    for k in range(KC):
                        last = pe.matmul(ps[:, j * SEQ + b * P:j * SEQ + (b + 1) * P], w(k)[:, (2 * i + j) * P:(2 * i + j + 1) * P],
                                         xT[:, k, b * P:(b + 1) * P], start=(k == 0), stop=(k == KC - 1))
                return last

            def cross_scores(h):
                need(f"xq{h}")
                ps = begin(f"xs{h}")
                for b in range(TB):
                    for j in range(2):
                        last = pe.matmul(ps[:, b * 256:(b + 1) * 256], dqk3[:, 2 * h + j, b * P:(b + 1) * P], km3[:, 2 * h + j, :],
                                         start=(j == 0), stop=(j == 1))
                last.then_inc(unit_filled, 1)

            need("x1T1")
            arrived(13)
            arrived(14)
            for i in range(2):
                begin(f"xq{i}")
                xq_part(i, 0)
            used_up(2, "h3")
            pe.wait_ge(ln_applied, 2)
            tokens_T("x1T", 2, x3)
            tokens_T("x1T", 3, x3)
            begin("xq2")
            xq_part(2, 0)
            need("x1T2", "x1T3", "km3")
            xq_part(0, 1).then_inc(unit_filled, 1)
            xq_part(1, 1).then_inc(unit_filled, 1)
            cross_scores(0)
            xq_part(2, 1).then_inc(unit_filled, 1)
            cross_scores(1)
            channel_major("xq3", through(13, 14), (6, 7), xT)
            cross_scores(2)
            cross_scores(3)
            vm_unit(2)

            def probs_T(h):
                pe.wait_ge(xp_ready, h + 1)
                ps = begin(f"pT{h}")
                for m in range(2):
                    for b in range(TB):
                        last = pe.transpose(ps[:, (2 * m + b) * P:(2 * m + b + 1) * P], xp[:, h, b, m * P:(m + 1) * P], ident)
                last.then_inc(unit_filled, 1)

            def cross_out(h):
                need(f"pT{h}")
                if h == 0:
                    need("vm3")
                ps = begin(f"oT{h}")
                for j in range(2):
                    for m in range(2):
                        c = 2 * h + j
                        last = pe.matmul(ps[:, j * SEQ:(j + 1) * SEQ], vm3[:, m, c * P:(c + 1) * P], pT[:, h, m, :],
                                         start=(m == 0), stop=(m == 1))
                last.then_inc(unit_filled, 1)

            probs_T(0)
            probs_T(1)
            vm_unit(3)
            used_up(4, "vm3")
            probs_T(2)
            cross_out(0)
            cross_out(1)
            probs_T(3)
            cross_out(2)
            cross_out(3)
            arrived(15)
            arrived(16)
            for i in range(4):
                if i == 3:
                    pe.wait_ge(ln_applied, 3)
                    tokens_T("x2T", 0, x3)
                    tokens_T("x2T", 1, x3)
                token_major(f"wo{i}", oT, i // 2, through(15, 16), (i % 2) * HALF, ((0, "oT2"), (6, "oT3")))
            pe.wait_ge(ld_bias, 32)
            ps = begin("bT")
            for w in range(2):
                for b in range(2):
                    last = pe.transpose(ps[:, (2 * w + b) * P:(2 * w + b + 1) * P], bias_raw[:, w, b, :], ident)
            last.then_inc(unit_filled, 1)
            pe.wait_ge(ld_rt, 32)
            router_ps = begin("router")

            def route_block(b, parts=()):
                for k in range(KC):
                    if k in dict(parts):
                        need(dict(parts)[k])
                    last = pe.matmul(router_ps[:, 32 * b:32 * b + 32], xT[:, k, b * P:(b + 1) * P], dv[:, 32 * k:32 * k + 32],
                                     start=(k == 0), stop=(k == KC - 1))
                return last

            need("x2T1")
            route_block(0)
            used_up(2, "wo3")
            pe.wait_ge(ln_applied, 4)
            tokens_T("x2T", 2, x3)
            tokens_T("x2T", 3, x3)
            route_block(1, ((0, "x2T2"), (4, "x2T3"))).then_inc(unit_filled, 1)
            pe.wait_ge(route_ready, 1)
            ps = begin("pos")
            pe.matmul(ps[:, 0:32], strict, M[:, 0:32], start=True, stop=True)
            pe.matmul(ps[:, 32:64], strict, M[:, 32:64], start=True, stop=False)
            pe.matmul(ps[:, 32:64], ones, M[:, 0:32], start=False, stop=True)
            pe.matmul(ps[0:32, 64:65], M[:, 0:32], ones[:, 0:1], start=True, stop=False)
            pe.matmul(ps[0:32, 64:65], M[:, 32:64], ones[:, 0:1], start=False, stop=True).then_inc(unit_filled, 1)

            pe.wait_ge(route_ready, 2)
            ps = begin("GT")
            for b in range(TB):
                last = pe.transpose(ps[0:32, b * P:(b + 1) * P], G[:, 32 * b:32 * b + 32], ident)
            last.then_inc(unit_filled, 1)
            need("GT")
            pe.wait_ge(ld_bdown, 16)

            def gated_bias(i):
                pe.matmul(begin(f"eb{i}")[:, :], GT[:, (i // 2) * P:(i // 2 + 1) * P],
                          bdown[:, (i % 2) * HALF:(i % 2 + 1) * HALF], start=True, stop=True).then_inc(unit_filled, 1)

            gated_bias(0)

            def gather(ps):
                for b in range(TB):
                    for h in range(2):
                        last = pe.matmul(ps[64 * h:64 * h + 64, :], selw[:, b, 0:CAP], x3[:, b, h * HALF:(h + 1) * HALF],
                                         start=(b == 0), stop=(b == 1))
                return last

            def gathered_T(ps):
                for j in range(4):
                    last = pe.transpose(ps[:, j * P:(j + 1) * P], xg_sb[:, j * P:(j + 1) * P], ident)
                return last

            pe.wait_ge(ln_ready, 4)
            pe.wait_ge(sel_ready, 1)
            gather(begin("xg0")).then_inc(unit_filled, 1)
            pe.wait_ge(cnt_ready, 1)
            ps = begin("cum")
            pe.matmul(ps[0:32, 0:1], upper[0:32, 0:32], nblk[0:32, 0:1], start=True, stop=True)
            pe.matmul(ps[0:1, 32:64], nblk[0:32, 0:1], upper[0:32, 0:32], start=True, stop=True).then_inc(unit_filled, 1)
            gated_bias(1)
            need("xg0")
            gathered_T(begin("xgT0")).then_inc(unit_filled, 1)
            pe.wait_ge(cnt_ready, 2)
            ps = begin("etab")
            pe.matmul(ps[0:1, 0:64], ones[0:32, 0:1], emask, start=True, stop=True).then_inc(unit_filled, 1)
            gated_bias(2)
            gated_bias(3)

            def xg_chunk(k):
                return xgT[:, k % 4, 64 * (k // 4):64 * (k // 4) + 64]

            def scatter():
                for b, targets in enumerate(((7, 5), (0, 1))):
                    for h in range(2):
                        last = pe.matmul(moe_bank[targets[h]][:, :], gselT[64 * h:64 * h + 64, b * P:(b + 1) * P],
                                         y_sb[64 * h:64 * h + 64, :], start=True, stop=True)
                    last.then_inc(scat_done, 1)

            need("xg0", "cum")
            pe.sem_inc(gselT_done, 1)
            pe.wait_ge(tab_ready, 1)
            blocks = pe.value_load(itab[0:1, T_CUM + N_EXPERTS - 1:T_CUM + N_EXPERTS], min_val=N_EXPERTS, max_val=MAX_BLOCKS)
            with pe.Fori(0, blocks) as n:
                e = pe.value_load(itab[0:1, bass.ds(n + T_E, 1)], min_val=0, max_val=N_EXPERTS - 1)
                parity = pe.to_reg(e % 2)

                def work(odd):
                    def arrived(role):
                        if role not in TWO_SLOT_ROLES:
                            pe.wait_ge(ring_full[ROLE_SLOT[role]], e * 16 + 16 * (ROLE_EARLIER[role] + 1))
                        elif odd:
                            pe.wait_ge(odd_full[role], e * 8 + 8)
                        else:
                            pe.wait_ge(ring_full[ROLE_SLOT[role]], e * 8 + 16 * (ROLE_EARLIER[role] + 1))

                    def weights(role, k, half):
                        at = weights_at(role, odd) + (k % 4) * D_MODEL + half * HALF
                        return main[:, at:at + HALF]

                    def gate_up(f, k):
                        for side, role in ((0, (G0, G1)[k // 4]), (1, (U0, U1)[k // 4])):
                            last = pe.matmul(moe_bank[f][64 * side:64 * side + 64, :], xg_chunk(k), weights(role, k, f),
                                             start=(k == 0), stop=(k == KC - 1))
                        return last

                    arrived(G0)
                    arrived(U0)
                    for k in range(4):
                        for f in range(2):
                            last = gate_up(f, k)
                    last.then_inc(gu0_used, 1)
                    arrived(G1)
                    arrived(U1)
                    for f in range(2):
                        for k in range(4, KC):
                            last = gate_up(f, k)
                        last.then_inc(gu_done, 1)
                    pe.wait_ge(sel_ready, n + 2)
                    pe.wait_ge(acc_done, n + 1)
                    gather(moe_bank[5]).then_inc(xg_done, 1)
                    for f in range(2):
                        pe.wait_ge(gu_copied, n * 2 + (f + 1))
                        for j in range(4):
                            last = pe.transpose(moe_bank[2 + f][:, j * P:(j + 1) * P], gu[:, f, j * P:(j + 1) * P], ident)
                        last.then_inc(guT_done, 1)
                    pe.wait_ge(xg_copied, n + 1)
                    gathered_T(moe_bank[6]).then_inc(xgT_done, 1)
                    pe.wait_ge(y_copied, n + 1)
                    pe.wait_ge(gselT_ready, n + 1)
                    scatter()
                    for f, role in enumerate((D0, D1)):
                        arrived(role)
                        pe.wait_ge(hT_ready, n * 2 + (f + 1))
                        for k in range(4 * f, 4 * f + 4):
                            for h in range(2):
                                last = pe.matmul(moe_bank[4][64 * h:64 * h + 64, :], hT[:, k, :], weights(role, k, h),
                                                 start=(k == 0), stop=(k == KC - 1))
                        last.then_inc((d0_used, y_done)[f], 1)
                    pe.wait_ge(acc_done, n + 2)
                    pe.wait_ge(gsel_ready, n + 1)
                    for b in range(TB):
                        last = pe.transpose(moe_bank[7][:, b * P:(b + 1) * P], gsel[:, b, :], ident)
                    last.then_inc(gselT_done, 1)

                pe.wait_ge(xgT_ready, n + 1)
                with pe.If_eq(parity, 0):
                    work(odd=False)
                with pe.If_ne(parity, 0):
                    work(odd=True)
            pe.wait_ge(y_copied, blocks + 1)
            pe.wait_ge(gselT_ready, blocks + 1)
            scatter()

        @block.vector
        def _(dve):
            tt, ts, stt = dve.tensor_tensor, dve.tensor_scalar, dve.scalar_tensor_tensor

            def filled(name):
                dve.wait_ge(unit_filled, UNIT_AT[name] + 1)
                return bank(name)

            def as3(ps, n):
                return ps[:, :].rearrange("p (g s) -> p g s", g=n)

            for i in range(4):
                dve.tensor_copy(xT[:, 4 * (i % 2):4 * (i % 2) + 4, (i // 2) * P:(i // 2 + 1) * P], as3(filled(f"xT{i}"), 4)).then_inc(dve_emptied, 1)
            ps = filled("ba")
            dve.tensor_copy(ba, ps[:, 0:16]).then_inc(dve_emptied, 1)
            dve.tensor_copy(columns, filled("columns")[:, 0:80]).then_inc(dve_emptied, 1)
            dve.drain()
            ba3 = ba.rearrange("p (b n) -> p b n", b=2)
            dt3 = dt_b.unsqueeze(1).broadcast_to([P, 2, 4])
            s3 = [v.rearrange("p (b n) -> p b n", b=2) for v in (sp_a, sp_b, sp_c)]
            dve.tensor_copy(s3[0], ba3[:, :, 0:4])
            tt(s3[2], ba3[:, :, 4:8], dt3, ALU.add)
            dve.drain()
            stt(sp_b, sp_c, -1.0, sp_c, ALU.mult, ALU.max).then_inc(gate_step, 1)
            ts(sp_c, sp_c, 0.0, None, ALU.max)
            dve.drain()
            dve.wait_ge(exp_ready, 4)
            ts(beta, sp_a, 1.0, None, ALU.add)
            tt(sp_c, sp_c, sp_b, ALU.add)
            dve.drain()
            dve.reciprocal(beta, beta)
            tt(s3[2], s3[2], a_log.unsqueeze(1).broadcast_to([P, 2, 4]), ALU.mult)
            dve.drain()
            ts(g_log, sp_c, -1.0, None, ALU.mult)
            dve.drain()
            dve.tensor_copy(gB, row_b(g_log, PAIRS, P))
            dve.drain()
            dve.sem_inc(gate_step, 1)

            names = {0: "qk0", 1: "qk1", 2: "qk2", 3: "qk3", 4: "v0", 5: "v1"}
            dve.wait_ge(pad_zero, 1)
            for j in range(6):
                wait_emptied(dve, names[j])
                for tap in range(GDN_TAPS):
                    for c in (2 * j, 2 * j + 1):
                        w = convw[:, 12 * tap + c:12 * tap + c + 1]
                        if tap == 0:
                            last = ts(cout[:, c, :], cin[:, c, 0:SEQ], w, None, ALU.mult)
                        else:
                            last = stt(cout[:, c, :], cin[:, c, tap:tap + SEQ], w, cout[:, c, :], ALU.mult, ALU.add)
                    if tap < GDN_TAPS - 1:
                        dve.drain()
                last.then_inc(conv_ready, 1)

            dve.wait_ge(ld_vec, 16 * 6)
            for i in range(2):
                tt(lam_raw[:, 128 * i:128 * i + 64], lam_raw[:, 128 * i:128 * i + 64], lam_raw[:, 128 * i + 64:128 * i + 128], ALU.mult)
            dve.drain()
            for i in range(2):
                dve.reduce_sum(lamv[:, i:i + 1], lam_raw[:, 128 * i:128 * i + 64], AX_X)
            dve.drain()
            dve.sem_inc(lam_in, 1)
            ts(dnw_keep[:, :], dnw, 1.0 - LAMBDA_INIT, None, ALU.mult)

            dve.tensor_copy(gcum, filled("gcum")[:, 0:PAIRS]).then_inc(dve_emptied, 1)
            dve.drain()
            dve.sem_inc(gate_step, 1)
            for g in range(TB):
                ps = as3(filled(f"R{g}"), 4)
                if g == 0:
                    tt(tails[:, 0:4], ps[:, :, P - 1:P].rearrange("p g s -> p (g s)"), gcum[:, 0:4], ALU.subtract)
                else:
                    dve.tensor_copy(qd, ps).then_inc(qd_in, 1)
                tt(diff[:, 4 * g:4 * g + 4, :], ps, row_b(gcum[:, 4 * g:4 * g + 4], 4, P), ALU.subtract).then_inc(dve_emptied, 1)
            dve.drain()
            dve.sem_inc(dec_in, 1)
            ts(Dm, diff, 0.0, None, ALU.max).then_inc(dec_in, 1)
            ts(DT, diff, 0.0, None, ALU.min).then_inc(dec_in, 1)
            wait_emptied(dve, "z1")
            tt(sz[:, :].rearrange("p (g s) -> p g s", g=PAIRS), sz[:, :].rearrange("p (g s) -> p g s", g=PAIRS),
               tile_b(gnw, PAIRS, P), ALU.mult)
            for i in range(4):
                dve.wait_ge(l2_exp, i + 1)
                part = conv_out[:, 512 * i:512 * (i + 1)]
                stt(part, part, GDN_DK ** -0.5 if i < 2 else 1.0, sq_mem[:, 512 * i:512 * (i + 1)],
                    ALU.mult, ALU.mult).then_inc(qk_normed, 1)
            dve.wait_ge(qd_exp, 1)
            dve.drain()
            tt(qd, qd, qn[:, :, P:SEQ], ALU.mult)
            dve.wait_ge(exp_ready, 6)
            tt(begs, beta, eg, ALU.mult)
            for g in range(TB):
                tt(vbeta[:, 4 * g:4 * g + 4, :], as3(filled(f"vtok{g}"), 4), row_b(beta[:, 4 * g:4 * g + 4], 4, P),
                   ALU.mult).then_inc(dve_emptied, 1)
            dve.wait_ge(dec_ready, 1)
            for g in range(TB):
                ps = as3(filled(f"KK{g}"), 4)
                for h in range(HEADS):
                    i = 4 * g + h
                    last = stt(L[:, i, :], ps[:, h, :], beta[:, i:i + 1], Dm[:, i, :], ALU.mult, ALU.mult)
                dve.drain()
                dve.sem_inc(dve_emptied, 1)
                dve.sem_inc(lmat_ready, 1)
            dve.wait_ge(dec_ready, 2)
            for g in range(TB):
                tt(AT[:, 4 * g:4 * g + 4, :], as3(filled(f"KQ{g}"), 4), DT[:, 4 * g:4 * g + 4, :], ALU.mult).then_inc(dve_emptied, 1)
            ps = as3(filled("ktok0"), 4)
            tt(ktail, ps, row_b(tails[:, 0:4], 4, P), ALU.mult)
            tt(kbg[:, 0:4, :], ps, row_b(begs[:, 0:4], 4, P), ALU.mult).then_inc(dve_emptied, 1)
            tt(kbg[:, 4:8, :], as3(filled("ktok1"), 4), row_b(begs[:, 4:8], 4, P), ALU.mult).then_inc(dve_emptied, 1)
            dve.wait_ge(ld_lev, 16)
            tt(X, L, tile_b(lev0, PAIRS, P), ALU.mult)
            dve.drain()
            tt(X, tile_b(ident, PAIRS, P), X, ALU.subtract).then_inc(x_init, 1)
            dve.wait_ge(xt_init, 1)
            dve.drain()
            dve.wait_ge(lam_exp, 1)
            tt(neglam, lamv[:, 1:2], lamv[:, 0:1], ALU.subtract)
            dve.drain()
            ts(neglam, neglam, LAMBDA_INIT, None, ALU.subtract)
            def shifted(h, c):
                if h >= 2:
                    dve.wait_ge(unit_filled, UNIT_AT[f"aT{h - 2}"] + 1)
                s = 4 * (h % 2) + 2 * c
                ps = filled(f"sc{h}_{c}")
                p = dp[h % 2][:, c, :]
                tt(p, ps[:, 0:384], causal, ALU.add).then_inc(dve_emptied, 1)
                dve.drain()
                dve.reduce_max(stat_mx[:, s:s + 1], p[:, 0:P], AX_X)
                dve.reduce_max(stat_mx[:, s + 1:s + 2], p[:, P:384], AX_X)
                dve.drain()
                ts(stat_nb[:, s:s + 2], stat_mx[:, s:s + 2], -DIFF_SCALE, None, ALU.mult).then_inc(sm_in, 1)

            def combine(h):
                dve.wait_ge(sm_exp, 4 * h + 4)
                s = 4 * (h % 2)
                dve.reciprocal(stat_r[:, s:s + 4], stat_l[:, s:s + 4])
                dve.drain()
                ts(stat_r[:, s + 2:s + 4], stat_r[:, s + 2:s + 4], neglam, None, ALU.mult)
                for q, (a, b) in enumerate(((0, P), (P, 384))):
                    ts(dp[h % 2][:, 0, a:b], dp[h % 2][:, 0, a:b], stat_r[:, s + q:s + q + 1], None, ALU.mult)
                dve.drain()
                for q, (a, b) in enumerate(((0, P), (P, 384))):
                    last = stt(dp[h % 2][:, 0, a:b], dp[h % 2][:, 1, a:b], stat_r[:, s + 2 + q:s + 3 + q], dp[h % 2][:, 0, a:b],
                               ALU.mult, ALU.add)
                last.then_inc(a_ready, 1)

            for level in range(1, LEVELS):
                for g in range(TB):
                    gs = slice(4 * g, 4 * g + 4)
                    if level < LEVELS - 1:
                        ps = as3(filled(f"X{level}_{g}"), 4)
                        tt(X[:, gs, :], X[:, gs, :], ps, ALU.subtract).then_inc(dve_emptied, 1)
                    ps = as3(filled(f"XT{level}_{g}"), 4)
                    tt(XT[:, gs, :], XT[:, gs, :], ps, ALU.subtract).then_inc(dve_emptied, 1)
                dve.drain()
                if level >= 4:
                    if level > 4:
                        combine(level - 5)
                    shifted(level - 4, 0)
                    shifted(level - 4, 1)

            roots = [0]

            def mean_square(i):
                part = rs16[:, 4 * i:4 * i + 4]
                ts(part, part, 1.0 / P, RMS_EPS, ALU.mult, ALU.add).then_inc(var_in, 1)
                roots[0] += 1

            def normed(src, i, b, col, weights):
                dve.wait_ge(var_out, i + 1)
                for h in range(HEADS):
                    last = stt(mem3[:, b, col + h * P:col + (h + 1) * P], src[:, h * P:(h + 1) * P],
                               rs16[:, 4 * i + h:4 * i + h + 1], weights(h), ALU.mult, ALU.mult)
                last.then_inc(mix_ready, 1)

            def gate(b):
                return lambda h: sz3[:, b, h * P:(h + 1) * P]

            combine(2)
            shifted(3, 0)
            shifted(3, 1)
            ps = as3(filled("WS"), 4)
            wait_emptied(dve, "U1")
            tt(vnew, u_sb[:, 4:8, :], ps, ALU.subtract).then_inc(vnew_ready, 1)
            dve.drain()
            dve.sem_inc(dve_emptied, 1)
            combine(3)
            wait_emptied(dve, "O0")
            mean_square(0)
            wait_emptied(dve, "O1")
            mean_square(1)
            wait_emptied(dve, "OD0")
            mean_square(2)
            wait_emptied(dve, "OD1")
            mean_square(3)
            normed(o_flat[:, 0:512], 0, 0, 0, gate(0))
            normed(o_flat[:, 512:1024], 1, 1, 0, gate(1))
            normed(od_sb[:, 0:512], 2, 0, 512, lambda h: dnw_keep[:, :])
            normed(od_sb[:, 512:1024], 3, 1, 512, lambda h: dnw_keep[:, :])

            bn3 = bn.rearrange("p (a s) -> p a s", a=2)

            def standardise(b):
                xb = x3[:, b, :]
                dve.drain()
                dve.bn_aggr(mv, bn3)
                dve.drain()
                ts(rstd, mv[:, 1:2], LN_EPS, None, ALU.add).then_inc(var_in, 1)
                roots[0] += 1
                dve.wait_ge(var_out, roots[0])
                return ts(xb, xb, mv[:, 0:1], rstd, ALU.subtract, ALU.mult)

            def residual(name, b, h):
                part = x3[:, b, h * HALF:(h + 1) * HALF]
                stt(part, part, ALPHA, filled(name)[:, :], ALU.mult, ALU.add).then_inc(dve_emptied, 1)
                dve.drain()
                dve.bn_stats(bn3[:, h, :], part)

            def gains(b, loads):
                dve.wait_ge(ld_ln, loads)
                dve.drain()
                tt(x3[:, b, :], x3[:, b, :], ln_g, ALU.mult)
                dve.drain()
                return tt(x3[:, b, :], x3[:, b, :], ln_b, ALU.add)

            def norm_both(unit, transposed, loads):
                for b in range(TB):
                    residual(f"{unit}{2 * b}", b, 0)
                    residual(f"{unit}{2 * b + 1}", b, 1)
                    standardise(b).then_inc(ln_applied, 1)
                    if b == 0:
                        dve.wait_ge(unit_filled, UNIT_AT[transposed + "1"] + 1)
                        gains(0, loads).then_inc(ln_ready, 1)

            def empty_T(name, gains):
                ps = filled(name)
                for j in range(4):
                    k = 4 + j
                    last = ts(xT[:, k, P:2 * P], ps[:, j * P:(j + 1) * P], gains[0][:, k:k + 1], gains[1][:, k:k + 1],
                              ALU.mult, ALU.add)
                last.then_inc(dve_emptied, 1)

            for b in range(TB):
                dve.tensor_copy(xT[:, 4:8, b * P:(b + 1) * P], as3(filled(f"mixT{2 * b + 1}"), 4)).then_inc(dve_emptied, 1)
            norm_both("h", "x1T", 32)
            empty_T("x1T3", (gcol1, bcol1))

            def cross_probs(h):
                dve.wait_ge(xsm_exp, 2 * h + 2)
                dve.sem_inc(dve_emptied, 1)
                dve.reciprocal(stat_r[:, 2 * h:2 * h + 2], stat_l[:, 2 * h:2 * h + 2])
                dve.drain()
                tt(xp[:, h, :, :], xp[:, h, :, :], row_b(stat_r[:, 2 * h:2 * h + 2], 2, 256), ALU.mult).then_inc(xp_ready, 1)

            for h in range(HEADS):
                if h > 0:
                    cross_probs(h - 1)
                ps = as3(filled(f"xs{h}"), 2)
                dve.reduce_max(stat_mx[:, 2 * h:2 * h + 2], ps, AX_X)
                dve.drain()
                ts(stat_nb[:, 2 * h:2 * h + 2], stat_mx[:, 2 * h:2 * h + 2], -XA_SCALE, None, ALU.mult).then_inc(xsm_in, 1)
            cross_probs(HEADS - 1)
            dve.wait_ge(ln_ready, 2)
            norm_both("wo", "x2T", 64)
            empty_T("x2T3", (gcol2, bcol2))

            ps = filled("router")
            l3, e3, M3, G3 = (v.rearrange("p (b n) -> p b n", b=2) for v in (logit, expl, M, G))
            tt(l3, ps[:, 0:64].rearrange("p (b n) -> p b n", b=2), rb.unsqueeze(1).broadcast_to([P, 2, 32]), ALU.add)\
                .then_inc(dve_emptied, 1)
            dve.drain()
            for b in range(TB):
                dve.max(top8[:, 8 * b:8 * b + 8], l3[:, b, :])
            dve.drain()
            for b in range(TB):
                ts(e3[:, b, :], l3[:, b, :], top8[:, 8 * b:8 * b + 1], None, ALU.subtract)
            dve.drain()
            dve.sem_inc(rt_in, 1)
            t8 = top8.rearrange("p (b n) -> p b n", b=2)
            dve.memset(t8[:, :, TOP_K:8], NEG)
            dve.drain()
            for b in range(TB):
                dve.match_replace(M3[:, b, :], t8[:, b, :], l3[:, b, :], NEG)
            dve.drain()
            ts(M, M, NEG, None, ALU.is_equal).then_inc(route_ready, 1)
            dve.wait_ge(rt_exp, 1)
            dve.drain()
            tt(G, expl, M, ALU.mult)
            dve.drain()
            dve.tensor_reduce(gsum, G3, AX_X, ALU.add)
            dve.drain()
            dve.reciprocal(gsum, gsum)
            dve.drain()
            tt(G3, G3, gsum.unsqueeze(2).broadcast_to([P, 2, 32]), ALU.mult)
            dve.drain()
            dve.sem_inc(route_ready, 1)
            dve.wait_ge(ld_iota, 16)
            ps = filled("pos")
            dve.tensor_copy(pos, ps[:, 0:64])
            dve.tensor_copy(cumc[0:32, 0:1], ps[0:32, 64:65])
            dve.drain()
            dve.sem_inc(dve_emptied, 1)
            M2, pos2, G2 = M3, pos.rearrange("p (b n) -> p b n", b=2), G3

            def select(e):
                for b in range(TB):
                    ts(selw[:, b, :], iota2, pos2[:, b, bass.ds(e, 1)], M2[:, b, bass.ds(e, 1)], ALU.is_equal, ALU.mult)
                dve.drain()
                for b in range(TB):
                    last = ts(pos2[:, b, bass.ds(e, 1)], pos2[:, b, bass.ds(e, 1)], float(CAP), None, ALU.subtract)
                last.then_inc(sel_ready, 1)

            select(0)
            ts(nblk[0:32, 0:1], cumc[0:32, 0:1], float(CAP), 1.0, ALU.is_gt, ALU.add)
            for r in range(2, SEQ // CAP):
                dve.drain()
                stt(nblk[0:32, 0:1], cumc[0:32, 0:1], float(r * CAP), nblk[0:32, 0:1], ALU.is_gt, ALU.add)
            dve.drain()
            dve.sem_inc(cnt_ready, 1)
            ps = filled("cum")
            dve.tensor_copy(cumc[0:32, 1:2], ps[0:32, 0:1])
            dve.tensor_copy(itab[0:1, T_CUM:T_CUM + 32], ps[0:1, 32:64])
            dve.drain()
            dve.sem_inc(dve_emptied, 1)
            ts(emask, niota[0:32, :], cumc[0:32, 1:2], None, ALU.is_ge).then_inc(cnt_ready, 1)
            dve.tensor_copy(xgT, filled("xgT0")[:, :].rearrange("p (k s) -> p k s", k=4)).then_inc(dve_emptied, 1)
            ps = filled("etab")
            ts(erow, ps[0:1, 0:64], float(N_EXPERTS - 1), None, ALU.min).then_inc(dve_emptied, 1)
            dve.drain()
            dve.tensor_copy(itab[0:1, T_E:T_E + 64], erow)
            dve.drain()
            dve.sem_inc(tab_ready, 1)
            dve.sem_inc(xgT_ready, 1)
            for i in range(4):
                b, cols = i // 2, slice((i % 2) * HALF, (i % 2 + 1) * HALF)
                last = stt(yacc[:, b, cols], x3[:, b, cols], ALPHA, filled(f"eb{i}")[:, :], ALU.mult, ALU.add)
                last.then_inc(dve_emptied, 1)
            dve.drain()
            dve.sem_inc(acc_done, 1)

            def copy_xgT():
                dve.tensor_copy(xgT, moe_bank[6][:, :].rearrange("p (k s) -> p k s", k=4)).then_inc(xgT_ready, 1)

            def accumulate(b):
                for h in range(2):
                    part = yacc[:, b, h * HALF:(h + 1) * HALF]
                    last = tt(part, part, moe_bank[((7, 5), (0, 1))[b][h]][:, :], ALU.add)
                return last

            blocks = dve.value_load(itab[0:1, T_CUM + N_EXPERTS - 1:T_CUM + N_EXPERTS], min_val=N_EXPERTS, max_val=MAX_BLOCKS)
            with dve.Fori(0, blocks) as n:
                e = dve.value_load(itab[0:1, bass.ds(n + T_E, 1)], min_val=0, max_val=N_EXPERTS - 1)
                e_next = dve.value_load(itab[0:1, bass.ds(n + (T_E + 1), 1)], min_val=0, max_val=N_EXPERTS - 1)
                dve.drain()
                dve.wait_ge(gselT_done, n + 1)
                for b in range(TB):
                    last = ts(gsel[:, b, :], selw[:, b, :], G2[:, b, bass.ds(e, 1)], None, ALU.mult)
                last.then_inc(gsel_ready, 1)
                dve.drain()
                select(e_next)
                bias4 = [ebias[:, w, :].rearrange("p (e k) -> p e k", k=KC) for w in range(2)]
                for f in range(2):
                    dve.wait_ge(guT_done, n * 2 + (f + 1))
                    gT = moe_bank[2 + f][:, :].rearrange("p (k g s) -> p k g s", k=4, g=2)

                    def bias(w):
                        b = bias4[w][:, bass.ds(e, 1), 4 * f:4 * f + 4].rearrange("p e k -> p (e k)")
                        return b.unsqueeze(2).broadcast_to([P, 4, CAP])

                    tt(mg[:, f, :, :], gT[:, :, 0, :], bias(0), ALU.add)
                    tt(mu[:, f, :, :], gT[:, :, 1, :], bias(1), ALU.add)
                    dve.drain()
                    ts(mg[:, f, :, :], mg[:, f, :, :], SWIGLU_LIMIT, None, ALU.min).then_inc(mg_ready, 1)
                    ts(mu[:, f, :, :], mu[:, f, :, :], SWIGLU_LIMIT, -SWIGLU_LIMIT, ALU.min, ALU.max)
                    dve.drain()
                    stt(tmp[:, f, :, :], mu[:, f, :, :], 1.0, mg[:, f, :, :], ALU.add, ALU.mult)
                dve.drain()
                for f in range(2):
                    dve.wait_ge(sig_ready, n * 2 + (f + 1))
                    tt(hT[:, 4 * f:4 * f + 4, :], tmp[:, f, :, :], sig[:, f, :, :], ALU.mult).then_inc(hT_ready, 1)
                dve.wait_ge(xgT_done, n + 1)
                copy_xgT()
                for b in range(TB):
                    dve.wait_ge(scat_done, n * 2 + (b + 1))
                    last = accumulate(b)
                last.then_inc(acc_done, 1)
            dve.drain()
            for b in range(TB):
                dve.wait_ge(scat_done, blocks * 2 + (b + 1))
                for h in range(2):
                    part = yacc[:, b, h * HALF:(h + 1) * HALF]
                    tt(x3[:, b, h * HALF:(h + 1) * HALF], part, moe_bank[((7, 5), (0, 1))[b][h]][:, :], ALU.add)
                    dve.drain()
                    dve.bn_stats(bn3[:, h, :], x3[:, b, h * HALF:(h + 1) * HALF])
                standardise(b)
                dve.wait_ge(ld_ln, 96)
                dve.drain()
                if b == 0:
                    tt(x3[:, 0, :], x3[:, 0, :], ln_g, ALU.mult).then_inc(fin_in, 1)
                else:
                    gains(1, 96).then_inc(out_ready, 1)


_INS = ['x', 'mem', 'w_in', 'gdn_conv_w', 'gdn_a_log', 'gdn_dt_bias', 'gdn_norm_w', 'diff_lq1', 'diff_lk1', 'diff_lq2',
        'diff_lk2', 'diff_norm_w', 'w_out', 'ln1_g', 'ln1_b', 'xa_wq', 'xa_wk', 'xa_wv', 'xa_wo', 'ln2_g', 'ln2_b',
        'router_w', 'router_b', 'exp_w_gate', 'exp_b_gate', 'exp_w_up', 'exp_b_up', 'exp_w_down', 'exp_b_down',
        'ln3_g', 'ln3_b']


def kernel(**inputs):
    import numpy as _np
    import concourse.bacc as _bacc
    from concourse import mybir as _mybir
    from concourse.bass_utils import run_bass_kernel_spmd as _run

    nc = _bacc.Bacc("TRN2", target_bir_lowering=False, num_devices=1, dynamic_dma_scratch_size=256)
    arrays, args = {}, {}
    for name in _INS:
        a = _np.ascontiguousarray(inputs[name])
        arrays[f"in_{name}_dram"] = a
        args[name] = nc.dram_tensor(f"in_{name}_dram", a.shape, _mybir.dt.from_np(a.dtype), kind="ExternalInput").ap()
    a = constants()
    arrays["in_consts_dram"] = a
    args["consts"] = nc.dram_tensor("in_consts_dram", a.shape, _mybir.dt.from_np(a.dtype), kind="ExternalInput").ap()
    out = nc.dram_tensor("out_dram", (1, SEQ, D_MODEL), F32, kind="ExternalOutput").ap()
    trunk_kernel(nc, args, out)
    r = _run(nc, [arrays], core_ids=[0])
    return r.results[0]["out_dram"]
```
